# Optimizing a Trainium2 kernel written in Bass

```python
import math
import jax
import jax.numpy as jnp
from jax import lax
import numpy as np

D_MODEL = 1024
BATCH = 1
SEQ = 256
DEPTH = 2

CTX_LEN = 256
GRID_W = 64
HALF_W = D_MODEL // 2
OUT_W = 2 * HALF_W
NA_HEADS = 8
NA_HD = HALF_W // NA_HEADS
NA_WIN_ROWS = 8
NA_WIN_COLS = 16
DN_HEADS = 4
DN_DK = HALF_W // DN_HEADS
DN_DV = DN_DK
WA_HEADS = 8
WA_KV_HEADS = 2
WA_GROUP = WA_HEADS // WA_KV_HEADS
WA_HD = HALF_W // WA_HEADS
WINDOW = 128
SSD_HEADS = 8
SSD_HD = HALF_W // SSD_HEADS
SSD_INNER = SSD_HEADS * SSD_HD
SSD_GROUPS = 2
SSD_STATE = 128
CHUNK = 64
CONV_K = 5
ROPE_BASE = 10000.0
EPS = 1e-6
NEG_INF = -1e30
FF_DENSE = 2816
N_EXPERTS = 8
TOP_K = 2
FF_EXPERT = 3584
N_EVEN = (DEPTH + 1) // 2
N_ODD = DEPTH // 2
EV_SIZES = (NA_HEADS * NA_HD, NA_HEADS * NA_HD, NA_HEADS * NA_HD, DN_HEADS * DN_DK, DN_HEADS * DN_DK, DN_HEADS * DN_DV, DN_HEADS * DN_DV, 4 * DN_HEADS)
EV_IN = sum(EV_SIZES)
OD_SIZES = (WA_HEADS * WA_HD, WA_KV_HEADS * WA_HD, WA_KV_HEADS * WA_HD, SSD_INNER, SSD_INNER, SSD_GROUPS * SSD_STATE, SSD_GROUPS * SSD_STATE, 2 * SSD_HEADS)
OD_IN = sum(OD_SIZES)

kernel_name = 'hybrid_natten_deltanet_swa_ssd_moe_dit'

F32 = jnp.float32

def rmsnorm(x, w):
    xf = x.astype(F32)
    y = xf * lax.rsqrt(jnp.mean(xf * xf, axis=-1, keepdims=True) + EPS)
    return (y * w.astype(F32)).astype(x.dtype)

def l2norm(x):
    xf = x.astype(F32)
    return xf * lax.rsqrt(jnp.sum(xf * xf, axis=-1, keepdims=True) + EPS)

def modulate(h, shift, scale):
    return h * (1 + scale) + shift

def split_cols(p, sizes):
    cuts = [int(v) for v in np.cumsum(sizes)[:-1]]
    return jnp.split(p, cuts, axis=-1)

def to_heads(t, n):
    b, s, _ = t.shape
    return t.reshape(b, s, n, -1).transpose(0, 2, 1, 3)

def from_heads(t):
    b, n, s, d = t.shape
    return t.transpose(0, 2, 1, 3).reshape(b, s, n * d)

def flip_time(z, rev, axis):
    return jnp.flip(z, axis) if rev else z

def conv_centred(x, w):
    k = w.shape[0]
    return lax.conv_general_dilated(x, w[:, None, :].astype(x.dtype), window_strides=(1,), padding=[(k // 2, k // 2)], dimension_numbers=('NWC', 'WIO', 'NWC'), feature_group_count=x.shape[-1])

def rope_1d(x, pos):
    half = x.shape[-1] // 2
    freqs = ROPE_BASE ** (-jnp.arange(half, dtype=F32) / half)
    ang = pos.astype(F32)[:, None] * freqs[None, :]
    cos, sin = jnp.cos(ang).astype(x.dtype), jnp.sin(ang).astype(x.dtype)
    x1, x2 = x[..., :half], x[..., half:]
    return jnp.concatenate([x1 * cos - x2 * sin, x1 * sin + x2 * cos], axis=-1)

def axial_rope(x):
    t = jnp.arange(x.shape[-2])
    h = x.shape[-1] // 2
    return jnp.concatenate([rope_1d(x[..., :h], t // GRID_W), rope_1d(x[..., h:], t % GRID_W)], axis=-1)

def context_attention(qc, kc, vc, sink=None):
    s = jnp.einsum('bkgqd,bkcd->bkgqc', qc, kc).astype(F32) * qc.shape[-1] ** -0.5
    if sink is not None:
        s = jnp.concatenate([s, jnp.broadcast_to(sink.astype(F32)[None, :, :, None, None], s.shape[:-1] + (1,))], axis=-1)
    p = jax.nn.softmax(s, axis=-1)[..., :kc.shape[2]].astype(vc.dtype)
    return jnp.einsum('bkgqc,bkcd->bkgqd', p, vc)

def neighbourhood_attention(q, k, v, kc, vc, rpb):
    b, h, s, d = q.shape
    rows = s // GRID_W
    kr = min(NA_WIN_ROWS, rows)
    r = jnp.arange(rows)
    row_idx = jnp.clip(r - kr // 2, 0, rows - kr)[:, None] + jnp.arange(kr)[None, :]
    col = jnp.arange(GRID_W)
    col_start = jnp.clip(col - NA_WIN_COLS // 2, 0, GRID_W - NA_WIN_COLS)
    col_ok = (col[None, :] >= col_start[:, None]) & (col[None, :] < col_start[:, None] + NA_WIN_COLS)
    dr = row_idx - r[:, None] + NA_WIN_ROWS - 1
    dc = jnp.clip(col[None, :] - col[:, None] + NA_WIN_COLS - 1, 0, 2 * NA_WIN_COLS - 2)
    bias = rpb[:, dr][..., dc].astype(F32).transpose(0, 1, 3, 2, 4)
    bias = jnp.where(col_ok[None, None, :, None, :], bias, NEG_INF).reshape(h, rows, GRID_W, kr * GRID_W)
    qg = q.reshape(b, h, rows, GRID_W, d)
    kg = k.reshape(b, h, rows, GRID_W, d)[:, :, row_idx].reshape(b, h, rows, kr * GRID_W, d)
    vg = v.reshape(b, h, rows, GRID_W, d)[:, :, row_idx].reshape(b, h, rows, kr * GRID_W, d)
    scale = d ** -0.5
    s_loc = jnp.einsum('bhrqd,bhrkd->bhrqk', qg, kg).astype(F32) * scale + bias
    s_ctx = jnp.einsum('bhrqd,bhcd->bhrqc', qg, kc).astype(F32) * scale
    p = jax.nn.softmax(jnp.concatenate([s_loc, s_ctx], axis=-1), axis=-1).astype(v.dtype)
    nk = kr * GRID_W
    o = jnp.einsum('bhrqk,bhrkd->bhrqd', p[..., :nk], vg) + jnp.einsum('bhrqc,bhcd->bhrqd', p[..., nk:], vc)
    return o.reshape(b, h, s, d)

def window_attention(q, k, v, kc, vc, sink):
    b, nkv, g, s, d = q.shape
    blk = WINDOW
    nb = s // blk

    def bands(t):
        tp = jnp.pad(t, ((0, 0), (0, 0), (blk, blk), (0, 0))).reshape(b, nkv, nb + 2, blk, d)
        return jnp.concatenate([tp[:, :, :-2], tp[:, :, 1:-1], tp[:, :, 2:]], axis=3)

    kb, vb = bands(k), bands(v)
    qb = q.reshape(b, nkv, g, nb, blk, d)
    qpos = jnp.arange(nb)[:, None] * blk + jnp.arange(blk)[None, :]
    kpos = (jnp.arange(nb)[:, None] - 1) * blk + jnp.arange(3 * blk)[None, :]
    kp = kpos[:, None, :]
    ok = (jnp.abs(kp - qpos[:, :, None]) <= WINDOW) & (kp >= 0) & (kp < s)
    scale = d ** -0.5
    s_loc = jnp.where(ok, jnp.einsum('bkgnqd,bknjd->bkgnqj', qb, kb).astype(F32) * scale, NEG_INF)
    s_ctx = jnp.einsum('bkgnqd,bkcd->bkgnqc', qb, kc).astype(F32) * scale
    s_sink = jnp.broadcast_to(sink.astype(F32)[None, :, :, None, None, None], s_ctx.shape[:-1] + (1,))
    p = jax.nn.softmax(jnp.concatenate([s_loc, s_ctx, s_sink], axis=-1), axis=-1).astype(v.dtype)
    nl, nc = 3 * blk, kc.shape[2]
    o = jnp.einsum('bkgnqj,bknjd->bkgnqd', p[..., :nl], vb) + jnp.einsum('bkgnqc,bkcd->bkgnqd', p[..., nl:nl + nc], vc)
    return o.reshape(b, nkv, g, s, d)

def gated_delta_chunked(q, k, v, beta, g, state0):
    b, h, t, dk = k.shape
    dv = v.shape[-1]
    n = t // CHUNK
    q, k, v = (z.reshape(b, h, n, CHUNK, -1) for z in (q, k, v))
    beta = beta.reshape(b, h, n, CHUNK)
    gc = jnp.cumsum(g.reshape(b, h, n, CHUNK), axis=-1)
    idx = jnp.arange(CHUNK)
    incl = idx[:, None] >= idx[None, :]
    strict = idx[:, None] > idx[None, :]
    decay = jnp.exp(jnp.where(incl, gc[..., :, None] - gc[..., None, :], -jnp.inf))
    kb = k * beta[..., None]
    a_low = jnp.where(strict, jnp.einsum('bhncd,bhnjd->bhncj', kb, k) * decay, 0.0)
    rhs = jnp.concatenate([v * beta[..., None], kb * jnp.exp(gc)[..., None]], axis=-1)
    sol = lax.linalg.triangular_solve(a_low + jnp.eye(CHUNK, dtype=k.dtype), rhs, left_side=True, lower=True, unit_diagonal=True)
    u, w = sol[..., :dv], sol[..., dv:]
    attn = jnp.einsum('bhncd,bhnjd->bhncj', q, k) * decay
    q_dec = q * jnp.exp(gc)[..., None]
    g_last = gc[..., -1]
    k_dec = k * jnp.exp(g_last[..., None] - gc)[..., None]

    def step(state, xs):
        u_c, w_c, a_c, qd_c, kd_c, gl_c = xs
        v_new = u_c - jnp.einsum('bhcd,bhde->bhce', w_c, state)
        o_c = jnp.einsum('bhcd,bhde->bhce', qd_c, state) + jnp.einsum('bhcj,bhje->bhce', a_c, v_new)
        state = state * jnp.exp(gl_c)[..., None, None] + jnp.einsum('bhcd,bhce->bhde', kd_c, v_new)
        return state, o_c

    xs = tuple(jnp.moveaxis(z, 2, 0) for z in (u, w, attn, q_dec, k_dec, g_last))
    state, o = lax.scan(step, state0, xs)
    return jnp.moveaxis(o, 0, 2).reshape(b, h, t, dv), state

def delta_inputs(q, k, v, gates, conv_w, a_log, dt_bias):
    qkv = jax.nn.silu(conv_centred(jnp.concatenate([q, k, v], axis=-1), conv_w))
    q, k, v = jnp.split(qkv, [DN_HEADS * DN_DK, 2 * DN_HEADS * DN_DK], axis=-1)
    q = l2norm(to_heads(q, DN_HEADS)) * DN_DK ** -0.5
    k = l2norm(to_heads(k, DN_HEADS))
    v = to_heads(v, DN_HEADS).astype(F32)
    b, t, _ = gates.shape
    raw = gates.astype(F32).reshape(b, t, 2, 2, DN_HEADS).transpose(2, 3, 0, 4, 1)
    beta = jax.nn.sigmoid(raw[0])
    g = -jnp.exp(a_log.astype(F32))[:, None, :, None] * jax.nn.softplus(raw[1] + dt_bias.astype(F32)[:, None, :, None])
    return q, k, v, beta, g

def bidir_gated_delta(ctx_in, lat_in):
    qc, kc, vc, bc, gcx = ctx_in
    ql, kl, vl, bl, gl = lat_in
    b, h, _, dk = kc.shape
    out_c = out_l = 0.0
    for d, rev in enumerate((False, True)):
        f = functools_flip(rev, 2)
        state0 = jnp.zeros((b, h, dk, vc.shape[-1]), F32)
        oc, st = gated_delta_chunked(f(qc), f(kc), f(vc), f(bc[d]), f(gcx[d]), state0)
        ol, _ = gated_delta_chunked(f(ql), f(kl), f(vl), f(bl[d]), f(gl[d]), st)
        out_c = out_c + f(oc)
        out_l = out_l + f(ol)
    return out_c, out_l

def functools_flip(rev, axis):
    return lambda z: flip_time(z, rev, axis)

def delta_gate_norm(o, z, w):
    o = rmsnorm(o, w)
    return (from_heads(o) * jax.nn.silu(z.astype(F32))).astype(z.dtype)

def ssd_chunked(x, dt, a, bm, cm, state0):
    b, t, h, p = x.shape
    n = t // CHUNK
    xd = (x * dt[..., None]).reshape(b, n, CHUNK, h, p)
    bm = bm.reshape(b, n, CHUNK, h, -1)
    cm = cm.reshape(b, n, CHUNK, h, -1)
    acum = jnp.cumsum((dt * a).reshape(b, n, CHUNK, h).transpose(0, 3, 1, 2), axis=-1)
    idx = jnp.arange(CHUNK)
    incl = idx[:, None] >= idx[None, :]
    lmat = jnp.exp(jnp.where(incl, acum[..., :, None] - acum[..., None, :], -jnp.inf))
    y_diag = jnp.einsum('bnlhs,bnjhs,bhnlj,bnjhp->bnlhp', cm, bm, lmat, xd)
    decay_states = jnp.exp(acum[..., -1:] - acum)
    states = jnp.einsum('bnlhs,bhnl,bnlhp->bnhps', bm, decay_states, xd)
    chunk_decay = jnp.exp(acum[..., -1])

    def step(hs, xs):
        st_c, dec_c = xs
        return hs * dec_c[..., None, None] + st_c, hs

    final, prev = lax.scan(step, state0, (jnp.moveaxis(states, 1, 0), jnp.moveaxis(chunk_decay, 2, 0)))
    prev = jnp.moveaxis(prev, 0, 1)
    y_off = jnp.einsum('bnlhs,bnhps,bhnl->bnlhp', cm, prev, jnp.exp(acum))
    return (y_diag + y_off).reshape(b, t, h, p), final

def ssd_inputs(x, bm, cm, dt_raw, conv_w, dt_bias):
    xbc = jax.nn.silu(conv_centred(jnp.concatenate([x, bm, cm], axis=-1), conv_w)).astype(F32)
    x, bm, cm = jnp.split(xbc, [SSD_INNER, SSD_INNER + SSD_GROUPS * SSD_STATE], axis=-1)
    b, t, _ = x.shape
    rep = SSD_HEADS // SSD_GROUPS
    x = x.reshape(b, t, SSD_HEADS, SSD_HD)
    bm = jnp.repeat(bm.reshape(b, t, SSD_GROUPS, SSD_STATE), rep, axis=2)
    cm = jnp.repeat(cm.reshape(b, t, SSD_GROUPS, SSD_STATE), rep, axis=2)
    dt = jax.nn.softplus(dt_raw.astype(F32).reshape(b, t, 2, SSD_HEADS) + dt_bias.astype(F32))
    return x, bm, cm, dt

def bidir_ssd(ctx_in, lat_in, a, d_skip):
    xc, bc, cc, dtc = ctx_in
    xl, bl, cl, dtl = lat_in
    b, _, h, p = xc.shape
    skip = d_skip.astype(F32)[:, None]
    out_c, out_l = xc * skip, xl * skip
    for d, rev in enumerate((False, True)):
        f = functools_flip(rev, 1)
        state0 = jnp.zeros((b, h, p, SSD_STATE), F32)
        yc, st = ssd_chunked(f(xc), f(dtc[:, :, d]), a[d], f(bc), f(cc), state0)
        yl, _ = ssd_chunked(f(xl), f(dtl[:, :, d]), a[d], f(bl), f(cl), st)
        out_c = out_c + f(yc)
        out_l = out_l + f(yl)
    return out_c, out_l

def ssd_gate_norm(y, z, w):
    b, t = z.shape[:2]
    y = y.reshape(b, t, SSD_INNER) * jax.nn.silu(z.astype(F32))
    y = rmsnorm(y.reshape(b, t, SSD_GROUPS, -1), w.reshape(SSD_GROUPS, -1))
    return y.reshape(b, t, SSD_INNER).astype(z.dtype)

def even_mixer(h, hc, w_in, w_out, rpb, conv_w, a_log, dt_bias, norm_w, with_ctx):
    nq, nk, nv, dq, dk, dv, dz, dg = split_cols(h @ w_in, EV_SIZES)
    cnq, cnk, cnv, cdq, cdk, cdv, cdz, cdg = split_cols(hc @ w_in, EV_SIZES)
    kc_a, vc_a = to_heads(cnk, NA_HEADS), to_heads(cnv, NA_HEADS)
    o_a = from_heads(neighbourhood_attention(to_heads(nq, NA_HEADS), to_heads(nk, NA_HEADS), to_heads(nv, NA_HEADS), kc_a, vc_a, rpb))
    oc_b, ol_b = bidir_gated_delta(delta_inputs(cdq, cdk, cdv, cdg, conv_w, a_log, dt_bias), delta_inputs(dq, dk, dv, dg, conv_w, a_log, dt_bias))
    y = jnp.concatenate([o_a, delta_gate_norm(ol_b, dz, norm_w)], axis=-1) @ w_out
    if not with_ctx:
        return y, None
    oc_a = context_attention(to_heads(cnq, NA_HEADS)[:, :, None], kc_a, vc_a)[:, :, 0]
    yc = jnp.concatenate([from_heads(oc_a), delta_gate_norm(oc_b, cdz, norm_w)], axis=-1) @ w_out
    return y, yc

def odd_mixer(h, hc, w_in, w_out, sink, conv_w, a_log, dt_bias, d_skip, norm_w, with_ctx):
    wq, wk, wv, z, xs, bs, cs, dtr = split_cols(h @ w_in, OD_SIZES)
    cwq, cwk, cwv, cz, cxs, cbs, ccs, cdtr = split_cols(hc @ w_in, OD_SIZES)
    b, s, _ = h.shape
    sink = sink.reshape(WA_KV_HEADS, WA_GROUP)
    q = axial_rope(to_heads(wq, WA_HEADS)).reshape(b, WA_KV_HEADS, WA_GROUP, s, WA_HD)
    k = axial_rope(to_heads(wk, WA_KV_HEADS))
    v = to_heads(wv, WA_KV_HEADS)
    kc, vc = to_heads(cwk, WA_KV_HEADS), to_heads(cwv, WA_KV_HEADS)
    o_c = from_heads(window_attention(q, k, v, kc, vc, sink).reshape(b, WA_HEADS, s, WA_HD))
    a = -jnp.exp(a_log.astype(F32))
    yc_d, yl_d = bidir_ssd(ssd_inputs(cxs, cbs, ccs, cdtr, conv_w, dt_bias), ssd_inputs(xs, bs, cs, dtr, conv_w, dt_bias), a, d_skip)
    y = jnp.concatenate([o_c, ssd_gate_norm(yl_d, z, norm_w)], axis=-1) @ w_out
    if not with_ctx:
        return y, None
    l = hc.shape[1]
    qc = to_heads(cwq, WA_HEADS).reshape(b, WA_KV_HEADS, WA_GROUP, l, WA_HD)
    oc_c = from_heads(context_attention(qc, kc, vc, sink).reshape(b, WA_HEADS, l, WA_HD))
    yc = jnp.concatenate([oc_c, ssd_gate_norm(yc_d, cz, norm_w)], axis=-1) @ w_out
    return y, yc

def swiglu(h, w1, w3, w2):
    return (jax.nn.silu(h @ w1) * (h @ w3)) @ w2

def moe_swiglu(h, router, w1, w3, w2):
    logits = (h @ router).astype(F32)
    top_v, top_i = lax.top_k(logits, TOP_K)
    gates = jax.nn.softmax(top_v, axis=-1)
    weight = jnp.sum(jax.nn.one_hot(top_i, N_EXPERTS, dtype=F32) * gates[..., None], axis=-2).astype(h.dtype)
    out = jnp.zeros_like(h)
    for e in range(N_EXPERTS):
        out = out + weight[..., e:e + 1] * swiglu(h, w1[e], w3[e], w2[e])
    return out

def setup_inputs(seed: int = 0) -> dict:
    key = jax.random.key(seed)
    ks = iter(list(jax.random.split(key, 40)))
    d = D_MODEL
    ne, no = N_EVEN, N_ODD

    def nrm(shape, scale):
        return jax.random.normal(next(ks), shape, F32) * scale

    def gain(shape):
        return 1.0 + nrm(shape, 0.05)

    def a_log(shape):
        return jnp.log(jax.random.uniform(next(ks), shape, F32, 1.0, 16.0))

    def dt_bias(shape):
        dt = jnp.exp(jax.random.uniform(next(ks), shape, F32, math.log(1e-3), math.log(1e-1)))
        return dt + jnp.log(-jnp.expm1(-dt))

    return {
        'x': nrm((BATCH, SEQ, d), 1.0),
        'c': nrm((BATCH, d), 1.0),
        'ctx': nrm((BATCH, CTX_LEN, d), 1.0),
        'c_ctx': nrm((d,), 1.0),
        'ada_w': nrm((DEPTH, d, 6 * d), 0.5 * d ** -0.5),
        'ada_b': nrm((DEPTH, 6 * d), 0.01),
        'norm_w': gain((DEPTH, 4, d)),
        'ev_w_in': nrm((ne, d, EV_IN), d ** -0.5),
        'ev_w_out': nrm((ne, OUT_W, d), OUT_W ** -0.5),
        'na_rpb': nrm((ne, NA_HEADS, 2 * NA_WIN_ROWS - 1, 2 * NA_WIN_COLS - 1), 0.02),
        'dn_conv': nrm((ne, CONV_K, 2 * DN_HEADS * DN_DK + DN_HEADS * DN_DV), CONV_K ** -0.5),
        'dn_a_log': a_log((ne, 2, DN_HEADS)),
        'dn_dt_bias': dt_bias((ne, 2, DN_HEADS)),
        'dn_norm': gain((ne, DN_DV)),
        'ffn_w1': nrm((ne, d, FF_DENSE), d ** -0.5),
        'ffn_w3': nrm((ne, d, FF_DENSE), d ** -0.5),
        'ffn_w2': nrm((ne, FF_DENSE, d), FF_DENSE ** -0.5),
        'od_w_in': nrm((no, d, OD_IN), d ** -0.5),
        'od_w_out': nrm((no, OUT_W, d), OUT_W ** -0.5),
        'wa_sink': nrm((no, WA_HEADS), 1.0),
        'ssd_conv': nrm((no, CONV_K, SSD_INNER + 2 * SSD_GROUPS * SSD_STATE), CONV_K ** -0.5),
        'ssd_a_log': a_log((no, 2, SSD_HEADS)),
        'ssd_dt_bias': dt_bias((no, 2, SSD_HEADS)),
        'ssd_d': gain((no, SSD_HEADS)),
        'ssd_norm': gain((no, SSD_INNER)),
        'moe_router': nrm((no, d, N_EXPERTS), d ** -0.5),
        'moe_w1': nrm((no, N_EXPERTS, d, FF_EXPERT), d ** -0.5),
        'moe_w3': nrm((no, N_EXPERTS, d, FF_EXPERT), d ** -0.5),
        'moe_w2': nrm((no, N_EXPERTS, FF_EXPERT, d), FF_EXPERT ** -0.5),
    }

def reference(x, c, ctx, c_ctx, ada_w, ada_b, norm_w, ev_w_in, ev_w_out, na_rpb, dn_conv, dn_a_log, dn_dt_bias, dn_norm, ffn_w1, ffn_w3, ffn_w2, od_w_in, od_w_out, wa_sink, ssd_conv, ssd_a_log, ssd_dt_bias, ssd_d, ssd_norm, moe_router, moe_w1, moe_w3, moe_w2):
    sc, scc = jax.nn.silu(c), jax.nn.silu(c_ctx)
    xc = ctx
    for layer in range(DEPTH):
        i = layer // 2
        with_ctx = layer < DEPTH - 1
        m = jnp.split((sc @ ada_w[layer] + ada_b[layer])[:, None, :], 6, axis=-1)
        mc = jnp.split(scc @ ada_w[layer] + ada_b[layer], 6, axis=-1)
        nw = norm_w[layer]
        h = modulate(rmsnorm(x, nw[0]), m[0], m[1])
        hc = modulate(rmsnorm(xc, nw[0]), mc[0], mc[1])
        if layer % 2 == 0:
            y, yc = even_mixer(h, hc, ev_w_in[i], ev_w_out[i], na_rpb[i], dn_conv[i], dn_a_log[i], dn_dt_bias[i], dn_norm[i], with_ctx)
            ffn = functools_ffn_dense(ffn_w1[i], ffn_w3[i], ffn_w2[i])
        else:
            y, yc = odd_mixer(h, hc, od_w_in[i], od_w_out[i], wa_sink[i], ssd_conv[i], ssd_a_log[i], ssd_dt_bias[i], ssd_d[i], ssd_norm[i], with_ctx)
            ffn = functools_ffn_moe(moe_router[i], moe_w1[i], moe_w3[i], moe_w2[i])
        x = x + m[2] * rmsnorm(y, nw[1])
        x = x + m[5] * rmsnorm(ffn(modulate(rmsnorm(x, nw[2]), m[3], m[4])), nw[3])
        if with_ctx:
            xc = xc + mc[2] * rmsnorm(yc, nw[1])
            xc = xc + mc[5] * rmsnorm(ffn(modulate(rmsnorm(xc, nw[2]), mc[3], mc[4])), nw[3])
    return x

def functools_ffn_dense(w1, w3, w2):
    return lambda t: swiglu(t, w1, w3, w2)

def functools_ffn_moe(router, w1, w3, w2):
    return lambda t: moe_swiglu(t, router, w1, w3, w2)


_drawn_inputs = setup_inputs


def setup_inputs(seed=0):
    import zlib

    import numpy as np

    out = dict(_drawn_inputs(seed))
    spreads = {}
    factors = {'na_rpb': 27.199, 'wa_sink': 8.0, 'ssd_d': 8.0}
    for name, (base, spread) in spreads.items():
        noise = np.random.default_rng([zlib.crc32(name.encode()), seed]).standard_normal(out[name].shape)
        drawn = base * np.exp(spread * noise) if base else spread * noise
        out[name] = jnp.asarray(drawn.astype(out[name].dtype))
    for name, factor in factors.items():
        out[name] = (out[name] * factor).astype(out[name].dtype)
    return out
```

```python
from contextlib import ExitStack

import concourse.bass as bass
from concourse import mybir

F32 = mybir.dt.float32
U32 = mybir.dt.uint32
ALU = mybir.AluOpType
ACT = mybir.ActivationFunctionType
AX = mybir.AxisListType

P = 128
D = 1024
KD = D // P
LAT, CTX = 256, 256
T = 4
NTOK = LAT + CTX
HALF = 512
HD = 64
EV_IN, OD_IN = 3600, 2320
FF = 2816
NF = FF // P
E, FE = 8, 3584
EPS = 1e-6
TAPS = 5
LEVELS = 7
CHUNK_ORDER = ((2, 3, 0, 1), (3, 2, 1, 0))

CONST = {}
_at = 0
for _n, _w in (("ident", P), ("cum0", P), ("cum1", P), ("ones", P), ("neg0", P), ("neg1", P), ("band", 2 * LAT),
               ("natcol", 64), ("cos", LAT), ("sin", LAT), ("rot", P), ("iota", P), ("before", P), ("pick", 2 * P)):
    CONST[_n] = (_at, _w)
    _at += _w
NCONST = _at


def build(nc, t, out):
    with ExitStack() as ctx:
        def sb(name, shape, dt=F32):
            return ctx.enter_context(nc.sbuf_tensor(name, shape, dt))

        stage_sems = []

        def sem(name):
            s = nc.alloc_semaphore(name=name)
            stage_sems.append(s)
            return s

        bank = [ctx.enter_context(nc.psum_tensor(f"bank{i}", [P, 512], F32)) for i in range(8)]

        def quad(i):
            return bank[i][:, :].rearrange("p (a b) -> p a b", a=4)

        X = sb("residual", [P, T, D])
        C = sb("const", [P, NCONST])
        G = sb("gate_rows", [P, 6, D])
        cols = sb("channel_cols", [P, 2, P])
        modc = sb("mod_cols", [P, 2, 4, KD, 2])
        hT = sb("hT", [P, KD, NTOK])
        catT = sb("catT", [P, KD, NTOK])
        ar = sb("arena", [P, 28768])
        small = sb("small", [P, 640])
        mhalf = sb("minus_half", [P, 64])
        gbias = sb("gate_bias", [16, 8])
        rowcol = sb("per_head_rows", [P, 16])

        def cst(name):
            a, w = CONST[name]
            return C[:, a:a + w]

        ident, ones = cst("ident"), cst("ones")
        cum, neg = (cst("cum0"), cst("cum1")), (cst("neg0"), cst("neg1"))

        def cut(at, *shape):
            n = 1
            for s in shape:
                n *= s
            v = ar[:, at:at + n]
            if len(shape) == 1:
                return v
            names = "abcd"[:len(shape)]
            return v.rearrange(f"p ({' '.join(names)}) -> p {' '.join(names)}", **dict(zip(names, shape)))

        chain = {k: [ctx.enter_context(nc.semaphore(f"{k}_chain")), 0] for k in ("act", "dve", "pool")}

        def linker(eng, key):
            def link(ins):
                chain[key][1] += 1
                ins.then_inc(chain[key][0], 1)
                eng.wait_ge(chain[key][0], chain[key][1])
            return link

        NORMW = lambda l, i, k: cols[:, 0, (l * 4 + i) * 8 + k:(l * 4 + i) * 8 + k + 1]
        DNCONV = lambda tap, c: cols[:, 0, 64 + tap * 12 + c:65 + tap * 12 + c]
        DNNORM = cols[:, 0, 124:125]
        SSDCONV = lambda tap, c: cols[:, 1, tap * 8 + c:tap * 8 + c + 1]
        SSDNORM = lambda c: cols[:, 1, 40 + c:41 + c]

        NSLOT, NCH = 4, 24
        aw = [cut(i * 4096, KD, 512) for i in range(NSLOT)]
        row0 = NSLOT * 4096
        ROW = ar[0:2, row0:row0 + 2 * 6 * D].rearrange("p (l n) -> p l n", l=2)
        rows = hT[:, 0:2, 0:P]
        abias = [catT[0:2, i, 0:512] for i in range(NSLOT)]
        nwr = catT[0:2, 4:8, :].rearrange("p a b -> p (a b)")
        nwr2 = hT[0:2, 4:8, :].rearrange("p a b -> p (a b)")
        scT = small[:, 0:16].rearrange("p (v k) -> p k v", v=2)
        s_x, s_const, s_rows, s_nw = sem("x_in"), sem("const_in"), sem("rows_in"), sem("norm_rows_in")
        s_slot = [sem(f"ada_w{i}") for i in range(NSLOT)]
        s_tr, s_trc = sem("rows_transposed"), sem("cols_copied")
        s_sc, s_ada, s_row = sem("silu_c"), sem("ada_product"), sem("ada_row")
        s_mp, s_mc, s_gp, s_gc, s_mh = sem("mod_transposed"), sem("mod_copied"), sem("gate_spread"), sem("gate_copied"), sem("minus_half_set")
        s_mg = sem("gate_times_norm")

        with nc.Block() as block:
            @block.sync
            def _(sp):
                sp.dma_start(C[:, :], t["const"]).then_inc(s_const, 16)
                sp.dma_start(rows[0:64, 0, :], t["norm_w"].rearrange("l i (k p) -> (l i k) p", p=P)).then_inc(s_rows, 16)
                sp.dma_start(rows[64:124, 0, :], t["dn_conv"].rearrange("t (c p) -> (t c) p", p=P)).then_inc(s_rows, 16)
                sp.dma_start(rows[124:125, 0, :], t["dn_norm"]).then_inc(s_rows, 16)
                sp.dma_start(rows[0:40, 1, :], t["ssd_conv"].rearrange("t (c p) -> (t c) p", p=P)).then_inc(s_rows, 16)
                sp.dma_start(rows[40:44, 1, :], t["ssd_norm"].rearrange("a (c p) -> (a c) p", p=P)).then_inc(s_rows, 16)
                sp.dma_start(rows[44:52, 1, :], t["c"].rearrange("a (k p) -> (a k) p", p=P)).then_inc(s_rows, 16)
                sp.dma_start(rows[52:60, 1, :], t["c_ctx"].rearrange("a (k p) -> (a k) p", p=P)).then_inc(s_rows, 16)
                adaw = [t["ada_w"][l].rearrange("(k p) n -> p k n", p=P) for l in range(2)]
                adab = [t["ada_b"][l:l + 1, :] for l in range(2)]

                def load(l, n, s):
                    w = slice(n * 512, n * 512 + 512) if isinstance(n, int) else bass.ds(n * 512, 512)
                    sp.dma_start(aw[s], adaw[l][:, :, w]).then_inc(s_slot[s], 16)
                    sp.dma_start(abias[s], adab[l][:, w].to_broadcast([2, 512])).then_inc(s_slot[s], 16)
                for s in range(NSLOT):
                    load(0, s, s)
                sp.dma_start(X[:, 0:2, :], t["x"].rearrange("(t p) d -> p t d", p=P)).then_inc(s_x, 16)
                sp.dma_start(X[:, 2:4, :], t["ctx"].rearrange("(t p) d -> p t d", p=P)).then_inc(s_x, 16)
                for l, dst in ((0, nwr), (1, nwr2)):
                    for j, i in enumerate((1, 3)):
                        sp.dma_start(dst[:, j * D:(j + 1) * D], t["norm_w"][l, i:i + 1, :].to_broadcast([2, D])).then_inc(s_nw, 16)
                sp.dma_start(gbias[0:8, 0:1], t["dn_dt_bias"]).then_inc(s_nw, 16)
                sp.dma_start(gbias[0:8, 1:2], t["dn_a_log"]).then_inc(s_nw, 16)
                sp.dma_start(gbias[:, 2:3], t["ssd_dt_bias"]).then_inc(s_nw, 16)
                sp.dma_start(gbias[:, 3:4], t["ssd_a_log"]).then_inc(s_nw, 16)
                sp.dma_start(rowcol[:, 0:8], t["wa_sink"].to_broadcast([P, 8])).then_inc(s_nw, 16)
                sp.dma_start(rowcol[:, 8:16], t["ssd_d"].to_broadcast([P, 8])).then_inc(s_nw, 16)
                for l in range(2):
                    with sp.Fori(max(1, 3 * l), 3 * l + 3) as i:
                        for s in range(NSLOT):
                            sp.wait_ge(s_row, NSLOT * i + (s + 1 - NSLOT))
                            load(l, NSLOT * i + (s - 12 * l), s)
                sp.wait_ge(s_x, 32)

            @block.tensor
            def _(pe):
                pe.wait_ge(s_const, 16)
                pe.wait_ge(s_rows, 112)
                pe.transpose(bank[4][:, 0:125], rows[0:125, 0, :], ident[0:125, 0:125]).then_inc(s_tr, 1)
                pe.transpose(bank[5][:, 0:60], rows[0:60, 1, :], ident[0:60, 0:60]).then_inc(s_tr, 1)
                pe.wait_ge(s_sc, 1)

                def chunk(i, first):
                    for s in range(NSLOT):
                        if not first:
                            pe.wait_ge(s_row, NSLOT * i + (s + 1 - NSLOT))
                        pe.wait_ge(s_slot[s], 32 * i + 32)
                        for k in range(KD):
                            mm = pe.matmul(bank[s][0:2, :], scT[:, k, :], aw[s][:, k, :], start=(k == 0), stop=(k == KD - 1))
                        mm.then_inc(s_ada, 1)
                chunk(0, True)
                with pe.Fori(1, NCH // NSLOT) as i:
                    chunk(i, False)
                pe.wait_ge(s_row, NCH)
                n = 0
                for l in range(2):
                    for j, part in enumerate((0, 1, 3, 4)):
                        for k in range(KD):
                            n += 1
                            a = part * D + k * P
                            mm = pe.transpose(bank[4 + l][:, (j * 8 + k) * 2:(j * 8 + k) * 2 + 2], ROW[:, l, a:a + P], ident[0:2, 0:2])
                    mm.then_inc(s_mp, 1)
                pe.wait_ge(s_mg, 4)
                for n, (l, j, v) in enumerate(((0, 0, 0), (0, 1, 0), (1, 0, 0), (1, 1, 0), (0, 0, 1), (0, 1, 1))):
                    if n >= 2:
                        pe.wait_ge(s_gc, n - 1)
                    for half in range(2):
                        part = 2 if j == 0 else 5
                        mm = pe.matmul(bank[2 * (n % 2) + half][:, :], cst("pick")[0:2, v * P:v * P + P],
                                       ROW[:, l, part * D + half * 512:part * D + half * 512 + 512], start=True, stop=True)
                    mm.then_inc(s_gp, 1)

            @block.vector
            def _(dve):
                link = linker(dve, "dve")
                dve.memset(mhalf[:, :], -0.5).then_inc(s_mh, 1)
                dve.wait_ge(s_tr, 2)
                dve.tensor_copy(cols[:, 0, 0:125], bank[4][:, 0:125]).then_inc(s_trc, 1)
                dve.tensor_copy(cols[:, 1, 0:60], bank[5][:, 0:60]).then_inc(s_trc, 1)

                def chunk(i):
                    for s in range(NSLOT):
                        dve.wait_ge(s_ada, NSLOT * i + s + 1)
                        n = NSLOT * i + s
                        flat = ROW.rearrange("p l (n w) -> p (l n) w", w=512)
                        dst = flat[:, n, :] if isinstance(n, int) else flat[:, bass.ds(n, 1), :].rearrange("p a w -> p (a w)")
                        dve.tensor_tensor(dst, bank[s][0:2, :], abias[s], ALU.add).then_inc(s_row, 1)
                chunk(0)
                with dve.Fori(1, NCH // NSLOT) as i:
                    chunk(i)
                dve.wait_ge(s_row, NCH)
                dve.wait_ge(s_nw, 160)
                for l, w in ((0, nwr), (1, nwr2)):
                    for j, part in enumerate((2, 5)):
                        m = ROW[:, l, part * D:(part + 1) * D]
                        dve.tensor_tensor(m, m, w[:, j * D:(j + 1) * D], ALU.mult).then_inc(s_mg, 1)
                dve.wait_ge(s_mp, 2)
                dve.wait_ge(s_trc, 2)
                for l in range(2):
                    m = bank[4 + l][:, 0:64].rearrange("p (j k v) -> p j k v", j=4, k=KD)
                    for j in range(4):
                        if j % 2 == 0:
                            dve.tensor_copy(modc[:, l, j, :, :], m[:, j, :, :])
                        else:
                            link(dve.tensor_scalar(modc[:, l, j, :, :], m[:, j, :, :], 1.0, None, ALU.add))
                            w = cols[:, 0, (l * 4 + j - 1) * 8:(l * 4 + j) * 8]
                            for v in range(2):
                                dve.tensor_tensor(modc[:, l, j, :, v], modc[:, l, j, :, v], w, ALU.mult)
                for n in range(1, 6, 2):
                    dve.wait_ge(s_gp, n + 1)
                    dve.wait_ge(s_gc, n)
                    for half in range(2):
                        cp = dve.tensor_copy(G[:, n, half * 512:half * 512 + 512], bank[2 * (n % 2) + half][:, :])
                    cp.then_inc(s_gc, 1)

            @block.scalar
            def _(act):
                act.wait_ge(s_trc, 2)
                act.activation(small[:, 0:16], cols[:, 1, 44:60], ACT.Silu).then_inc(s_sc, 1)
                for n in range(0, 6, 2):
                    act.wait_ge(s_gp, n + 1)
                    if n:
                        act.wait_ge(s_gc, n)
                    for half in range(2):
                        cp = act.activation(G[:, n, half * 512:half * 512 + 512], bank[2 * (n % 2) + half][:, :], ACT.Copy)
                    cp.then_inc(s_gc, 1)

        def norm_to_hT(tag, l, which, tiles, xn):
            n = len(tiles)
            s_sq, s_r, s_xn, s_tp = sem(f"{tag}_squares"), sem(f"{tag}_rms"), sem(f"{tag}_xn"), sem(f"{tag}_transposed")
            ss, r = small[:, 0:4], small[:, 4:8]
            junk = hT[:, :, :].rearrange("p (t a) b -> p t (a b)", t=4)
            shift, scale = modc[:, l, 2 * which, :, :], modc[:, l, 2 * which + 1, :, :]
            with nc.Block() as block:
                @block.scalar
                def _(act):
                    link = linker(act, "act")
                    for i in range(n):
                        ins = act.activation(junk[:, i, :], X[:, i, :], ACT.Square, accum_out=ss[:, i:i + 1])
                        if i == n - 1:
                            ins.then_inc(s_sq, 1)
                    act.wait_ge(s_sq, 1)
                    for k in range(0, KD, 2):
                        for v in range(n // 2):
                            act.wait_ge(s_tp, 8 * (n - 1) + k + 1)
                            act.activation(hT[:, k, 256 * v:256 * v + 256], bank[k][:, 256 * v:256 * v + 256], ACT.Identity,
                                           bias=shift[:, k, v:v + 1], scale=scale[:, k, v:v + 1])

                @block.gpsimd
                def _(pool):
                    link = linker(pool, "pool")
                    pool.wait_ge(s_sq, 1)
                    link(pool.tensor_scalar(r[:, 0:n], ss[:, 0:n], 1.0 / D, EPS, ALU.mult, ALU.add))
                    pool.tensor_tensor(r[:, 0:n], r[:, 0:n], mhalf[:, 0:n], ALU.pow).then_inc(s_r, 1)

                @block.vector
                def _(dve):
                    dve.wait_ge(s_r, 1)
                    for i in range(n):
                        dve.tensor_scalar(xn[:, i, :], X[:, i, :], r[:, i:i + 1], None, ALU.mult).then_inc(s_xn, 1)
                    for k in range(1, KD, 2):
                        for v in range(n // 2):
                            dve.wait_ge(s_tp, 8 * (n - 1) + k + 1)
                            dve.tensor_scalar(hT[:, k, 256 * v:256 * v + 256], bank[k][:, 256 * v:256 * v + 256],
                                              scale[:, k, v:v + 1], shift[:, k, v:v + 1], ALU.mult, ALU.add)

                @block.tensor
                def _(pe):
                    for i in range(n):
                        pe.wait_ge(s_xn, i + 1)
                        for k in range(KD):
                            pe.transpose(bank[k][:, i * P:(i + 1) * P], xn[:, i, k * P:(k + 1) * P], ident).then_inc(s_tp, 1)

        def project_and_add(tag, w_rows, n, gate_lat, gate_ctx, wbuf):
            s_w, s_y, s_ss, s_r = sem(f"{tag}_w"), sem(f"{tag}_y"), sem(f"{tag}_squares"), sem(f"{tag}_rms")
            ss, r = small[:, 0:8], small[:, 8:16]
            with nc.Block() as block:
                @block.sync
                def _(sp):
                    for dst, src in w_rows:
                        sp.dma_start(dst, src).then_inc(s_w, 16)

                @block.tensor
                def _(pe):
                    pe.wait_ge(s_w, 16 * len(w_rows))
                    for i in range(n):
                        for half in range(2):
                            for k in range(KD):
                                mm = pe.matmul(bank[2 * i + half][:, :], catT[:, k, i * P:(i + 1) * P],
                                               wbuf[:, k, half * 512:half * 512 + 512], start=(k == 0), stop=(k == KD - 1))
                            mm.then_inc(s_y, 1)
                add_normed(block, n, gate_lat, gate_ctx, s_y, s_ss, s_r, ss, r, cut(0, D))

        def add_normed(block, n, gate_lat, gate_ctx, s_y, s_ss, s_r, ss, r, tmp):

            @block.scalar
            def _(act):
                for i in range(n):
                    for half in range(2):
                        act.wait_ge(s_y, 2 * i + half + 1)
                        act.activation(hT[:, 2 * i + half, :], bank[2 * i + half][:, :], ACT.Square,
                                       accum_out=ss[:, 2 * i + half:2 * i + half + 1]).then_inc(s_ss, 1)

            @block.gpsimd
            def _(pool):
                link = linker(pool, "pool")
                for i in range(n):
                    pool.wait_ge(s_ss, 2 * i + 2)
                    link(pool.tensor_tensor(r[:, i:i + 1], ss[:, 2 * i:2 * i + 1], ss[:, 2 * i + 1:2 * i + 2], ALU.add))
                    link(pool.tensor_scalar(r[:, i:i + 1], r[:, i:i + 1], 1.0 / D, EPS, ALU.mult, ALU.add))
                    pool.tensor_tensor(r[:, i:i + 1], r[:, i:i + 1], mhalf[:, 0:1], ALU.pow).then_inc(s_r, 1)

            @block.vector
            def _(dve):
                link = linker(dve, "dve")
                for i in range(n):
                    dve.wait_ge(s_r, i + 1)
                    gate = G[:, gate_lat if i < 2 else gate_ctx, :]
                    for half in range(2):
                        h = slice(half * 512, half * 512 + 512)
                        link(dve.scalar_tensor_tensor(tmp[:, h], bank[2 * i + half][:, :], r[:, i:i + 1], gate[:, h], ALU.mult, ALU.mult))
                    link(dve.tensor_tensor(X[:, i, :], X[:, i, :], tmp, ALU.add))

        def attention(tag, jobs, qT, kT_of, v_of, bias_of, sink_of, prob, probT, extra_sync=None, prep=None):
            s_s, s_m, s_e, s_n, s_t, s_tc, s_o, s_oc = (sem(f"{tag}_{x}") for x in
                ("scores", "max", "exp", "probs", "probs_turned", "turned_copied", "pv", "pv_copied"))
            s_b = sem(f"{tag}_bias")
            nm, rs, ri, sk = small[:, 32:34], small[:, 34:36], small[:, 36:38], small[:, 38:40]
            n_jobs = len(jobs)
            with nc.Block() as block:
                if prep:
                    prep(block, s_b)

                @block.tensor
                def _(pe):
                    def scores(j):
                        tile, c, part = jobs[j]
                        a = 64 * part
                        if j >= 2:
                            pe.wait_ge(s_e, j - 1)
                        lo = 0 if tile < 2 else 256
                        if tile < 2:
                            if prep:
                                pe.wait_ge(s_b, 4)
                            pe.matmul(bank[j % 2][:, :], qT[a:a + 64, c, tile * P:tile * P + P], kT_of(c)[a:a + 64, :], start=True, stop=False)
                            pe.matmul(bank[j % 2][:, 0:256], ident, bias_of(tile, c, part), start=False, stop=True).then_inc(s_s, 1)
                        else:
                            pe.matmul(bank[j % 2][:, 256:512], qT[a:a + 64, c, tile * P:tile * P + P], kT_of(c)[a:a + 64, 256:512],
                                      start=True, stop=True).then_inc(s_s, 1)

                    def turn(j):
                        tile = jobs[j][0]
                        pe.wait_ge(s_n, j + 1)
                        if j >= 2:
                            pe.wait_ge(s_tc, j - 1)
                        for b in range(0 if tile < 2 else 2, 4):
                            mm = pe.transpose(bank[2 + j % 2][:, b * P:b * P + P], prob[:, j % 2, b * P:b * P + P], ident)
                        mm.then_inc(s_t, 1)

                    def pv(j):
                        tile, c, part = jobs[j]
                        pe.wait_ge(s_tc, j + 1)
                        if j >= 4:
                            pe.wait_ge(s_oc, j // 2 - 1)
                        blocks = range(0 if tile < 2 else 2, 4)
                        for b in blocks:
                            mm = pe.matmul(bank[4 + (j // 2) % 2][64 * part:64 * part + 64, 0:P], v_of(b, c, part),
                                           probT[:, j % 2, b * P:b * P + P], start=(b == blocks[0]), stop=(b == 3), skip_group_check=True)
                        mm.then_inc(s_o, 1)
                    for j in range(n_jobs + 2):
                        if j < n_jobs:
                            scores(j)
                        if 1 <= j <= n_jobs:
                            turn(j - 1)
                        if j >= 2:
                            pv(j - 2)

                @block.vector
                def _(dve):
                    link = linker(dve, "dve")

                    def maximum(j):
                        lo = 0 if jobs[j][0] < 2 else 256
                        dve.wait_ge(s_s, j + 1)
                        if sink_of:
                            link(dve.tensor_reduce(nm[:, j % 2:j % 2 + 1], bank[j % 2][:, lo:512], AX.X, ALU.max))
                            dve.tensor_scalar(nm[:, j % 2:j % 2 + 1], nm[:, j % 2:j % 2 + 1], sink_of(*jobs[j][1:]), -1.0,
                                              ALU.max, ALU.mult).then_inc(s_m, 1)
                        else:
                            dve.tensor_reduce(nm[:, j % 2:j % 2 + 1], bank[j % 2][:, lo:512], AX.X, ALU.max, negate=True).then_inc(s_m, 1)

                    def normalise(j):
                        lo = 0 if jobs[j][0] < 2 else 256
                        m = j % 2
                        dve.wait_ge(s_e, j + 1)
                        if sink_of:
                            link(dve.tensor_tensor(rs[:, m:m + 1], rs[:, m:m + 1], sk[:, m:m + 1], ALU.add))
                        link(dve.reciprocal(ri[:, m:m + 1], rs[:, m:m + 1]))
                        dve.tensor_scalar(prob[:, m, lo:512], prob[:, m, lo:512], ri[:, m:m + 1], None, ALU.mult).then_inc(s_n, 1)

                    def copy_o(j):
                        tile, c, _ = jobs[2 * j]
                        dve.wait_ge(s_o, 2 * j + 2)
                        dve.tensor_copy(catT[:, c, tile * P:tile * P + P], bank[4 + j % 2][:, 0:P]).then_inc(s_oc, 1)
                    for j in range(n_jobs + 4):
                        if j < n_jobs:
                            maximum(j)
                        if 1 <= j <= n_jobs:
                            normalise(j - 1)
                        if j >= 4 and j % 2 == 0:
                            copy_o(j // 2 - 2)

                @block.scalar
                def _(act):
                    def expo(j):
                        m = j % 2
                        lo = 0 if jobs[j][0] < 2 else 256
                        act.wait_ge(s_m, j + 1)
                        if j >= 2:
                            act.wait_ge(s_t, j - 1)
                        if sink_of:
                            act.activation(sk[:, m:m + 1], sink_of(*jobs[j][1:]), ACT.Exp, bias=nm[:, m:m + 1])
                        act.activation(prob[:, m, lo:512], bank[m][:, lo:512], ACT.Exp, bias=nm[:, m:m + 1],
                                       accum_out=rs[:, m:m + 1]).then_inc(s_e, 1)

                    def copy_t(j):
                        lo = 0 if jobs[j][0] < 2 else 256
                        act.wait_ge(s_t, j + 1)
                        if j >= 2:
                            act.wait_ge(s_o, j - 1)
                        act.activation(probT[:, j % 2, lo:512], bank[2 + j % 2][:, lo:512], ACT.Copy).then_inc(s_tc, 1)
                    for j in range(n_jobs + 1):
                        if j < n_jobs:
                            expo(j)
                        if j >= 1:
                            copy_t(j - 1)

        norm_to_hT("l0_mix", 0, 0, range(4), cut(8192, 4, D))

        nqT, nkT, V, zT = cut(0, 4, NTOK), cut(2048, 4, NTOK), cut(4096, T, 512), cut(6144, 4, NTOK)
        CX = cut(8192, 12, 2, 260)
        WR = [cut(14432 + i * 4096, KD, 512) for i in range(3)]
        natb = cut(14432, 2, 8, 256)
        graw = catT[0:16, 4:8, :]
        wg = sb("gate_weights", [P, KD, 16])

        s_wi = [sem(f"in_w{i}") for i in range(3)]
        s_pj, s_pe_a, s_pe_v, s_wg, s_bias_in = (sem(x) for x in
            ("in_product", "in_copied_act", "in_copied_dve", "gate_w", "nat_bias_in"))
        WIN = t["ev_w_in"].rearrange("(k p) n -> p k n", p=P)
        with nc.Block() as block:
            @block.sync
            def _(sp):
                sp.dma_start(wg[:, :, :], WIN[:, :, 3584:3600]).then_inc(s_wg, 16)
                for c in range(7):
                    if c >= 3:
                        sp.wait_ge(s_pj, 4 * (c - 2))
                    sp.dma_start(WR[c % 3], WIN[:, :, c * 512:c * 512 + 512]).then_inc(s_wi[c % 3], 16)

            @block.gpsimd
            def _(pool):
                pool.memset(CX[:, :, :, 0:2], 0.0)
                pool.memset(CX[:, :, :, 258:260], 0.0)

            @block.tensor
            def _(pe):
                for c in range(7):
                    pe.wait_ge(s_wi[c % 3], 16 * (c // 3) + 16)
                    for m in range(4):
                        j = 4 * c + m
                        b = bank[j % 6][:, :]
                        if j >= 6:
                            pe.wait_ge((s_pe_a, s_pe_v)[j % 2], (j - 6) // 2 + 1)
                        for k in range(KD):
                            if c == 2:
                                mm = pe.matmul(b, hT[:, k, m * P:m * P + P], WR[c % 3][:, k, :], start=(k == 0), stop=(k == KD - 1))
                            else:
                                mm = pe.matmul(b, WR[c % 3][:, k, m * P:m * P + P], hT[:, k, :], start=(k == 0), stop=(k == KD - 1))
                        mm.then_inc(s_pj, 1)
                pe.wait_ge(s_wg, 16)
                for g in range(2):
                    for k in range(KD):
                        mm = pe.matmul(bank[6 + g][0:8, :], wg[:, k, 8 * g:8 * g + 8], hT[:, k, :], start=(k == 0), stop=(k == KD - 1))
                mm.then_inc(s_pj, 1)

            def evacuate(eng, parity, s_done):
                for j in range(parity, 28, 2):
                    c, m = divmod(j, 4)
                    eng.wait_ge(s_pj, j + 1)
                    b = bank[j % 6][:, :]
                    if c == 0:
                        dst, scale = nqT[:, m, :], 0.125
                    elif c == 1:
                        dst, scale = nkT[:, m, :], 1.0
                    elif c == 2:
                        dst, scale = V[:, m, :], 1.0
                    elif c < 6:
                        dst, scale = CX[:, 4 * (c - 3) + m, :, 2:258], 1.0
                        b = b.rearrange("p (s n) -> p s n", s=2)
                    else:
                        dst, scale = zT[:, m, :], 1.0
                    if parity == 0:
                        ins = eng.activation(dst, b, ACT.Copy, scale=scale)
                    else:
                        ins = eng.tensor_scalar(dst, b, scale, None, ALU.mult)
                    ins.then_inc(s_done, 1)

            @block.scalar
            def _(act):
                evacuate(act, 0, s_pe_a)
                act.wait_ge(s_pj, 29)
                act.activation(graw[0:8, 0, :], bank[6][0:8, :], ACT.Copy)
                act.activation(graw[0:8, 1, :], bank[7][0:8, :], ACT.Copy)

            @block.vector
            def _(dve):
                evacuate(dve, 1, s_pe_v)

        s_ncol = sem("nat_column_mask")

        def nat_bias(block, s_b):
            @block.sync
            def _(sp):
                sp.dma_start(natb, t["nat_bias"]).then_inc(s_bias_in, 16)

            @block.gpsimd
            def _(pool):
                pool.wait_ge(s_bias_in, 16)
                for i in range(2):
                    for g in range(2):
                        v = natb[:, i, 4 * g:4 * g + 4, :].rearrange("p h (r c) -> p (h r) c", c=64)
                        m = cst("natcol").rearrange("p (a c) -> p a c", a=1).to_broadcast([P, 16, 64])
                        pool.tensor_tensor(v, v, m, ALU.add).then_inc(s_b, 1)

        nat_jobs = [(tile, c, part) for tile in range(4) for c in range(4) for part in range(2)]
        attention("nat", nat_jobs, nqT, lambda c: nkT[:, c, :], lambda b, c, part: V[:, b, (2 * c + part) * HD:(2 * c + part + 1) * HD],
                  lambda tile, c, part: natb[:, tile, 2 * c + part, :], None, cut(20576, 2, 512), cut(21600, 2, 512), prep=nat_bias)

        def convolve(tag, n, src, dst, tap_col, acc):
            s_cv, s_si = sem(f"{tag}_convolved"), sem(f"{tag}_silu")
            with nc.Block() as block:
                @block.vector
                def _(dve):
                    link = linker(dve, "dve")
                    for c in range(n):
                        a = acc[:, c % 2, :].rearrange("p (s n) -> p s n", s=2)
                        if c >= 2:
                            dve.wait_ge(s_si, c - 1)
                        link(dve.tensor_scalar(a, src[:, c, :, 0:256], tap_col(0, c), None, ALU.mult))
                        for tap in range(1, TAPS):
                            ins = dve.scalar_tensor_tensor(a, src[:, c, :, tap:tap + 256], tap_col(tap, c), a, ALU.mult, ALU.add)
                            link(ins) if tap < TAPS - 1 else ins.then_inc(s_cv, 1)

                @block.scalar
                def _(act):
                    for c in range(n):
                        act.wait_ge(s_cv, c + 1)
                        act.activation(dst[:, c, :], acc[:, c % 2, :], ACT.Silu).then_inc(s_si, 1)

        FX = cut(14432, 12, NTOK)
        convolve("dn", 12, CX, FX, DNCONV, cut(20576, 2, 512))

        def gate_rows(tag, n, x, bias, alog, out_dt, out_g, sigmoid=None):
            s_1, s_2 = sem(f"{tag}_dve"), sem(f"{tag}_act")
            e, u, lnu, w, a = (hT[0:n, i, :] for i in range(5))
            a = gbias[0:n, 6:7]
            with nc.Block() as block:
                @block.vector
                def _(dve):
                    link = linker(dve, "dve")
                    link(dve.tensor_scalar(x, x, bias, None, ALU.add))
                    dve.scalar_tensor_tensor(e, x, -1.0, x, ALU.mult, ALU.min).then_inc(s_1, 1)
                    dve.wait_ge(s_2, 1)
                    dve.tensor_scalar(u, e, 1.0, None, ALU.add).then_inc(s_1, 1)
                    dve.wait_ge(s_1, 2)
                    link(dve.tensor_scalar(w, u, 1.0, None, ALU.subtract))
                    link(dve.tensor_tensor(e, e, w, ALU.subtract))
                    link(dve.reciprocal(w, u))
                    link(dve.tensor_tensor(e, e, w, ALU.mult))
                    dve.wait_ge(s_2, 2)
                    link(dve.tensor_tensor(e, e, lnu, ALU.add))
                    link(dve.scalar_tensor_tensor(out_dt, x, 0.0, e, ALU.max, ALU.add))
                    dve.wait_ge(s_2, 3)
                    link(dve.tensor_scalar(a, a, -1.0, None, ALU.mult))
                    dve.tensor_scalar(out_g, out_dt, a, None, ALU.mult)

                @block.scalar
                def _(act):
                    act.wait_ge(s_1, 1)
                    act.activation(e, e, ACT.Exp).then_inc(s_2, 1)
                    act.wait_ge(s_1, 2)
                    act.activation(lnu, u, ACT.Ln).then_inc(s_2, 1)
                    act.activation(a, alog, ACT.Exp).then_inc(s_2, 1)
                    if sigmoid is not None:
                        act.activation(sigmoid, sigmoid, ACT.Sigmoid)

        def spread(col, n, w):
            return col.rearrange("p (a b) -> p a b", b=1).to_broadcast([P, n, w])

        def heads(v, n):
            return v.rearrange("p (h e) -> p h e", h=n)

        gate_rows("dn_gates", 8, graw[0:8, 1, :], gbias[0:8, 0:1], gbias[0:8, 1:2], graw[0:8, 2, :], graw[0:8, 3, :],
                  sigmoid=graw[0:8, 0, :])

        dc = sb("delta_cols", [P, 9, 32])
        BETA, GS, GC, NGC, GL, EGC, EGL, EKD, BEG = (dc[:, i, :] for i in range(9))
        RL = small[:, 64:96]
        sq = cut(20576, 8, 512)
        s_q2, s_ssp, s_sse, s_rl, s_bc, s_nrm = (sem(f"dn_{x}") for x in
            ("squares", "norm_sums", "norm_sums_eps", "rnorm", "rnorm_spread", "normed"))
        with nc.Block() as block:
            @block.scalar
            def _(act):
                for c in range(8):
                    act.activation(sq[:, c, :], FX[:, c, :], ACT.Square).then_inc(s_q2, 1)

            @block.tensor
            def _(pe):
                for c in range(8):
                    pe.wait_ge(s_q2, c + 1)
                    for i in range(T):
                        mm = pe.matmul(bank[0][:, c * T + i:c * T + i + 1], sq[:, c, i * P:i * P + P], ones[:, 0:1], start=True, stop=True)
                mm.then_inc(s_ssp, 1)
                pe.wait_ge(s_rl, 1)
                for c in range(8):
                    if c >= 4:
                        pe.wait_ge(s_nrm, c - 3)
                    for i in range(T):
                        mm = pe.matmul(bank[1 + c % 4][:, i * P:i * P + P], RL[:, c * T + i:c * T + i + 1].to_broadcast([P, P]), ident,
                                       start=True, stop=True)
                    mm.then_inc(s_bc, 1)

            @block.gpsimd
            def _(pool):
                link = linker(pool, "pool")
                pool.wait_ge(s_sse, 1)
                link(pool.tensor_tensor(RL, RL, mhalf[:, 0:32], ALU.pow))
                link(pool.tensor_scalar(RL[:, 0:16], RL[:, 0:16], float(P) ** -0.5, None, ALU.mult))
                pool.sem_inc(s_rl, 1)

            @block.vector
            def _(dve):
                dve.wait_ge(s_ssp, 1)
                dve.tensor_scalar(RL, bank[0][:, 0:32], EPS, None, ALU.add).then_inc(s_sse, 1)
                for c in range(8):
                    dve.wait_ge(s_bc, c + 1)
                    dve.tensor_tensor(FX[:, c, :], FX[:, c, :], bank[1 + c % 4][:, :], ALU.mult).then_inc(s_nrm, 1)

        def columns_and_turns(tag, n_raw, raw, cols_out, n_g, gs, gc, ngc, gl, ekd, exps, after, turned):
            s_gt, s_gcp, s_cs, s_gl, s_ex, s_kv, s_kva, s_kvv = (sem(f"{tag}_{x}") for x in
                ("gates_turned", "gates_copied", "cumsums", "sums_copied", "exponents", "turned", "turned_copied_act", "turned_copied_dve"))
            w = T * n_raw
            nj = len(turned)
            with nc.Block() as block:
                @block.tensor
                def _(pe):
                    for g, r in enumerate(raw):
                        for i in range(T):
                            mm = pe.transpose(bank[0][:, w * g + n_raw * i:w * g + n_raw * (i + 1)], r[:, i * P:i * P + P], ident[0:n_raw, 0:n_raw])
                    mm.then_inc(s_gt, 1)

                    def turn(j):
                        if j >= 4:
                            pe.wait_ge((s_kva, s_kvv)[j % 2], (j - 4) // 2 + 1)
                        for b, src in enumerate(turned[j][0]):
                            mm = pe.transpose(bank[4 + j % 4][:, b * P:b * P + P], src, ident)
                        mm.then_inc(s_kv, 1)
                    for j in range(min(4, nj)):
                        turn(j)
                    pe.wait_ge(s_gcp, len(raw))
                    h = n_raw // 2
                    for i in range(T):
                        for d in range(2):
                            a = n_raw * i + h * d
                            pe.matmul(bank[1][:, a:a + h], cum[d], gs[:, a:a + h], start=True, stop=True)
                            mm = pe.matmul(bank[1][:, w + a:w + a + h], ones, gs[:, a:a + h], start=True, stop=True)
                    mm.then_inc(s_cs, 1)
                    for j in range(4, nj):
                        turn(j)

                def copy(eng, parity, s_done, lo, hi):
                    for j in range(lo + (parity - lo) % 2, hi, 2):
                        eng.wait_ge(s_kv, j + 1)
                        n = P * len(turned[j][0])
                        if parity == 0:
                            eng.activation(turned[j][1], bank[4 + j % 4][:, 0:n], ACT.Copy).then_inc(s_done, 1)
                        else:
                            eng.tensor_copy(turned[j][1], bank[4 + j % 4][:, 0:n]).then_inc(s_done, 1)

                @block.vector
                def _(dve):
                    link = linker(dve, "dve")
                    dve.wait_ge(s_gt, 1)
                    for g, dst in enumerate(cols_out):
                        dve.tensor_copy(dst, bank[0][:, w * g:w * g + w]).then_inc(s_gcp, 1)
                    copy(dve, 1, s_kvv, 0, min(4, nj))
                    dve.wait_ge(s_cs, 1)
                    link(dve.tensor_copy(gc, bank[1][:, 0:w]))
                    link(dve.tensor_copy(gl, bank[1][:, w:2 * w]))
                    link(dve.tensor_scalar(ngc, gc, -1.0, None, ALU.mult))
                    dve.tensor_tensor(ekd, gl, gc, ALU.subtract).then_inc(s_gl, 1)
                    copy(dve, 1, s_kvv, 4, nj)
                    dve.wait_ge(s_ex, 3)
                    after(dve)

                @block.scalar
                def _(act):
                    copy(act, 0, s_kva, 0, min(4, nj))
                    act.wait_ge(s_gl, 1)
                    for dst, src in exps:
                        act.activation(dst, src, ACT.Exp).then_inc(s_ex, 1)
                    copy(act, 0, s_kva, 4, nj)

        KT, VT = cut(0, T, 512), cut(2048, T, 512)
        columns_and_turns("dn_cols", 8, (graw[0:8, 0, :], graw[0:8, 3, :]), (BETA, GS), 8, GS, GC, NGC, GL, EKD,
                          ((EGC, GC), (EGL, GL), (EKD, EKD)),
                          lambda dve: dve.tensor_tensor(BEG, BETA, EGC, ALU.mult),
                          [([FX[:, c0 + h, i * P:i * P + P] for h in range(4)], dst[:, i, :]) for c0, dst in ((4, KT), (8, VT)) for i in range(T)])

        def col(v, i, d, h, w=4):
            a = (2 * w) * i + w * d + h
            return v[:, a:a + 1]

        KB = cut(8192, 2, 4, NTOK)
        AT, QA = cut(20576, 8, 512), cut(24672, 8, 512)
        DT = cut(12288, 2, 512)
        LMT = cut(4096, 2, LEVELS, P)
        s_bs, s_kb, s_lm, s_pd, s_pa, s_pq, s_dt, s_am, s_qm = (sem(f"dn_{x}") for x in
            ("beta_spread", "beta_keys", "level_masks", "log_decay", "kk", "kq", "decay", "a_masked", "q_masked"))
        with nc.Block() as block:
            @block.sync
            def _(sp):
                sp.dma_start(LMT, t["levels"]).then_inc(s_lm, 16)

            @block.tensor
            def _(pe):
                for d in range(2):
                    for h in range(4):
                        j = 4 * d + h
                        if j >= 2:
                            pe.wait_ge(s_kb, j - 1)
                        for i in range(T):
                            mm = pe.matmul(bank[6 + j % 2][:, i * P:i * P + P], col(BETA, i, d, h).to_broadcast([P, P]), ident, start=True, stop=True)
                        mm.then_inc(s_bs, 1)
                for g in range(8):
                    d, i = divmod(g, T)
                    tk = slice(i * P, i * P + P)
                    if g >= 2:
                        pe.wait_ge(s_dt, g - 1)
                    pe.matmul(quad(g % 2), ident, neg[d].rearrange("p (a c) -> p a c", a=1).to_broadcast([P, 4, P]), start=True, stop=False, skip_group_check=True)
                    for h in range(4):
                        mm = pe.matmul(quad(g % 2)[:, h, :], col(GS, i, d, h).to_broadcast([P, P]), cum[d], start=False, stop=(h == 3), skip_group_check=True)
                    mm.then_inc(s_pd, 1)
                    if g >= 2:
                        pe.wait_ge(s_am, g - 1)
                    pe.wait_ge(s_kb, 4 * d + 4)
                    for h in range(4):
                        mm = pe.matmul(quad(2 + g % 2)[:, h, :], FX[:, 4 + h, tk], KB[:, d, h, tk], start=True, stop=True)
                    mm.then_inc(s_pa, 1)
                    if g >= 2:
                        pe.wait_ge(s_qm, g - 1)
                    for h in range(4):
                        mm = pe.matmul(quad(4 + g % 2)[:, h, :], FX[:, 4 + h, tk], FX[:, h, tk], start=True, stop=True)
                    mm.then_inc(s_pq, 1)

            @block.scalar
            def _(act):
                for g in range(8):
                    d, i = divmod(g, T)
                    act.wait_ge(s_pd, g + 1)
                    if g >= 2:
                        act.wait_ge(s_qm, g - 1)
                    for h in range(4):
                        ins = act.activation(DT[:, g % 2, h * P:h * P + P], quad(g % 2)[:, h, :], ACT.Exp, bias=col(NGC, i, d, h))
                    ins.then_inc(s_dt, 1)

            @block.vector
            def _(dve):
                for j in range(8):
                    dve.wait_ge(s_bs, j + 1)
                    dve.tensor_tensor(KB[:, j // 4, j % 4, :], FX[:, 4 + j % 4, :], bank[6 + j % 2][:, :], ALU.mult).then_inc(s_kb, 1)
                for g in range(8):
                    dve.wait_ge(s_dt, g + 1)
                    dve.wait_ge(s_pa, g + 1)
                    dve.tensor_tensor(AT[:, g, :], bank[2 + g % 2][:, :], DT[:, g % 2, :], ALU.mult).then_inc(s_am, 1)
                    dve.wait_ge(s_pq, g + 1)
                    dve.tensor_tensor(QA[:, g, :], bank[4 + g % 2][:, :], DT[:, g % 2, :], ALU.mult).then_inc(s_qm, 1)

        XI, XT = cut(8192, 8, 512), cut(16480, 8, 512)
        T1 = hT[:, :, :]
        BT = cut(12288, 4, 512)
        s_bt, s_xt0, s_a, s_x0, s_t1, s_b, s_up = (sem(f"inv_{x}") for x in
            ("level_block", "first_xt", "first_product", "first_x", "product_copied", "second_product", "updated"))
        with nc.Block() as block:
            @block.gpsimd
            def _(pool):
                pool.wait_ge(s_lm, 16)
                for n in range(8 * LEVELS):
                    l, g = divmod(n, 8)
                    if n >= 4:
                        pool.wait_ge(s_a, n - 3)
                        pool.wait_ge(s_xt0, min(n - 3, 8))
                    m = LMT[:, g // 4, l, :].rearrange("p (a c) -> p a c", a=1).to_broadcast([P, 4, P])
                    pool.tensor_tensor(heads(BT[:, n % 4, :], 4), heads(AT[:, g, :], 4), m, ALU.mult).then_inc(s_bt, 1)
                    if l == 0:
                        pool.wait_ge(s_bt, n + 1)
                        pool.tensor_tensor(heads(XT[:, g, :], 4), ident.rearrange("p (a c) -> p a c", a=1).to_broadcast([P, 4, P]),
                                           heads(BT[:, n % 4, :], 4), ALU.subtract).then_inc(s_xt0, 1)

            @block.tensor
            def _(pe):
                for l in range(LEVELS):
                    for g in range(8):
                        n = 8 * l + g
                        pe.wait_ge(s_bt, n + 1)
                        if n >= 4:
                            pe.wait_ge(s_x0, n - 3) if n < 12 else pe.wait_ge(s_t1, n - 11)
                        if l == 1:
                            pe.wait_ge(s_x0, g + 1)
                        if l >= 2:
                            pe.wait_ge(s_up, 8 * (l - 2) + g + 1)
                        for h in range(4):
                            mm = pe.matmul(quad(n % 4)[:, h, :], BT[:, n % 4, h * P:h * P + P], ident if l == 0 else XI[:, g, h * P:h * P + P],
                                           start=True, stop=True)
                        mm.then_inc(s_a, 1)
                    if l == 0:
                        continue
                    for g in range(8):
                        m = 8 * (l - 1) + g
                        pe.wait_ge(s_t1, m + 1)
                        pe.wait_ge(s_xt0, g + 1) if l == 1 else None
                        if m >= 2:
                            pe.wait_ge(s_up, m - 1)
                        for h in range(4):
                            hs = slice(h * P, h * P + P)
                            if l < LEVELS - 1:
                                pe.matmul(quad(4 + 2 * (m % 2))[:, h, :], XT[:, g, hs], T1[:, g, hs], start=True, stop=True)
                            mm = pe.matmul(quad(5 + 2 * (m % 2))[:, h, :], T1[:, g, hs], XT[:, g, hs], start=True, stop=True)
                        mm.then_inc(s_b, 1)

            @block.scalar
            def _(act):
                for n in range(8, 8 * LEVELS):
                    act.wait_ge(s_a, n + 1)
                    act.activation(T1[:, n % 8, :], bank[n % 4][:, :], ACT.Copy).then_inc(s_t1, 1)

            @block.vector
            def _(dve):
                for g in range(8):
                    dve.wait_ge(s_a, g + 1)
                    dve.tensor_tensor(heads(XI[:, g, :], 4), ident.rearrange("p (a c) -> p a c", a=1).to_broadcast([P, 4, P]),
                                      quad(g % 4), ALU.subtract).then_inc(s_x0, 1)
                for m in range(8 * (LEVELS - 1)):
                    l, g = m // 8 + 1, m % 8
                    dve.wait_ge(s_b, m + 1)
                    if l < LEVELS - 1:
                        dve.tensor_tensor(XI[:, g, :], XI[:, g, :], bank[4 + 2 * (m % 2)][:, :], ALU.subtract)
                    dve.tensor_tensor(XT[:, g, :], XT[:, g, :], bank[5 + 2 * (m % 2)][:, :], ALU.subtract).then_inc(s_up, 1)

        U, WT, KDV = cut(8192, 8, 512), cut(20576, 8, 512), hT[:, :, :]
        BV, BW = cut(4096, 2, 512), cut(5120, 2, 512)
        s_bv, s_bw, s_pu, s_cu, s_cw = (sem(f"uw_{x}") for x in ("beta_v", "beta_k", "products", "u_copied", "w_copied"))

        def gcol(v, g, w=4):
            d, i = divmod(g, T)
            a = 2 * w * i + w * d
            return v[:, a:a + w]
        with nc.Block() as block:
            @block.vector
            def _(dve):
                for g in range(9):
                    if g < 8:
                        if g >= 2:
                            dve.wait_ge(s_pu, g - 1)
                        dve.tensor_tensor(heads(BV[:, g % 2, :], 4), heads(VT[:, g % T, :], 4), spread(gcol(BETA, g), 4, P), ALU.mult).then_inc(s_bv, 1)
                    if g >= 1:
                        dve.wait_ge(s_pu, g)
                        dve.tensor_copy(WT[:, g - 1, :], bank[2 + (g - 1) % 2][:, :]).then_inc(s_cw, 1)

            @block.gpsimd
            def _(pool):
                for g in range(8):
                    if g >= 2:
                        pool.wait_ge(s_pu, g - 1)
                    pool.tensor_tensor(heads(BW[:, g % 2, :], 4), heads(KT[:, g % T, :], 4), spread(gcol(BEG, g), 4, P), ALU.mult).then_inc(s_bw, 1)
                    pool.tensor_tensor(heads(KDV[:, g, :], 4), heads(KT[:, g % T, :], 4), spread(gcol(EKD, g), 4, P), ALU.mult)

            @block.tensor
            def _(pe):
                for g in range(8):
                    pe.wait_ge(s_bv, g + 1)
                    pe.wait_ge(s_bw, g + 1)
                    if g >= 2:
                        pe.wait_ge(s_cu, g - 1)
                        pe.wait_ge(s_cw, g - 1)
                    for h in range(4):
                        hs = slice(h * P, h * P + P)
                        pe.matmul(quad(g % 2)[:, h, :], XT[:, g, hs], BV[:, g % 2, hs], start=True, stop=True)
                        mm = pe.matmul(quad(2 + g % 2)[:, h, :], BW[:, g % 2, hs], XT[:, g, hs], start=True, stop=True)
                    mm.then_inc(s_pu, 1)

            @block.scalar
            def _(act):
                for g in range(8):
                    act.wait_ge(s_pu, g + 1)
                    act.activation(U[:, g, :], bank[g % 2][:, :], ACT.Copy).then_inc(s_cu, 1)

        S, VN = cut(12288, 2, 512), cut(13312, 2, 512)
        O = cut(16480, T, 512)
        tmp = cut(18528, 2, 512)
        s_s0, s_p1, s_vn, s_p2, s_se, s_st = (sem(f"scan_{x}") for x in
            ("state_zero", "from_state", "v_new", "products", "state_decayed", "state"))
        with nc.Block() as block:
            @block.gpsimd
            def _(pool):
                pool.memset(S, 0.0).then_inc(s_s0, 1)
                for n in range(8):
                    i, d = divmod(n, 2)
                    g = d * T + CHUNK_ORDER[d][i]
                    pool.wait_ge(s_p1, n + 1)
                    if n >= 2:
                        pool.wait_ge(s_st, n - 1)
                    else:
                        pool.wait_ge(s_s0, 1)
                    pool.tensor_tensor(heads(S[:, d, :], 4), heads(S[:, d, :], 4), spread(gcol(EGL, g), 4, P), ALU.mult).then_inc(s_se, 1)

            @block.tensor
            def _(pe):
                pe.wait_ge(s_s0, 1)
                for i in range(T):
                    for d in range(2):
                        n, tile = 2 * i + d, CHUNK_ORDER[d][i]
                        g = d * T + tile
                        if n >= 2:
                            pe.wait_ge(s_st, n - 1)
                        for h in range(4):
                            hs = slice(h * P, h * P + P)
                            pe.matmul(quad(d)[:, h, :], WT[:, g, hs], S[:, d, hs], start=True, stop=True)
                            mm = pe.matmul(quad(2 + d)[:, h, :], FX[:, h, tile * P:tile * P + P], S[:, d, hs], start=True, stop=True)
                        mm.then_inc(s_p1, 1)
                    for d in range(2):
                        n, tile = 2 * i + d, CHUNK_ORDER[d][i]
                        g = d * T + tile
                        pe.wait_ge(s_vn, n + 1)
                        for h in range(4):
                            hs = slice(h * P, h * P + P)
                            pe.matmul(quad(6 + d)[:, h, :], KDV[:, g, hs], VN[:, d, hs], start=True, stop=True)
                        for h in range(4):
                            hs = slice(h * P, h * P + P)
                            mm = pe.matmul(quad(4 + d)[:, h, :], QA[:, g, hs], VN[:, d, hs], start=True, stop=True)
                        mm.then_inc(s_p2, 1)

            @block.vector
            def _(dve):
                link = linker(dve, "dve")
                for i in range(T):
                    for d in range(2):
                        n, g = 2 * i + d, d * T + CHUNK_ORDER[d][i]
                        dve.wait_ge(s_p1, n + 1)
                        dve.tensor_tensor(VN[:, d, :], U[:, g, :], bank[d][:, :], ALU.subtract).then_inc(s_vn, 1)
                    for d in range(2):
                        n, g = 2 * i + d, d * T + CHUNK_ORDER[d][i]
                        last = dve.tensor_tensor(heads(tmp[:, d, :], 4), quad(2 + d), spread(gcol(EGC, g), 4, P), ALU.mult)
                    link(last)
                    for d in range(2):
                        n, tile = 2 * i + d, CHUNK_ORDER[d][i]
                        dve.wait_ge(s_p2, n + 1)
                        dve.wait_ge(s_se, n + 1)
                        dve.tensor_tensor(S[:, d, :], S[:, d, :], bank[6 + d][:, :], ALU.add).then_inc(s_st, 1)
                        if i in (0, 2):
                            link(dve.tensor_tensor(O[:, tile, :], tmp[:, d, :], bank[4 + d][:, :], ALU.add))
                        else:
                            link(dve.tensor_tensor(O[:, tile, :], O[:, tile, :], tmp[:, d, :], ALU.add))
                            link(dve.tensor_tensor(O[:, tile, :], O[:, tile, :], bank[4 + d][:, :], ALU.add))

        osq, zs, orr = cut(8192, 16, P), cut(0, 4, NTOK), small[:, 96:112]
        s_q, s_oss, s_or, s_on, s_ot, s_zs = (sem(f"gn_{x}") for x in ("squares", "sums", "rms", "normed", "turned", "silu_z"))
        with nc.Block() as block:
            @block.scalar
            def _(act):
                act.activation(zs, zT, ACT.Silu).then_inc(s_zs, 1)

            @block.vector
            def _(dve):
                link = linker(dve, "dve")
                o3 = O.rearrange("p t (h e) -> p (t h) e", h=4)
                link(dve.tensor_tensor(osq, o3, o3, ALU.mult))
                dve.tensor_reduce(orr, osq, AX.X, ALU.add).then_inc(s_oss, 1)
                dve.wait_ge(s_or, 1)
                dve.tensor_tensor(o3, o3, spread(orr, 16, P), ALU.mult).then_inc(s_on, 1)
                dve.wait_ge(s_zs, 1)
                for h in range(4):
                    dve.wait_ge(s_ot, h + 1)
                    dve.scalar_tensor_tensor(catT[:, 4 + h, :], bank[h][:, :], DNNORM, zs[:, h, :], ALU.mult, ALU.mult)

            @block.gpsimd
            def _(pool):
                link = linker(pool, "pool")
                pool.wait_ge(s_oss, 1)
                link(pool.tensor_scalar(orr, orr, 1.0 / P, EPS, ALU.mult, ALU.add))
                pool.tensor_tensor(orr, orr, mhalf[:, 0:16], ALU.pow).then_inc(s_or, 1)

            @block.tensor
            def _(pe):
                pe.wait_ge(s_on, 1)
                for h in range(4):
                    for i in range(T):
                        mm = pe.transpose(bank[h][:, i * P:i * P + P], O[:, i, h * P:h * P + P], ident)
                    mm.then_inc(s_ot, 1)

        wout = cut(8192, KD, D)
        project_and_add("l0_out", [(wout, t["ev_w_out"].rearrange("(k p) n -> p k n", p=P))], 4, 0, 4, wout)

        norm_to_hT("l0_ffn", 0, 1, range(4), cut(0, 4, D))
        gT = cut(0, NF, NTOK)
        W13 = [cut(11264 + i * 4096, 2, KD, 256) for i in range(2)]
        NW2 = 4
        W2 = [cut(19456 + i * 2048, 2, D) for i in range(NW2)]
        sl = cut(27648, 2, 512)
        s_w13 = [sem(f"ffn_w13_{i}") for i in range(2)]
        s_w2 = [sem(f"ffn_w2_{i}") for i in range(NW2)]
        s_h1, s_h3, s_sl, s_g = (sem(f"ffn_{x}") for x in ("h1", "h3", "silu", "gated"))
        w1v = t["ffn_w1"].rearrange("(k p) (c w) -> p k c w", p=P, w=256)
        w3v = t["ffn_w3"].rearrange("(k p) (c w) -> p k c w", p=P, w=256)
        w2v = t["ffn_w2"].rearrange("(c two p) n -> p c two n", p=P, two=2)
        NC = NF // 2
        with nc.Block() as block:
            @block.sync
            def _(sp):
                def load(c, s):
                    for m, w in enumerate((w1v, w3v)):
                        sp.dma_start(W13[s][:, m, :, :], w[:, :, c, :]).then_inc(s_w13[s], 16)
                load(0, 0)
                load(1, 1)
                for s in range(NW2):
                    sp.dma_start(W2[s], w2v[:, s, :, :]).then_inc(s_w2[s], 16)
                for c in range(2, NC):
                    sp.wait_ge(s_h3, 2 * (c - 1))
                    load(c, c % 2)

            @block.tensor
            def _(pe):
                for c in range(NC):
                    pe.wait_ge(s_w13[c % 2], 32 * (c // 2) + 32)
                    for f in range(2):
                        n = 2 * c + f
                        for m, s_h in enumerate((s_h1, s_h3)):
                            if n >= 2:
                                pe.wait_ge((s_sl, s_g)[m], n - 1)
                            for k in range(KD):
                                mm = pe.matmul(bank[4 * m + n % 2][:, :], W13[c % 2][:, m, k, f * P:f * P + P], hT[:, k, :], start=(k == 0), stop=(k == KD - 1))
                            mm.then_inc(s_h, 1)

            @block.scalar
            def _(act):
                for n in range(NF):
                    act.wait_ge(s_h1, n + 1)
                    if n >= 2:
                        act.wait_ge(s_g, n - 1)
                    act.activation(sl[:, n % 2, :], bank[n % 2][:, :], ACT.Silu).then_inc(s_sl, 1)

            @block.vector
            def _(dve):
                for n in range(NF):
                    dve.wait_ge(s_sl, n + 1)
                    dve.wait_ge(s_h3, n + 1)
                    dve.tensor_tensor(gT[:, n, :], sl[:, n % 2, :], bank[4 + n % 2][:, :], ALU.mult).then_inc(s_g, 1)

        s_dn, s_dy, s_dss, s_dr = (sem(f"ffn_{x}") for x in ("down", "down_y", "down_squares", "down_rms"))
        with nc.Block() as block:
            @block.sync
            def _(sp):
                for c in range(NW2, NC):
                    sp.wait_ge(s_dn, c - NW2 + 1)
                    sp.dma_start(W2[c % NW2], w2v[:, c, :, :]).then_inc(s_w2[c % NW2], 16)

            @block.tensor
            def _(pe):
                for c in range(NC):
                    pe.wait_ge(s_w2[c % NW2], 16 * (c // NW2) + 16)
                    for f in range(2):
                        for i in range(T):
                            for half in range(2):
                                mm = pe.matmul(bank[2 * i + half][:, :], gT[:, 2 * c + f, i * P:i * P + P], W2[c % NW2][:, f, half * 512:half * 512 + 512],
                                               start=(c == 0 and f == 0), stop=(c == NC - 1 and f == 1))
                    mm.then_inc(s_dn, 1)
                pe.wait_ge(s_dn, NC)
                pe.sem_inc(s_dy, 8)
            add_normed(block, 4, 1, 5, s_dy, s_dss, s_dr, small[:, 0:8], small[:, 8:16], cut(27648, D))

        nc.clear_and_free_semaphores(stage_sems)
        nc.all_engine_barrier()
        stage_sems = []

        norm_to_hT("l1_mix", 1, 0, range(4), cut(0, 4, D))
        qT, kT, V1, Z1 = cut(0, 4, LAT), cut(1024, NTOK), cut(1536, T, P), cut(2048, 2, 512)
        CS = cut(3072, 8, 2, 260)
        dtr = catT[0:16, 4:8, :]
        WI = cut(7232, KD, OD_IN)
        cuts = ((0, 512), (512, 1280), (1280, 1792), (1792, OD_IN))
        s_oi = [sem(f"od_in_w{i}") for i in range(4)]
        s_oj, s_oa, s_ov = sem("od_in_product"), sem("od_in_copied_act"), sem("od_in_copied_dve")
        WOD = t["od_w_in"].rearrange("(k p) n -> p k n", p=P)
        od_jobs = [("q", c) for c in range(4)] + [("k", 0), ("v", 0)] + [("z", i) for i in range(2)] + [("conv", c) for c in range(8)] + [("dt", 0)]
        od_part = {"q": 0, "k": 1, "v": 1, "z": 1}
        with nc.Block() as block:
            @block.sync
            def _(sp):
                for i, (a, b) in enumerate(cuts):
                    sp.dma_start(WI[:, :, a:b], WOD[:, :, a:b]).then_inc(s_oi[i], 16)

            @block.gpsimd
            def _(pool):
                pool.memset(CS[:, :, :, 0:2], 0.0)
                pool.memset(CS[:, :, :, 258:260], 0.0)

            @block.tensor
            def _(pe):
                for j, (kind, c) in enumerate(od_jobs):
                    pe.wait_ge(s_oi[od_part.get(kind, 2 if c < 4 and kind == "conv" else 3)], 16)
                    if j >= 8:
                        pe.wait_ge((s_oa, s_ov)[j % 2], (j - 8) // 2 + 1)
                    b = bank[j % 8]
                    for i in range(T if kind == "v" else 1):
                        for k in range(KD):
                            st, sp_ = k == 0, k == KD - 1
                            if kind == "q":
                                for part in range(2):
                                    a = (c + 4 * part) * HD
                                    mm = pe.matmul(b[64 * part:64 * part + 64, 0:LAT], WI[:, k, a:a + HD], hT[:, k, 0:LAT], start=st, stop=sp_, skip_group_check=True)
                            elif kind == "k":
                                mm = pe.matmul(b[:, :], WI[:, k, 512:640], hT[:, k, :], start=st, stop=sp_)
                            elif kind == "v":
                                mm = pe.matmul(b[:, i * P:i * P + P], hT[:, k, i * P:i * P + P], WI[:, k, 640:768], start=st, stop=sp_)
                            elif kind == "z":
                                mm = pe.matmul(b[:, :], hT[:, k, c * P:c * P + P], WI[:, k, 768:1280], start=st, stop=sp_)
                            elif kind == "conv":
                                mm = pe.matmul(b[:, :], WI[:, k, 1280 + c * P:1408 + c * P], hT[:, k, :], start=st, stop=sp_)
                            else:
                                mm = pe.matmul(b[0:16, :], WI[:, k, 2304:2320], hT[:, k, :], start=st, stop=sp_)
                    mm.then_inc(s_oj, 1)

            def od_copy(eng, parity, s_done):
                for j in range(parity, len(od_jobs), 2):
                    kind, c = od_jobs[j]
                    eng.wait_ge(s_oj, j + 1)
                    b, scale = bank[j % 8][:, :], 1.0
                    if kind == "q":
                        dst, b, scale = qT[:, c, :], bank[j % 8][:, 0:LAT], 0.125
                    elif kind == "k":
                        dst = kT
                    elif kind == "v":
                        dst = V1.rearrange("p t n -> p (t n)")
                    elif kind == "z":
                        dst = Z1[:, c, :]
                    elif kind == "conv":
                        dst, b = CS[:, c, :, 2:258], b.rearrange("p (s n) -> p s n", s=2)
                    else:
                        dst, b = dtr[:, 0, :], bank[j % 8][0:16, :]
                    if parity == 0:
                        eng.activation(dst, b, ACT.Copy, scale=scale).then_inc(s_done, 1)
                    else:
                        eng.tensor_scalar(dst, b, scale, None, ALU.mult).then_inc(s_done, 1)

            @block.scalar
            def _(act):
                od_copy(act, 0, s_oa)

            @block.vector
            def _(dve):
                od_copy(dve, 1, s_ov)

        rt = cut(7232, 2, 2, LAT)
        s_rp, s_rd = sem("rope_turned"), sem("rope_done")
        with nc.Block() as block:
            @block.tensor
            def _(pe):
                for c in range(5):
                    src = qT[:, c, :] if c < 4 else kT[:, 0:LAT]
                    if c >= 2:
                        pe.wait_ge(s_rd, c - 1)
                    pe.matmul(bank[c % 2][:, 0:LAT], cst("rot"), src, start=True, stop=True).then_inc(s_rp, 1)

            @block.vector
            def _(dve):
                link = linker(dve, "dve")
                for c in range(5):
                    src = qT[:, c, :] if c < 4 else kT[:, 0:LAT]
                    dve.wait_ge(s_rp, c + 1)
                    link(dve.tensor_tensor(rt[:, c % 2, 0, :], src, cst("cos"), ALU.mult))
                    link(dve.tensor_tensor(rt[:, c % 2, 1, :], bank[c % 2][:, 0:LAT], cst("sin"), ALU.mult))
                    ins = dve.tensor_tensor(src, rt[:, c % 2, 0, :], rt[:, c % 2, 1, :], ALU.add)
                    link(ins) if c >= 5 else ins.then_inc(s_rd, 1)
                    dve.wait_ge(s_rd, c + 1)

        band = cst("band").rearrange("p (t k) -> p t k", t=2)
        wa_jobs = [(tile, c, part) for tile in range(2) for c in range(4) for part in range(2)]
        attention("win", wa_jobs, qT, lambda c: kT, lambda b, c, part: V1[:, b, part * HD:part * HD + HD],
                  lambda tile, c, part: band[:, tile, :], lambda c, part: rowcol[:, c + 4 * part:c + 4 * part + 1],
                  cut(7232, 2, 512), cut(8256, 2, 512))

        FS = cut(9280, 8, NTOK)
        convolve("ssd", 8, CS, FS, SSDCONV, cut(7232, 2, 512))
        gate_rows("ssd_gates", 16, dtr[:, 0, :], gbias[:, 2:3], gbias[:, 3:4], dtr[:, 1, :], dtr[:, 2, :])
        sc = cut(13376, 9, 64)
        DTC, DA, AC, NAC, AL, EAC, EAL, EDS, DTD = (sc[:, i, :] for i in range(9))
        XT1, BT1 = cut(13952, T, 512), cut(16000, T, 2 * P)
        columns_and_turns("ssd_cols", 16, (dtr[:, 1, :], dtr[:, 2, :]), (DTC, DA), 16, DA, AC, NAC, AL, EDS,
                          ((EAC, AC), (EAL, AL), (EDS, EDS)),
                          lambda dve: dve.tensor_tensor(DTD, DTC, EDS, ALU.mult),
                          [([FS[:, c, i * P:i * P + P] for c in range(4)], XT1[:, i, :]) for i in range(T)]
                          + [([FS[:, 4 + c, i * P:i * P + P] for c in range(2)], BT1[:, i, :]) for i in range(T)])

        XS, XD = cut(17024, 2, 512), cut(18048, 2, 512)
        H, Y = cut(19072, 2, 512), cut(20096, 2, 512)
        LT, MT = cut(21120, 2, 512), cut(22144, 2, 512)
        yt = cut(23168, 512)

        def hcol(v, tile, d):
            return v[:, 16 * tile + 8 * d:16 * tile + 8 * d + 8]
        ssd_steps = [(i, d, CHUNK_ORDER[d][i]) for i in range(T) for d in range(2)]
        lat_steps = [n for n, s in enumerate(ssd_steps) if s[2] < 2]
        s_h0, s_xs, s_st, s_hd, s_h, s_ld, s_lx, s_cb, s_mt, s_mu, s_yd, s_yo, s_yv, s_xd = (sem(f"ssd_{x}") for x in
            ("state_zero", "decayed_x", "state_product", "state_decayed", "state", "log_decay", "decay", "cb", "m", "y_diag_half", "y_diag", "y_off", "y_added", "xd"))
        with nc.Block() as block:
            @block.gpsimd
            def _(pool):
                pool.memset(H, 0.0).then_inc(s_h0, 1)
                pool.wait_ge(s_h0, 1)
                for n, (i, d, tile) in enumerate(ssd_steps):
                    if n < 6:
                        if n >= 2:
                            pool.wait_ge(s_st, n - 1)
                        pool.tensor_tensor(heads(XS[:, n % 2, :], 8), heads(XT1[:, tile, :], 8), spread(hcol(DTD, tile, d), 8, HD), ALU.mult).then_inc(s_xs, 1)
                        if n >= 2:
                            pool.wait_ge(s_h, n - 1)
                        if n >= 4:
                            pool.wait_ge(s_yo, n - 3)
                        pool.tensor_tensor(heads(H[:, d, :], 8), heads(H[:, d, :], 8), spread(hcol(EAL, tile, d), 8, HD), ALU.mult).then_inc(s_hd, 1)

            @block.tensor
            def _(pe):
                for n, (i, d, tile) in enumerate(ssd_steps):
                    tk = slice(tile * P, tile * P + P)
                    if n >= 4:
                        m = n - 4
                        if m >= 1:
                            pe.wait_ge(s_mt, 2 * m)
                        for g in range(2):
                            mm = pe.matmul(quad(4)[:, g, :], FS[:, 4 + g, tk], FS[:, 6 + g, tk], start=True, stop=True)
                        mm.then_inc(s_cb, 1)
                        for g in range(2):
                            q = 2 * m + g
                            if q >= 2:
                                pe.wait_ge(s_lx, q - 1)
                            pe.matmul(quad(q % 2), ident, neg[d].rearrange("p (a c) -> p a c", a=1).to_broadcast([P, 4, P]), start=True, stop=False, skip_group_check=True)
                            for h in range(4):
                                mm = pe.matmul(quad(q % 2)[:, h, :], hcol(DA, tile, d)[:, 4 * g + h:4 * g + h + 1].to_broadcast([P, P]), cum[d], start=False, stop=(h == 3), skip_group_check=True)
                            mm.then_inc(s_ld, 1)
                        pe.wait_ge(s_h, n - 1)
                        if m >= 1:
                            pe.wait_ge(s_yv, m)
                        for g in range(2):
                            mm = pe.matmul(bank[5][:, g * 256:g * 256 + 256], FS[:, 6 + g, tk], H[:, d, g * 256:g * 256 + 256], start=True, stop=True)
                        mm.then_inc(s_yo, 1)
                        pe.wait_ge(s_xd, m + 1)
                        for g in range(2):
                            pe.wait_ge(s_mt, 2 * m + g + 1)
                            for h in range(4):
                                hh = 4 * g + h
                                mm = pe.matmul(bank[6][:, hh * HD:hh * HD + HD], MT[:, g, h * P:h * P + P], XD[:, m % 2, hh * HD:hh * HD + HD], start=True, stop=True)
                            mm.then_inc(s_yd, 1)
                    if n < 6:
                        pe.wait_ge(s_xs, n + 1)
                        if n >= 2:
                            pe.wait_ge(s_h, n - 1)
                        for g in range(2):
                            mm = pe.matmul(bank[2 + n % 2][:, g * 256:g * 256 + 256], BT1[:, tile, g * P:g * P + P], XS[:, n % 2, g * 256:g * 256 + 256], start=True, stop=True)
                        mm.then_inc(s_st, 1)

            @block.scalar
            def _(act):
                for m in range(4):
                    i, d, tile = ssd_steps[4 + m]
                    for g in range(2):
                        q = 2 * m + g
                        act.wait_ge(s_ld, q + 1)
                        if q >= 2:
                            act.wait_ge(s_mt, q - 1)
                        for h in range(4):
                            ins = act.activation(LT[:, q % 2, h * P:h * P + P], quad(q % 2)[:, h, :], ACT.Exp, bias=hcol(NAC, tile, d)[:, 4 * g + h:4 * g + h + 1])
                        ins.then_inc(s_lx, 1)

            @block.vector
            def _(dve):
                link = linker(dve, "dve")
                for i in range(2):
                    dve.tensor_tensor(heads(Y[:, i, :], 8), heads(XT1[:, i, :], 8), spread(rowcol[:, 8:16], 8, HD), ALU.mult)
                for n, (i, d, tile) in enumerate(ssd_steps):
                    m = n - 4
                    if n >= 4:
                        if m >= 2:
                            dve.wait_ge(s_yd, 2 * (m - 1))
                        dve.tensor_tensor(heads(XD[:, m % 2, :], 8), heads(XT1[:, tile, :], 8), spread(hcol(DTC, tile, d), 8, HD), ALU.mult).then_inc(s_xd, 1)
                        dve.wait_ge(s_cb, m + 1)
                        for g in range(2):
                            q = 2 * m + g
                            dve.wait_ge(s_lx, q + 1)
                            if m >= 1:
                                dve.wait_ge(s_yd, 2 * (m - 1) + g + 1)
                            dve.tensor_tensor(heads(MT[:, g, :], 4), heads(LT[:, q % 2, :], 4),
                                              quad(4)[:, g:g + 1, :].to_broadcast([P, 4, P]), ALU.mult).then_inc(s_mt, 1)
                        dve.wait_ge(s_yo, m + 1)
                        link(dve.tensor_tensor(heads(yt, 8), heads(bank[5][:, :], 8), spread(hcol(EAC, tile, d), 8, HD), ALU.mult))
                        link(dve.tensor_tensor(Y[:, tile, :], Y[:, tile, :], yt, ALU.add))
                        dve.wait_ge(s_yd, 2 * m + 2)
                        dve.tensor_tensor(Y[:, tile, :], Y[:, tile, :], bank[6][:, :], ALU.add).then_inc(s_yv, 1)
                        dve.wait_ge(s_yv, m + 1)
                    if n < 6:
                        dve.wait_ge(s_st, n + 1)
                        dve.wait_ge(s_hd, n + 1)
                        dve.tensor_tensor(H[:, d, :], H[:, d, :], bank[2 + n % 2][:, :], ALU.add).then_inc(s_h, 1)

        ysq, zs1, yr = cut(21120, 4, 256), cut(22144, 2, 512), small[:, 96:100]
        s_zs1, s_ys, s_yr, s_yn, s_yt1 = (sem(f"sgn_{x}") for x in ("silu_z", "sums", "rms", "normed", "turned"))
        with nc.Block() as block:
            @block.scalar
            def _(act):
                act.activation(zs1, Z1, ACT.Silu).then_inc(s_zs1, 1)

            @block.vector
            def _(dve):
                link = linker(dve, "dve")
                dve.wait_ge(s_zs1, 1)
                link(dve.tensor_tensor(Y, Y, zs1, ALU.mult))
                y4 = Y.rearrange("p t (g n) -> p (t g) n", g=2)
                link(dve.tensor_tensor(ysq, y4, y4, ALU.mult))
                dve.tensor_reduce(yr, ysq, AX.X, ALU.add).then_inc(s_ys, 1)
                dve.wait_ge(s_yr, 1)
                dve.tensor_tensor(y4, y4, spread(yr, 4, 256), ALU.mult).then_inc(s_yn, 1)
                for c in range(4):
                    dve.wait_ge(s_yt1, c + 1)
                    dve.tensor_scalar(catT[:, 4 + c, 0:LAT], bank[c][:, 0:LAT], SSDNORM(c), None, ALU.mult)

            @block.gpsimd
            def _(pool):
                link = linker(pool, "pool")
                pool.wait_ge(s_ys, 1)
                link(pool.tensor_scalar(yr, yr, 1.0 / 256, EPS, ALU.mult, ALU.add))
                pool.tensor_tensor(yr, yr, mhalf[:, 0:4], ALU.pow).then_inc(s_yr, 1)

            @block.tensor
            def _(pe):
                pe.wait_ge(s_yn, 1)
                for c in range(4):
                    for i in range(2):
                        mm = pe.transpose(bank[c][:, i * P:i * P + P], Y[:, i, c * P:c * P + P], ident)
                    mm.then_inc(s_yt1, 1)

        wod = t["od_w_out"]
        wo1 = cut(8192, KD, D)
        att_rows = wod[0:512, :].rearrange("(two c p) n -> two p c n", two=2, p=HD)
        project_and_add("l1_out", [(wo1[0:64, 0:4, :], att_rows[0]), (wo1[64:128, 0:4, :], att_rows[1]),
                                   (wo1[:, 4:8, :], wod[512:1024, :].rearrange("(k p) n -> p k n", p=P))], 2, 2, 2, wo1)

        xn1 = cut(0, 2, D)
        norm_to_hT("l1_ffn", 1, 1, range(2), xn1)
        wr = cut(2048, KD, E)
        sm = small[:, 128:640]
        lg, top, gw = sm[:, 0:16], sm[:, 16:32], sm[:, 48:64]
        sel, pos, oh = sm[:, 64:80], sm[:, 80:96], sm[:, 96:128]
        ix = sb("expert_index", [P, 16], U32)
        ixf, ee, tot = sm[:, 128:144], sm[:, 144:160], sm[:, 160:176]
        most = sb("most_tokens", [1, 1], mybir.dt.int32)
        s_wr, s_lg, s_lv, s_e1, s_cp1, s_ps = (sem(f"route_{x}") for x in ("w", "logits", "picked", "exp", "selected", "positions"))
        with nc.Block() as block:
            @block.sync
            def _(sp):
                sp.dma_start(wr, t["moe_router"].rearrange("(k p) e -> p k e", p=P)).then_inc(s_wr, 16)

            @block.tensor
            def _(pe):
                pe.wait_ge(s_wr, 16)
                for i in range(2):
                    for k in range(KD):
                        mm = pe.matmul(bank[0][:, 8 * i:8 * i + 8], hT[:, k, i * P:i * P + P], wr[:, k, :], start=(k == 0), stop=(k == KD - 1))
                mm.then_inc(s_lg, 1)
                pe.wait_ge(s_cp1, 1)
                pe.matmul(bank[1][:, 0:8], cst("before"), sel[:, 0:8], start=True, stop=True)
                pe.matmul(bank[1][:, 8:16], cst("before"), sel[:, 8:16], start=True, stop=False)
                pe.matmul(bank[1][:, 8:16], ones, sel[:, 0:8], start=False, stop=True)
                pe.matmul(bank[1][:, 16:24], ones, sel[:, 0:8], start=True, stop=False)
                pe.matmul(bank[1][:, 16:24], ones, sel[:, 8:16], start=False, stop=True).then_inc(s_ps, 1)

            @block.scalar
            def _(act):
                act.wait_ge(s_lv, 1)
                act.activation(ee[:, 0:2], ee[:, 0:2], ACT.Exp).then_inc(s_e1, 1)

            @block.vector
            def _(dve):
                link = linker(dve, "dve")
                dve.wait_ge(s_lg, 1)
                link(dve.tensor_copy(lg, bank[0][:, 0:16]))
                for i in range(2):
                    a = slice(8 * i, 8 * i + 8)
                    link(dve.max(top[:, a], lg[:, a]))
                    link(dve.max_index(ix[:, a], top[:, a], lg[:, a]))
                link(dve.tensor_copy(ixf, ix[:, :]))
                for i in range(2):
                    ins = dve.tensor_tensor(ee[:, i:i + 1], top[:, 8 * i + 1:8 * i + 2], top[:, 8 * i:8 * i + 1], ALU.subtract)
                ins.then_inc(s_lv, 1)
                dve.wait_ge(s_e1, 1)
                link(dve.tensor_scalar(ee[:, 2:4], ee[:, 0:2], 1.0, None, ALU.add))
                link(dve.reciprocal(ee[:, 4:6], ee[:, 2:4]))
                link(dve.tensor_tensor(ee[:, 6:8], ee[:, 4:6], ee[:, 0:2], ALU.mult))
                for i in range(2):
                    a = slice(8 * i, 8 * i + 8)
                    io = cst("iota")[:, 0:8]
                    link(dve.tensor_scalar(oh[:, 0:8], io, ixf[:, 8 * i:8 * i + 1], None, ALU.is_equal))
                    link(dve.tensor_scalar(oh[:, 8:16], io, ixf[:, 8 * i + 1:8 * i + 2], None, ALU.is_equal))
                    link(dve.tensor_tensor(sel[:, a], oh[:, 0:8], oh[:, 8:16], ALU.add))
                    link(dve.tensor_scalar(oh[:, 16:24], oh[:, 8:16], ee[:, 6 + i:7 + i], None, ALU.mult))
                    link(dve.scalar_tensor_tensor(gw[:, a], oh[:, 0:8], ee[:, 4 + i:5 + i], oh[:, 16:24], ALU.mult, ALU.add))
                dve.sem_inc(s_cp1, 1)
                dve.wait_ge(s_ps, 1)
                dve.tensor_copy(pos, bank[1][:, 0:16])
                link(dve.tensor_reduce(tot[:, 0:1], bank[1][:, 16:24], AX.X, ALU.max))
                dve.tensor_copy(most[:, :], tot[0:1, 0:1])

        NB = FE // 512
        PB, PM = 2 * NB, 26
        W1S, W3S, W2S = ([cut(4096 + (3 * s + m) * 4096, *((KD, 512), (KD, 512), (4, D))[m]) for s in range(2)] for m in range(3))
        xg = [cut(2048 + q * 1024, KD, P) for q in range(2)]
        disp = X[:, 2:4, :].rearrange("p a (e i s) -> p (a e) i s", i=2, s=P)
        back = catT[:, 0:4, :].rearrange("p a (e n) -> p (a e) n", n=LAT)
        backs = catT[:, 4, :].rearrange("p (q n) -> p q n", q=2)
        weighted = hT[:, 0:4, :].rearrange("p a (e i s) -> p (a e) i s", i=2, s=P)
        silu_h, prod, prodT = hT[:, 0:2, :], hT[:, 2:4, :], hT[:, 4:6, :]
        ysb = hT[:, 6:8, :].rearrange("p a b -> p (a b)")
        ACC = G[:, 0:2, :]
        w1e = t["moe_w1"].rearrange("e (k p) f -> p e k f", p=P)
        w3e = t["moe_w3"].rearrange("e (k p) f -> p e k f", p=P)
        w2e = t["moe_w2"].rearrange("e (c j p) n -> p e c j n", p=P, j=4)

        def at_expert(v, e):
            return v[:, bass.ds(e, 1)]

        def experts(r):
            tag = f"moe{r}"
            chain[tag] = [sem(f"{tag}_chain"), 0]
            s_dp, s_dt, s_dc = sem(f"{tag}_dispatch"), sem(f"{tag}_turned"), sem(f"{tag}_turned_copied")
            s_w1 = [sem(f"{tag}_w1_{i}") for i in range(2)]
            s_w3 = [sem(f"{tag}_w3_{i}") for i in range(2)]
            s_w2 = [sem(f"{tag}_w2_{i}") for i in range(2)]
            s_h1, s_h3, s_sl, s_pr, s_ms, s_mf, s_dn, s_y, s_yc, s_sc, s_bk = (sem(f"{tag}_{x}") for x in
                ("h1", "h3", "silu", "gated", "misc", "misc_free", "down", "y", "y_copied", "scattered", "back_copied"))

            def load(sp, m, e, c, slot):
                pick = (lambda v: v[:, e]) if isinstance(e, int) else (lambda v: at_expert(v, e))
                if m < 2:
                    src = pick((w1e, w3e)[m])
                    src = src[:, :, c * 512:c * 512 + 512] if isinstance(e, int) else src[:, :, :, c * 512:c * 512 + 512].rearrange("p a k f -> p (a k) f")
                else:
                    src = pick(w2e)
                    src = src[:, c] if isinstance(e, int) else src[:, :, c].rearrange("p a j n -> p (a j) n")
                sp.dma_start((W1S, W3S, W2S)[m][slot], src).then_inc((s_w1, s_w3, s_w2)[m][slot], 16)

            with nc.Block() as block:
                @block.sync
                def _(sp):
                    for n in range(2):
                        for m in range(3):
                            load(sp, m, 0, n, n)

                @block.vector
                def _(dve):
                    link = linker(dve, tag)
                    dve.sem_inc(s_pr, 2)
                    dve.sem_inc(s_mf, 2)
                    if r == 0:
                        dve.memset(ACC, 0.0)
                    else:
                        link(dve.tensor_scalar(pos, pos, float(P), None, ALU.subtract))
                    for e in range(E):
                        for i in range(2):
                            a = slice(8 * i + e, 8 * i + e + 1)
                            link(dve.tensor_scalar(disp[:, e, i, :], cst("iota"), pos[:, a], sel[:, a], ALU.is_equal, ALU.mult))
                            dve.tensor_scalar(weighted[:, e, i, :], disp[:, e, i, :], gw[:, a], None, ALU.mult).then_inc(s_dp, 1)
                    for b in range(4):
                        dve.wait_ge(s_dt, b + 1)
                        dve.tensor_copy(back[:, 2 * b:2 * b + 2, :], bank[b][:, :].rearrange("p (e n) -> p e n", e=2)).then_inc(s_dc, 1)

                @block.tensor
                def _(pe):
                    pe.sem_inc(s_dn, 2)
                    for b in range(4):
                        pe.wait_ge(s_dp, 4 * b + 4)
                        for x in range(4):
                            mm = pe.transpose(quad(b)[:, x, :], weighted[:, 2 * b + x // 2, x % 2, :], ident)
                        mm.then_inc(s_dt, 1)

                @block.scalar
                def _(act):
                    act.sem_inc(s_sl, 2)

                @block.gpsimd
                def _(pool):
                    pool.sem_inc(s_sc, 1)

            with nc.Block() as block:
                @block.sync
                def _(sp):
                    def chunks(p, last):
                        for n in range(2, PB if last else PB + 2):
                            e, c = n // NB, n % NB
                            for m, used in enumerate((s_h1, s_h3, s_dn)):
                                sp.wait_ge(used, PB * p + (n - 1 + (2 if m == 2 else 0)))
                                load(sp, m, 2 * p + e, c, n % 2)
                    with sp.Fori(0, E // 2 - 1) as p:
                        chunks(p, False)
                    chunks(E // 2 - 1, True)

                @block.tensor
                def _(pe):
                    with pe.Fori(0, E // 2) as p:
                        m = 0
                        for q in range(2):
                            def misc():
                                pe.wait_ge(s_mf, PM * p + (m + 1))
                                return 4 + m % 2

                            def turn(n):
                                b = misc()
                                pe.wait_ge(s_pr, PB * p + (n + 3))
                                for j in range(4):
                                    mm = pe.transpose(quad(b)[:, j, :], prod[:, n % 2, j * P:j * P + P], ident)
                                mm.then_inc(s_ms, 1)

                            def down(n, m_turn, first, last):
                                pe.wait_ge(s_w2[n % 2], 16 * NB * p + 16 * (n // 2 + 1))
                                pe.wait_ge(s_mf, PM * p + (m_turn + 3))
                                for j in range(4):
                                    for half in range(2):
                                        mm = pe.matmul(bank[6 + half][:, :], prodT[:, n % 2, j * P:j * P + P], W2S[n % 2][:, j, half * 512:half * 512 + 512],
                                                       start=(first and j == 0), stop=(last and j == 3))
                                mm.then_inc(s_dn, 1)

                            for g in range(2):
                                b = misc()
                                for k in range(4):
                                    for i in range(2):
                                        sl_ = at_expert(disp, 2 * p + q)[:, :, i, :].rearrange("p a s -> p (a s)")
                                        mm = pe.matmul(quad(b)[:, k, :], xn1[:, i, (4 * g + k) * P:(4 * g + k + 1) * P], sl_, start=(i == 0), stop=(i == 1))
                                mm.then_inc(s_ms, 1)
                                m += 1
                            pe.wait_ge(s_mf, PM * p + (m + 2))
                            m_turn = None
                            for c in range(NB):
                                n = NB * q + c
                                pe.wait_ge(s_w1[n % 2], 16 * NB * p + 16 * (n // 2 + 1))
                                pe.wait_ge(s_sl, PB * p + (n + 1))
                                for k in range(KD):
                                    mm = pe.matmul(bank[n % 2][:, :], xg[q][:, k, :], W1S[n % 2][:, k, :], start=(k == 0), stop=(k == KD - 1))
                                mm.then_inc(s_h1, 1)
                                if c:
                                    turn(n - 1)
                                    m_turn = m
                                    m += 1
                                pe.wait_ge(s_w3[n % 2], 16 * NB * p + 16 * (n // 2 + 1))
                                pe.wait_ge(s_pr, PB * p + (n + 1))
                                for k in range(KD):
                                    mm = pe.matmul(bank[2 + n % 2][:, :], xg[q][:, k, :], W3S[n % 2][:, k, :], start=(k == 0), stop=(k == KD - 1))
                                mm.then_inc(s_h3, 1)
                                if c:
                                    down(n - 1, m_turn, c == 1, False)
                            turn(n)
                            m_turn = m
                            m += 1
                            down(n, m_turn, False, True)
                            pe.wait_ge(s_dn, PB * p + (n + 3))
                            pe.sem_inc(s_y, 1)
                            pe.wait_ge(s_yc, 2 * p + (q + 1))
                            pe.wait_ge(s_bk, 2 * p + (q + 1))
                            for i in range(2):
                                for half in range(2):
                                    b = misc()
                                    mm = pe.matmul(bank[b][:, :], backs[:, q, i * P:i * P + P], ysb[:, half * 512:half * 512 + 512], start=True, stop=True)
                                    mm.then_inc(s_ms, 1)
                                    m += 1
                            pe.sem_inc(s_sc, 1)
                        assert m == PM

                @block.scalar
                def _(act):
                    with act.Fori(0, E // 2) as p:
                        for q in range(2):
                            for c in range(NB):
                                n = NB * q + c
                                act.wait_ge(s_h1, PB * p + (n + 1))
                                act.wait_ge(s_pr, PB * p + (n + 1))
                                act.activation(silu_h[:, n % 2, :], bank[n % 2][:, :], ACT.Silu).then_inc(s_sl, 1)
                            act.wait_ge(s_y, 2 * p + (q + 1))
                            act.wait_ge(s_sc, 2 * p + (q + 1))
                            for half in range(2):
                                ins = act.activation(ysb[:, half * 512:half * 512 + 512], bank[6 + half][:, :], ACT.Copy)
                            ins.then_inc(s_yc, 1)

                @block.gpsimd
                def _(pool):
                    with pool.Fori(0, E // 2) as p:
                        for q in range(2):
                            pool.wait_ge(s_sc, 2 * p + (q + 1))
                            src = at_expert(back, 2 * p + q).rearrange("p a n -> p (a n)")
                            pool.tensor_copy(backs[:, q, :], src).then_inc(s_bk, 1)

                @block.vector
                def _(dve):
                    shift, scale = modc[:, 1, 2, :, 0], modc[:, 1, 3, :, 0]
                    with dve.Fori(0, E // 2) as p:
                        m = 0
                        for q in range(2):
                            for g in range(2):
                                dve.wait_ge(s_ms, PM * p + (m + 1))
                                for k in range(4):
                                    kk = 4 * g + k
                                    ins = dve.tensor_scalar(xg[q][:, kk, :], quad(4 + m % 2)[:, k, :], scale[:, kk:kk + 1], shift[:, kk:kk + 1], ALU.mult, ALU.add)
                                ins.then_inc(s_mf, 1)
                                m += 1
                            for c in range(NB):
                                n = NB * q + c
                                dve.wait_ge(s_sl, PB * p + (n + 3))
                                dve.wait_ge(s_h3, PB * p + (n + 1))
                                dve.tensor_tensor(prod[:, n % 2, :], silu_h[:, n % 2, :], bank[2 + n % 2][:, :], ALU.mult).then_inc(s_pr, 1)
                                dve.wait_ge(s_ms, PM * p + (m + 1))
                                dve.wait_ge(s_dn, PB * p + (n + 1))
                                dve.tensor_copy(prodT[:, n % 2, :], bank[4 + m % 2][:, :]).then_inc(s_mf, 1)
                                m += 1
                            for i in range(2):
                                for half in range(2):
                                    dve.wait_ge(s_ms, PM * p + (m + 1))
                                    h = slice(half * 512, half * 512 + 512)
                                    dve.tensor_tensor(ACC[:, i, h], ACC[:, i, h], bank[4 + m % 2][:, :], ALU.add).then_inc(s_mf, 1)
                                    m += 1
                            dve.wait_ge(s_mf, PM * p + (m + 2))

        experts(0)
        full = nc.values_load(most[0:1, 0:1], engines=mybir.ALL_ENGINES, min_val=0, max_val=LAT)
        with nc.If(full > P):
            experts(1)

        s_fs, s_fr, s_fx, s_out = (sem(f"end_{x}") for x in ("squares", "rms", "residual", "stored"))
        fs, tmp = small[:, 0:2], xn1
        with nc.Block() as block:
            @block.scalar
            def _(act):
                for i in range(2):
                    act.activation(cut(4096, 2, D)[:, i, :], ACC[:, i, :], ACT.Square, accum_out=fs[:, i:i + 1]).then_inc(s_fs, 1)

            @block.gpsimd
            def _(pool):
                link = linker(pool, "pool")
                pool.wait_ge(s_fs, 2)
                link(pool.tensor_scalar(fs, fs, 1.0 / D, EPS, ALU.mult, ALU.add))
                pool.tensor_tensor(fs, fs, mhalf[:, 0:2], ALU.pow).then_inc(s_fr, 1)

            @block.vector
            def _(dve):
                link = linker(dve, "dve")
                dve.wait_ge(s_fr, 1)
                for i in range(2):
                    link(dve.scalar_tensor_tensor(tmp[:, i, :], ACC[:, i, :], fs[:, i:i + 1], G[:, 3, :], ALU.mult, ALU.mult))
                    dve.tensor_tensor(X[:, i, :], X[:, i, :], tmp[:, i, :], ALU.add).then_inc(s_fx, 1)

            @block.sync
            def _(sp):
                for i in range(2):
                    sp.wait_ge(s_fx, i + 1)
                    sp.dma_start(out.rearrange("(t p) d -> p t d", p=P)[:, i, :], X[:, i, :]).then_inc(s_out, 16)
                sp.wait_ge(s_out, 32)


def shape_constants():
    import numpy as np
    c = {n: np.zeros((P, w), np.float32) for n, (_, w) in CONST.items()}
    r = np.arange(P)
    c["ident"][r, r] = 1
    c["cum0"][:] = r[:, None] <= r[None, :]
    c["cum1"][:] = r[:, None] >= r[None, :]
    c["ones"][:] = 1
    c["neg0"][:] = np.where(r[None, :] >= r[:, None], 0, -30000)
    c["neg1"][:] = np.where(r[None, :] <= r[:, None], 0, -30000)
    k = np.arange(LAT)
    for i in range(2):
        c["band"][:, i * LAT:(i + 1) * LAT] = np.where(np.abs(k[None, :] - (r[:, None] + P * i)) <= 128, 0, -1e30)
    q = r % 64
    start = np.clip(q - 8, 0, 48)[:, None]
    k = np.arange(64)[None, :]
    c["natcol"][:] = np.where((k >= start) & (k < start + 16), 0, -1e30)
    half = 16
    freqs = (10000.0 ** (-np.arange(half, dtype=np.float32) / np.float32(half))).astype(np.float32)
    pos = np.arange(LAT)
    for p in range(P):
        dd = p % 64
        at = (pos // 64 if dd < 32 else pos % 64).astype(np.float32)
        ang = (at * freqs[dd % 16]).astype(np.float32)
        c["cos"][p], c["sin"][p] = np.cos(ang), np.sin(ang)
        if dd % 32 < 16:
            c["rot"][p + 16, p] = -1
        else:
            c["rot"][p - 16, p] = 1
    c["iota"][:] = r[None, :]
    c["before"][:] = r[:, None] < r[None, :]
    c["pick"][0, 0:P] = 1
    c["pick"][1, P:2 * P] = 1
    levels = np.zeros((P, 2, LEVELS, P), np.float32)
    for l in range(LEVELS):
        b = 1 << l
        same = r[:, None] // (2 * b) == r[None, :] // (2 * b)
        levels[:, 0, l, :] = same & (r[:, None] // b < r[None, :] // b)
        levels[:, 1, l, :] = same & (r[:, None] // b > r[None, :] // b)
    return np.concatenate([c[n] for n in CONST], axis=1), levels


def nat_bias_places():
    import numpy as np
    q = np.arange(LAT)
    dr = np.arange(4)[None, :, None] - (q // 64)[:, None, None] + 7
    dc = np.clip(np.arange(64)[None, None, :] - (q % 64)[:, None, None] + 15, 0, 30)
    return (dr * 31 + dc).reshape(LAT, LAT)


def kernel(**inputs):
    import numpy as np
    import concourse.bacc as bacc
    from concourse.bass_utils import run_bass_kernel_spmd as run

    a = {k: np.ascontiguousarray(v) for k, v in inputs.items()}
    const, levels = shape_constants()
    rpb = a["na_rpb"][0].reshape(8, 15 * 31)[:, nat_bias_places()]
    arrays = {
        "x": a["x"][0], "ctx": a["ctx"][0], "c": a["c"], "c_ctx": a["c_ctx"][None, :],
        "ada_w": a["ada_w"], "ada_b": a["ada_b"], "norm_w": a["norm_w"],
        "ev_w_in": a["ev_w_in"][0], "ev_w_out": a["ev_w_out"][0],
        "nat_bias": rpb.reshape(8, 2, P, LAT).transpose(2, 1, 0, 3),
        "dn_conv": a["dn_conv"][0], "dn_a_log": a["dn_a_log"].reshape(8, 1), "dn_dt_bias": a["dn_dt_bias"].reshape(8, 1), "dn_norm": a["dn_norm"],
        "ffn_w1": a["ffn_w1"][0], "ffn_w3": a["ffn_w3"][0], "ffn_w2": a["ffn_w2"][0],
        "od_w_in": a["od_w_in"][0], "od_w_out": a["od_w_out"][0], "wa_sink": a["wa_sink"],
        "ssd_conv": a["ssd_conv"][0], "ssd_a_log": a["ssd_a_log"].reshape(16, 1), "ssd_dt_bias": a["ssd_dt_bias"].reshape(16, 1),
        "ssd_d": a["ssd_d"], "ssd_norm": a["ssd_norm"],
        "moe_router": a["moe_router"][0], "moe_w1": a["moe_w1"][0], "moe_w3": a["moe_w3"][0], "moe_w2": a["moe_w2"][0],
        "const": const, "levels": levels,
    }
    arrays = {f"in_{k}": np.ascontiguousarray(v) for k, v in arrays.items()}
    nc = bacc.Bacc("TRN2", target_bir_lowering=False, num_devices=1)
    t = {k[3:]: nc.dram_tensor(k, v.shape, mybir.dt.from_np(v.dtype), kind="ExternalInput").ap() for k, v in arrays.items()}
    out = nc.dram_tensor("out", (LAT, D), F32, kind="ExternalOutput").ap()
    build(nc, t, out)
    got = run(nc, [arrays], core_ids=[0])
    return got.results[0]["out"].reshape(1, LAT, D)
```

```python
from contextlib import ExitStack

import concourse.bass as bass
from concourse import mybir

F32 = mybir.dt.float32
F32R = mybir.dt.float32r
U32 = mybir.dt.uint32
ALU = mybir.AluOpType
ACT = mybir.ActivationFunctionType
AX = mybir.AxisListType

P = 128
D = 1024
KD = D // P
LAT, CTX = 256, 256
T = 4
NTOK = LAT + CTX
HALF = 512
HD = 64
EV_IN, OD_IN = 3600, 2320
FF = 2816
NF = FF // P
E, FE = 8, 3584
EPS = 1e-6
TAPS = 5
LEVELS = 7
CHUNK_ORDER = ((2, 3, 0, 1), (3, 2, 1, 0))

CONST = {}
_at = 0
for _n, _w in (("ident", P), ("cum0", P), ("cum1", P), ("ones", P), ("neg0", P), ("neg1", P), ("band", 2 * LAT),
               ("natcol", 64), ("cos", LAT), ("sin", LAT), ("rot", P), ("iota", P), ("before", P), ("pick", 2 * P)):
    CONST[_n] = (_at, _w)
    _at += _w
NCONST = _at


def build(nc, t, out):
    with ExitStack() as ctx:
        def sb(name, shape, dt=F32):
            return ctx.enter_context(nc.sbuf_tensor(name, shape, dt))

        twins = {}

        def sb_split(name, width, shape=None, parts=None):
            at = (nc.sbuf_base + 31) // 32 * 32
            v = sb(name, shape or [P, width])
            ends = parts or [width]
            twins[v.name] = (width, [(a, b, nc.alloc_sbuf_tensor_at(f"{name}_r{a}", [P, b - a], F32R, offset=at + 4 * a))
                                     for a, b in zip([0] + ends, ends)])
            return v

        def rounded(v):
            width, parts = twins[v.tensor.name]
            for a, b, twin in parts:
                if a <= v.offset < b:
                    return bass.AP(tensor=twin, offset=v.offset - a, ap=[[b - a, v.ap[0][1]]] + [list(x) for x in v.ap][1:])

        stage_sems = []

        def sem(name):
            s = nc.alloc_semaphore(name=name)
            stage_sems.append(s)
            return s

        bank = [ctx.enter_context(nc.psum_tensor(f"bank{i}", [P, 512], F32)) for i in range(8)]

        def quad(i):
            return bank[i][:, :].rearrange("p (a b) -> p a b", a=4)

        X = sb("residual", [P, T, D])
        C = sb("const", [P, NCONST])
        G = sb_split("gate_rows", 6 * D, [P, 6, D])
        cols = sb("channel_cols", [P, 2, P])
        modc = sb("mod_cols", [P, 2, 4, KD, 2])
        hT = sb_split("hT", KD * NTOK, [P, KD, NTOK])
        catT = sb_split("catT", KD * NTOK, [P, KD, NTOK])
        ar = sb_split("arena", 28768, parts=[8192, 16384, 28768])
        small = sb_split("small", 640)
        mhalf = sb("minus_half", [P, 64])
        gbias = sb("gate_bias", [16, 8])
        rowcol = sb("per_head_rows", [P, 16])

        def cst(name):
            a, w = CONST[name]
            return C[:, a:a + w]

        ident, ones = cst("ident"), cst("ones")
        cum, neg = (cst("cum0"), cst("cum1")), (cst("neg0"), cst("neg1"))

        def cut(at, *shape):
            n = 1
            for s in shape:
                n *= s
            v = ar[:, at:at + n]
            if len(shape) == 1:
                return v
            names = "abcd"[:len(shape)]
            return v.rearrange(f"p ({' '.join(names)}) -> p {' '.join(names)}", **dict(zip(names, shape)))

        chain = {k: [ctx.enter_context(nc.semaphore(f"{k}_chain")), 0] for k in ("act", "dve", "pool")}

        def linker(eng, key):
            def link(ins):
                chain[key][1] += 1
                ins.then_inc(chain[key][0], 1)
                eng.wait_ge(chain[key][0], chain[key][1])
            return link

        def high(act, hi, v):
            return act.activation(rounded(hi), v, ACT.Copy)

        def low(dve, v, hi):
            return dve.tensor_tensor(rounded(v), v, rounded(hi).bitcast(F32), ALU.subtract)

        def split_matmul(pe, acc, x, w, start, stop):
            xh_, xl_, wh_, wl_ = (rounded(v) for v in (*x, *w))
            pe.matmul(acc, xh_, wh_, start=start, stop=False)
            pe.matmul(acc, xh_, wl_, start=False, stop=False)
            return pe.matmul(acc, xl_, wh_, start=False, stop=stop)

        NORMW = lambda l, i, k: cols[:, 0, (l * 4 + i) * 8 + k:(l * 4 + i) * 8 + k + 1]
        DNCONV = lambda tap, c: cols[:, 0, 64 + tap * 12 + c:65 + tap * 12 + c]
        DNNORM = cols[:, 0, 124:125]
        SSDCONV = lambda tap, c: cols[:, 1, tap * 8 + c:tap * 8 + c + 1]
        SSDNORM = lambda c: cols[:, 1, 40 + c:41 + c]

        NSLOT, NCH = 4, 24
        aw = [cut(i * 4096, KD, 512) for i in range(NSLOT)]
        row0 = NSLOT * 4096
        ROW = ar[0:2, row0:row0 + 2 * 6 * D].rearrange("p (l n) -> p l n", l=2)
        rows = hT[:, 0:2, 0:P]
        abias = [catT[0:2, i, 0:512] for i in range(NSLOT)]
        nwr = catT[0:2, 4:8, :].rearrange("p a b -> p (a b)")
        nwr2 = hT[0:2, 4:8, :].rearrange("p a b -> p (a b)")
        scT = small[:, 0:16].rearrange("p (v k) -> p k v", v=2)
        s_x, s_const, s_rows, s_nw = sem("x_in"), sem("const_in"), sem("rows_in"), sem("norm_rows_in")
        s_slot = [sem(f"ada_w{i}") for i in range(NSLOT)]
        s_tr, s_trc = sem("rows_transposed"), sem("cols_copied")
        s_sc, s_ada, s_row = sem("silu_c"), sem("ada_product"), sem("ada_row")
        s_mp, s_mc, s_gp, s_gc, s_mh = sem("mod_transposed"), sem("mod_copied"), sem("gate_spread"), sem("gate_copied"), sem("minus_half_set")
        s_mg = sem("gate_times_norm")

        with nc.Block() as block:
            @block.sync
            def _(sp):
                sp.dma_start(C[:, :], t["const"]).then_inc(s_const, 16)
                sp.dma_start(rows[0:64, 0, :], t["norm_w"].rearrange("l i (k p) -> (l i k) p", p=P)).then_inc(s_rows, 16)
                sp.dma_start(rows[64:124, 0, :], t["dn_conv"].rearrange("t (c p) -> (t c) p", p=P)).then_inc(s_rows, 16)
                sp.dma_start(rows[124:125, 0, :], t["dn_norm"]).then_inc(s_rows, 16)
                sp.dma_start(rows[0:40, 1, :], t["ssd_conv"].rearrange("t (c p) -> (t c) p", p=P)).then_inc(s_rows, 16)
                sp.dma_start(rows[40:44, 1, :], t["ssd_norm"].rearrange("a (c p) -> (a c) p", p=P)).then_inc(s_rows, 16)
                sp.dma_start(rows[44:52, 1, :], t["c"].rearrange("a (k p) -> (a k) p", p=P)).then_inc(s_rows, 16)
                sp.dma_start(rows[52:60, 1, :], t["c_ctx"].rearrange("a (k p) -> (a k) p", p=P)).then_inc(s_rows, 16)
                adaw = [t["ada_w"][l].rearrange("(k p) n -> p k n", p=P) for l in range(2)]
                adab = [t["ada_b"][l:l + 1, :] for l in range(2)]

                def load(l, n, s):
                    w = slice(n * 512, n * 512 + 512) if isinstance(n, int) else bass.ds(n * 512, 512)
                    sp.dma_start(aw[s], adaw[l][:, :, w]).then_inc(s_slot[s], 16)
                    sp.dma_start(abias[s], adab[l][:, w].to_broadcast([2, 512])).then_inc(s_slot[s], 16)
                for s in range(NSLOT):
                    load(0, s, s)
                sp.dma_start(X[:, 0:2, :], t["x"].rearrange("(t p) d -> p t d", p=P)).then_inc(s_x, 16)
                sp.dma_start(X[:, 2:4, :], t["ctx"].rearrange("(t p) d -> p t d", p=P)).then_inc(s_x, 16)
                for l, dst in ((0, nwr), (1, nwr2)):
                    for j, i in enumerate((1, 3)):
                        sp.dma_start(dst[:, j * D:(j + 1) * D], t["norm_w"][l, i:i + 1, :].to_broadcast([2, D])).then_inc(s_nw, 16)
                sp.dma_start(gbias[0:8, 0:1], t["dn_dt_bias"]).then_inc(s_nw, 16)
                sp.dma_start(gbias[0:8, 1:2], t["dn_a_log"]).then_inc(s_nw, 16)
                sp.dma_start(gbias[:, 2:3], t["ssd_dt_bias"]).then_inc(s_nw, 16)
                sp.dma_start(gbias[:, 3:4], t["ssd_a_log"]).then_inc(s_nw, 16)
                sp.dma_start(rowcol[:, 0:8], t["wa_sink"].to_broadcast([P, 8])).then_inc(s_nw, 16)
                sp.dma_start(rowcol[:, 8:16], t["ssd_d"].to_broadcast([P, 8])).then_inc(s_nw, 16)
                for l in range(2):
                    with sp.Fori(max(1, 3 * l), 3 * l + 3) as i:
                        for s in range(NSLOT):
                            sp.wait_ge(s_row, NSLOT * i + (s + 1 - NSLOT))
                            load(l, NSLOT * i + (s - 12 * l), s)
                sp.wait_ge(s_x, 32)

            @block.tensor
            def _(pe):
                pe.wait_ge(s_const, 16)
                pe.wait_ge(s_rows, 112)
                pe.transpose(bank[4][:, 0:125], rows[0:125, 0, :], ident[0:125, 0:125]).then_inc(s_tr, 1)
                pe.transpose(bank[5][:, 0:60], rows[0:60, 1, :], ident[0:60, 0:60]).then_inc(s_tr, 1)
                pe.wait_ge(s_sc, 1)

                def chunk(i, first):
                    for s in range(NSLOT):
                        if not first:
                            pe.wait_ge(s_row, NSLOT * i + (s + 1 - NSLOT))
                        pe.wait_ge(s_slot[s], 32 * i + 32)
                        for k in range(KD):
                            mm = pe.matmul(bank[s][0:2, :], scT[:, k, :], aw[s][:, k, :], start=(k == 0), stop=(k == KD - 1))
                        mm.then_inc(s_ada, 1)
                chunk(0, True)
                with pe.Fori(1, NCH // NSLOT) as i:
                    chunk(i, False)
                pe.wait_ge(s_row, NCH)
                n = 0
                for l in range(2):
                    for j, part in enumerate((0, 1, 3, 4)):
                        for k in range(KD):
                            n += 1
                            a = part * D + k * P
                            mm = pe.transpose(bank[4 + l][:, (j * 8 + k) * 2:(j * 8 + k) * 2 + 2], ROW[:, l, a:a + P], ident[0:2, 0:2])
                    mm.then_inc(s_mp, 1)
                pe.wait_ge(s_mg, 4)
                for n, (l, j, v) in enumerate(((0, 0, 0), (0, 1, 0), (1, 0, 0), (1, 1, 0), (0, 0, 1), (0, 1, 1))):
                    if n >= 2:
                        pe.wait_ge(s_gc, n - 1)
                    for half in range(2):
                        part = 2 if j == 0 else 5
                        mm = pe.matmul(bank[2 * (n % 2) + half][:, :], cst("pick")[0:2, v * P:v * P + P],
                                       ROW[:, l, part * D + half * 512:part * D + half * 512 + 512], start=True, stop=True)
                    mm.then_inc(s_gp, 1)

            @block.vector
            def _(dve):
                link = linker(dve, "dve")
                dve.memset(mhalf[:, :], -0.5).then_inc(s_mh, 1)
                dve.wait_ge(s_tr, 2)
                dve.tensor_copy(cols[:, 0, 0:125], bank[4][:, 0:125]).then_inc(s_trc, 1)
                dve.tensor_copy(cols[:, 1, 0:60], bank[5][:, 0:60]).then_inc(s_trc, 1)

                def chunk(i):
                    for s in range(NSLOT):
                        dve.wait_ge(s_ada, NSLOT * i + s + 1)
                        n = NSLOT * i + s
                        flat = ROW.rearrange("p l (n w) -> p (l n) w", w=512)
                        dst = flat[:, n, :] if isinstance(n, int) else flat[:, bass.ds(n, 1), :].rearrange("p a w -> p (a w)")
                        dve.tensor_tensor(dst, bank[s][0:2, :], abias[s], ALU.add).then_inc(s_row, 1)
                chunk(0)
                with dve.Fori(1, NCH // NSLOT) as i:
                    chunk(i)
                dve.wait_ge(s_row, NCH)
                dve.wait_ge(s_nw, 160)
                for l, w in ((0, nwr), (1, nwr2)):
                    for j, part in enumerate((2, 5)):
                        m = ROW[:, l, part * D:(part + 1) * D]
                        dve.tensor_tensor(m, m, w[:, j * D:(j + 1) * D], ALU.mult).then_inc(s_mg, 1)
                dve.wait_ge(s_mp, 2)
                dve.wait_ge(s_trc, 2)
                for l in range(2):
                    m = bank[4 + l][:, 0:64].rearrange("p (j k v) -> p j k v", j=4, k=KD)
                    for j in range(4):
                        if j % 2 == 0:
                            dve.tensor_copy(modc[:, l, j, :, :], m[:, j, :, :])
                        else:
                            link(dve.tensor_scalar(modc[:, l, j, :, :], m[:, j, :, :], 1.0, None, ALU.add))
                            w = cols[:, 0, (l * 4 + j - 1) * 8:(l * 4 + j) * 8]
                            for v in range(2):
                                dve.tensor_tensor(modc[:, l, j, :, v], modc[:, l, j, :, v], w, ALU.mult)
                for n in range(1, 6, 2):
                    dve.wait_ge(s_gp, n + 1)
                    dve.wait_ge(s_gc, n)
                    for half in range(2):
                        cp = dve.tensor_copy(G[:, n, half * 512:half * 512 + 512], bank[2 * (n % 2) + half][:, :])
                    cp.then_inc(s_gc, 1)

            @block.scalar
            def _(act):
                act.wait_ge(s_trc, 2)
                act.activation(small[:, 0:16], cols[:, 1, 44:60], ACT.Silu).then_inc(s_sc, 1)
                for n in range(0, 6, 2):
                    act.wait_ge(s_gp, n + 1)
                    if n:
                        act.wait_ge(s_gc, n)
                    for half in range(2):
                        cp = act.activation(G[:, n, half * 512:half * 512 + 512], bank[2 * (n % 2) + half][:, :], ACT.Copy)
                    cp.then_inc(s_gc, 1)

        def norm_to_hT(tag, l, which, tiles, xn, split=True, ahead=None):
            n = len(tiles)
            s_sq, s_r, s_xn, s_tp = sem(f"{tag}_squares"), sem(f"{tag}_rms"), sem(f"{tag}_xn"), sem(f"{tag}_transposed")
            ss, r = small[:, 0:4], small[:, 4:8]
            junk = hT[:, :, :].rearrange("p (t a) b -> p t (a b)", t=4)
            shift, scale = modc[:, l, 2 * which, :, :], modc[:, l, 2 * which + 1, :, :]
            dst = catT if split else hT
            if split:
                s_va, s_vd, s_hh = sem(f"{tag}_modulated_act"), sem(f"{tag}_modulated_dve"), sem(f"{tag}_high")
            with nc.Block() as block:
                if ahead:
                    @block.sync
                    def _(sp):
                        ahead(sp)

                @block.scalar
                def _(act):
                    link = linker(act, "act")
                    for i in range(n):
                        ins = act.activation(junk[:, i, :], X[:, i, :], ACT.Square, accum_out=ss[:, i:i + 1])
                        if i == n - 1:
                            ins.then_inc(s_sq, 1)
                    act.wait_ge(s_sq, 1)
                    for k in range(0, KD, 2):
                        for v in range(n // 2):
                            act.wait_ge(s_tp, 8 * (n - 1) + k + 1)
                            ins = act.activation(dst[:, k, 256 * v:256 * v + 256], bank[k][:, 256 * v:256 * v + 256], ACT.Identity,
                                                 bias=shift[:, k, v:v + 1], scale=scale[:, k, v:v + 1])
                        if split:
                            ins.then_inc(s_va, 1)
                    for k in range(KD if split else 0):
                        act.wait_ge((s_va, s_vd)[k % 2], k // 2 + 1)
                        high(act, hT[:, k, :], catT[:, k, :]).then_inc(s_hh, 1)

                @block.gpsimd
                def _(pool):
                    link = linker(pool, "pool")
                    pool.wait_ge(s_sq, 1)
                    link(pool.tensor_scalar(r[:, 0:n], ss[:, 0:n], 1.0 / D, EPS, ALU.mult, ALU.add))
                    pool.tensor_tensor(r[:, 0:n], r[:, 0:n], mhalf[:, 0:n], ALU.pow).then_inc(s_r, 1)

                @block.vector
                def _(dve):
                    dve.wait_ge(s_r, 1)
                    for i in range(n):
                        dve.tensor_scalar(xn[:, i, :], X[:, i, :], r[:, i:i + 1], None, ALU.mult).then_inc(s_xn, 1)
                    for k in range(1, KD, 2):
                        for v in range(n // 2):
                            dve.wait_ge(s_tp, 8 * (n - 1) + k + 1)
                            ins = dve.tensor_scalar(dst[:, k, 256 * v:256 * v + 256], bank[k][:, 256 * v:256 * v + 256],
                                                    scale[:, k, v:v + 1], shift[:, k, v:v + 1], ALU.mult, ALU.add)
                        if split:
                            ins.then_inc(s_vd, 1)
                    for k in range(KD if split else 0):
                        dve.wait_ge(s_hh, k + 1)
                        low(dve, catT[:, k, :], hT[:, k, :])

                @block.tensor
                def _(pe):
                    for i in range(n):
                        pe.wait_ge(s_xn, i + 1)
                        for k in range(KD):
                            pe.transpose(bank[k][:, i * P:(i + 1) * P], xn[:, i, k * P:(k + 1) * P], ident).then_inc(s_tp, 1)

        def load_out_weights(sp, src, raw, s_w):
            for g in range(4):
                sp.dma_start(raw[:, 2 * g:2 * g + 2, :], src[:, 2 * g:2 * g + 2, :]).then_inc(s_w[g], 16)

        def project_and_add(tag, n, gate_lat, gate_ctx, s_w, raw, hi):
            s_y, s_ss, s_r, s_h, s_l = (sem(f"{tag}_{x}") for x in ("y", "squares", "rms", "high", "low"))
            ss, r = small[:, 0:8], small[:, 8:16]
            tok = slice(0, n * P)
            with nc.Block() as block:
                @block.tensor
                def _(pe):
                    for i in range(n):
                        for half in range(2):
                            o = slice(half * 512, half * 512 + 512)
                            for k in range(KD):
                                if i == 0 and half == 0:
                                    pe.wait_ge(s_l, k + 1)
                                x = slice(i * P, i * P + P)
                                mm = split_matmul(pe, bank[2 * i + half][:, :], (hT[:, k, x], catT[:, k, x]), (hi[:, k, o], raw[:, k, o]), k == 0, k == KD - 1)
                            mm.then_inc(s_y, 1)

                def split_high(act):
                    for k in range(KD):
                        act.wait_ge(s_w[k // 2], 16)
                        high(act, hT[:, k, tok], catT[:, k, tok])
                        high(act, hi[:, k, :], raw[:, k, :]).then_inc(s_h, 1)

                def split_low(dve):
                    for k in range(KD):
                        dve.wait_ge(s_h, k + 1)
                        low(dve, catT[:, k, tok], hT[:, k, tok])
                        low(dve, raw[:, k, :], hi[:, k, :]).then_inc(s_l, 1)
                add_normed(block, n, gate_lat, gate_ctx, s_y, s_ss, s_r, ss, r, cut(16480, 8, 512), cut(0, D), split_high, split_low)

        def add_normed(block, n, gate_lat, gate_ctx, s_y, s_ss, s_r, ss, r, junk, tmp, act_first=None, dve_first=None):

            @block.scalar
            def _(act):
                if act_first:
                    act_first(act)
                for i in range(n):
                    for half in range(2):
                        act.wait_ge(s_y, 2 * i + half + 1)
                        act.activation(junk[:, 2 * i + half, :], bank[2 * i + half][:, :], ACT.Square,
                                       accum_out=ss[:, 2 * i + half:2 * i + half + 1]).then_inc(s_ss, 1)

            @block.gpsimd
            def _(pool):
                link = linker(pool, "pool")
                for i in range(n):
                    pool.wait_ge(s_ss, 2 * i + 2)
                    link(pool.tensor_tensor(r[:, i:i + 1], ss[:, 2 * i:2 * i + 1], ss[:, 2 * i + 1:2 * i + 2], ALU.add))
                    link(pool.tensor_scalar(r[:, i:i + 1], r[:, i:i + 1], 1.0 / D, EPS, ALU.mult, ALU.add))
                    pool.tensor_tensor(r[:, i:i + 1], r[:, i:i + 1], mhalf[:, 0:1], ALU.pow).then_inc(s_r, 1)

            @block.vector
            def _(dve):
                link = linker(dve, "dve")
                if dve_first:
                    dve_first(dve)
                for i in range(n):
                    dve.wait_ge(s_r, i + 1)
                    gate = G[:, gate_lat if i < 2 else gate_ctx, :]
                    for half in range(2):
                        h = slice(half * 512, half * 512 + 512)
                        link(dve.scalar_tensor_tensor(tmp[:, h], bank[2 * i + half][:, :], r[:, i:i + 1], gate[:, h], ALU.mult, ALU.mult))
                    link(dve.tensor_tensor(X[:, i, :], X[:, i, :], tmp, ALU.add))

        def attention(tag, jobs, qT, kT_of, v_of, bias_of, sink_of, prob, probT, extra_sync=None, prep=None):
            s_s, s_m, s_e, s_n, s_t, s_tc, s_o, s_oc = (sem(f"{tag}_{x}") for x in
                ("scores", "max", "exp", "probs", "probs_turned", "turned_copied", "pv", "pv_copied"))
            s_b = sem(f"{tag}_bias")
            nm, rs, ri, sk = small[:, 32:35], small[:, 35:38], small[:, 38:41], small[:, 41:44]
            n_jobs = len(jobs)
            with nc.Block() as block:
                if prep:
                    prep(block, s_b)

                @block.tensor
                def _(pe):
                    def scores(j):
                        tile, c, part = jobs[j]
                        a = 64 * part
                        if j >= 3:
                            pe.wait_ge(s_e, j - 2)
                        lo = 0 if tile < 2 else 256
                        if tile < 2:
                            if prep:
                                pe.wait_ge(s_b, 4)
                            pe.matmul(bank[j % 3][:, :], qT[a:a + 64, c, tile * P:tile * P + P], kT_of(c)[a:a + 64, :], start=True, stop=False)
                            pe.matmul(bank[j % 3][:, 0:256], ident, bias_of(tile, c, part), start=False, stop=True).then_inc(s_s, 1)
                        else:
                            pe.matmul(bank[j % 3][:, 256:512], qT[a:a + 64, c, tile * P:tile * P + P], kT_of(c)[a:a + 64, 256:512],
                                      start=True, stop=True).then_inc(s_s, 1)

                    def turn(j):
                        tile = jobs[j][0]
                        pe.wait_ge(s_n, j + 1)
                        if j >= 2:
                            pe.wait_ge(s_tc, j - 1)
                        for b in range(0 if tile < 2 else 2, 4):
                            mm = pe.transpose(bank[3 + j % 2][:, b * P:b * P + P], prob[:, j % 3, b * P:b * P + P], ident)
                        mm.then_inc(s_t, 1)

                    def pv(j):
                        tile, c, part = jobs[j]
                        pe.wait_ge(s_tc, j + 1)
                        if j >= 4:
                            pe.wait_ge(s_oc, j // 2 - 1)
                        blocks = range(0 if tile < 2 else 2, 4)
                        for b in blocks:
                            mm = pe.matmul(bank[5 + (j // 2) % 2][64 * part:64 * part + 64, 0:P], v_of(b, c, part),
                                           probT[:, j % 2, b * P:b * P + P], start=(b == blocks[0]), stop=(b == 3), skip_group_check=True)
                        mm.then_inc(s_o, 1)
                    for j in range(n_jobs + 3):
                        if j < n_jobs:
                            scores(j)
                        if 2 <= j < n_jobs + 2:
                            turn(j - 2)
                        if j >= 3:
                            pv(j - 3)

                @block.vector
                def _(dve):
                    link = linker(dve, "dve")

                    def maximum(j):
                        lo = 0 if jobs[j][0] < 2 else 256
                        dve.wait_ge(s_s, j + 1)
                        if sink_of:
                            link(dve.tensor_reduce(nm[:, j % 3:j % 3 + 1], bank[j % 3][:, lo:512], AX.X, ALU.max))
                            dve.tensor_scalar(nm[:, j % 3:j % 3 + 1], nm[:, j % 3:j % 3 + 1], sink_of(*jobs[j][1:]), -1.0,
                                              ALU.max, ALU.mult).then_inc(s_m, 1)
                        else:
                            dve.tensor_reduce(nm[:, j % 3:j % 3 + 1], bank[j % 3][:, lo:512], AX.X, ALU.max, negate=True).then_inc(s_m, 1)

                    def normalise(j):
                        lo = 0 if jobs[j][0] < 2 else 256
                        m = j % 3
                        dve.wait_ge(s_e, j + 1)
                        if sink_of:
                            link(dve.tensor_tensor(rs[:, m:m + 1], rs[:, m:m + 1], sk[:, m:m + 1], ALU.add))
                        link(dve.reciprocal(ri[:, m:m + 1], rs[:, m:m + 1]))
                        dve.tensor_scalar(prob[:, m, lo:512], prob[:, m, lo:512], ri[:, m:m + 1], None, ALU.mult).then_inc(s_n, 1)

                    def copy_o(j):
                        tile, c, _ = jobs[2 * j]
                        dve.wait_ge(s_o, 2 * j + 2)
                        dve.tensor_copy(catT[:, c, tile * P:tile * P + P], bank[5 + j % 2][:, 0:P]).then_inc(s_oc, 1)
                    for j in range(n_jobs + 5):
                        if j < n_jobs:
                            maximum(j)
                        if 1 <= j <= n_jobs:
                            normalise(j - 1)
                        if j >= 5 and j % 2 == 1:
                            copy_o((j - 5) // 2)

                @block.scalar
                def _(act):
                    def expo(j):
                        m = j % 3
                        lo = 0 if jobs[j][0] < 2 else 256
                        act.wait_ge(s_m, j + 1)
                        if j >= 3:
                            act.wait_ge(s_t, j - 2)
                        if sink_of:
                            act.activation(sk[:, m:m + 1], sink_of(*jobs[j][1:]), ACT.Exp, bias=nm[:, m:m + 1])
                        act.activation(prob[:, m, lo:512], bank[m][:, lo:512], ACT.Exp, bias=nm[:, m:m + 1],
                                       accum_out=rs[:, m:m + 1]).then_inc(s_e, 1)

                    def copy_t(j):
                        lo = 0 if jobs[j][0] < 2 else 256
                        act.wait_ge(s_t, j + 1)
                        if j >= 2:
                            act.wait_ge(s_o, j - 1)
                        act.activation(probT[:, j % 2, lo:512], bank[3 + j % 2][:, lo:512], ACT.Copy).then_inc(s_tc, 1)
                    for j in range(n_jobs + 2):
                        if j < n_jobs:
                            expo(j)
                        if j >= 2:
                            copy_t(j - 2)

        nqT, nkT, V, zT = cut(0, 4, NTOK), cut(2048, 4, NTOK), cut(4096, T, 512), cut(6144, 4, NTOK)
        CX = cut(8192, 12, 2, 260)
        NWR, WCH = 3, 14
        WR = [cut(16384 + i * 4096, KD, 256) for i in range(NWR)]
        WRH = [cut(18432 + i * 4096, KD, 256) for i in range(NWR)]
        natb = cut(14432, 2, 8, 256)
        graw = catT[0:16, 4:8, :]
        wg = sb_split("gate_weights", KD * 16, [P, KD, 16])
        wgh = small[:, 256:384].rearrange("p (k n) -> p k n", k=KD)

        s_wi = [sem(f"in_w{i}") for i in range(NWR)]
        s_pj, s_pe_a, s_pe_v, s_wg, s_bias_in, s_ih, s_il = (sem(x) for x in
            ("in_product", "in_copied_act", "in_copied_dve", "gate_w", "nat_bias_in", "in_w_high", "in_w_low"))
        WIN = t["ev_w_in"].rearrange("(k p) n -> p k n", p=P)

        def load_in(sp, c):
            sp.dma_start(WR[c % NWR], WIN[:, :, c * 256:c * 256 + 256]).then_inc(s_wi[c % NWR], 16)

        def in_ahead(sp):
            for c in range(NWR):
                load_in(sp, c)
            sp.dma_start(wg[:, :, :], WIN[:, :, 3584:3600]).then_inc(s_wg, 16)
        norm_to_hT("l0_mix", 0, 0, range(4), cut(8192, 4, D), ahead=in_ahead)

        in_jobs = [(c, m) for c in range(WCH) for m in range(4 if c in (4, 5) else 2)]
        made = [sum(cc <= c for cc, _ in in_jobs) for c in range(WCH)]
        with nc.Block() as block:
            @block.sync
            def _(sp):
                for c in range(NWR, WCH):
                    sp.wait_ge(s_pj, made[c - NWR])
                    load_in(sp, c)

            @block.gpsimd
            def _(pool):
                pool.memset(CX[:, :, :, 0:2], 0.0)
                pool.memset(CX[:, :, :, 258:260], 0.0)

            @block.tensor
            def _(pe):
                for j, (c, m) in enumerate(in_jobs):
                    s = c % NWR
                    if m == 0:
                        pe.wait_ge(s_il, c + 1)
                    if j >= 6:
                        pe.wait_ge((s_pe_a, s_pe_v)[j % 2], (j - 6) // 2 + 1)
                    for k in range(KD):
                        st, sp_ = k == 0, k == KD - 1
                        x = slice(m * P, m * P + P)
                        if c in (4, 5):
                            mm = split_matmul(pe, bank[j % 6][:, 0:256], (hT[:, k, x], catT[:, k, x]), (WRH[s][:, k, :], WR[s][:, k, :]), st, sp_)
                        else:
                            mm = split_matmul(pe, bank[j % 6][:, :], (WRH[s][:, k, x], WR[s][:, k, x]), (hT[:, k, :], catT[:, k, :]), st, sp_)
                    mm.then_inc(s_pj, 1)
                pe.wait_ge(s_il, WCH + 1)
                for g in range(2):
                    x = slice(8 * g, 8 * g + 8)
                    for k in range(KD):
                        mm = split_matmul(pe, bank[6 + g][0:8, :], (wgh[:, k, x], wg[:, k, x]), (hT[:, k, :], catT[:, k, :]), k == 0, k == KD - 1)
                mm.then_inc(s_pj, 1)

            def evacuate(eng, parity, s_done, c):
                for j, (cc, m) in enumerate(in_jobs):
                    if cc != c or j % 2 != parity:
                        continue
                    eng.wait_ge(s_pj, j + 1)
                    b, scale = bank[j % 6][:, :], 1.0
                    f = (c % 2) * 2 + m
                    if c < 2:
                        dst, scale = nqT[:, f, :], 0.125
                    elif c < 4:
                        dst = nkT[:, f, :]
                    elif c < 6:
                        dst, b = V[:, m, (c % 2) * 256:(c % 2) * 256 + 256], b[:, 0:256]
                    elif c < 12:
                        dst, b = CX[:, 2 * (c - 6) + m, :, 2:258], b.rearrange("p (s n) -> p s n", s=2)
                    else:
                        dst = zT[:, f, :]
                    if parity == 0:
                        ins = eng.activation(dst, b, ACT.Copy, scale=scale)
                    else:
                        ins = eng.tensor_scalar(dst, b, scale, None, ALU.mult)
                    ins.then_inc(s_done, 1)

            @block.scalar
            def _(act):
                def split(c):
                    if c < WCH:
                        act.wait_ge(s_wi[c % NWR], 16 * (c // NWR) + 16)
                        high(act, WRH[c % NWR], WR[c % NWR]).then_inc(s_ih, 1)
                    elif c == WCH:
                        act.wait_ge(s_wg, 16)
                        high(act, wgh, wg[:, :, :]).then_inc(s_ih, 1)
                split(0)
                split(1)
                for c in range(WCH):
                    evacuate(act, 0, s_pe_a, c)
                    split(c + 2)
                act.wait_ge(s_pj, len(in_jobs) + 1)
                act.activation(graw[0:8, 0, :], bank[6][0:8, :], ACT.Copy)
                act.activation(graw[0:8, 1, :], bank[7][0:8, :], ACT.Copy)

            @block.vector
            def _(dve):
                def split(c):
                    if c <= WCH:
                        dve.wait_ge(s_ih, c + 1)
                        v, hi = (WR[c % NWR], WRH[c % NWR]) if c < WCH else (wg[:, :, :], wgh)
                        low(dve, v, hi).then_inc(s_il, 1)
                split(0)
                split(1)
                for c in range(WCH):
                    evacuate(dve, 1, s_pe_v, c)
                    split(c + 2)

        s_ncol = sem("nat_column_mask")

        def nat_bias(block, s_b):
            @block.sync
            def _(sp):
                sp.dma_start(natb, t["nat_bias"]).then_inc(s_bias_in, 16)

            @block.gpsimd
            def _(pool):
                pool.wait_ge(s_bias_in, 16)
                for i in range(2):
                    for g in range(2):
                        v = natb[:, i, 4 * g:4 * g + 4, :].rearrange("p h (r c) -> p (h r) c", c=64)
                        m = cst("natcol").rearrange("p (a c) -> p a c", a=1).to_broadcast([P, 16, 64])
                        pool.tensor_tensor(v, v, m, ALU.add).then_inc(s_b, 1)

        nat_jobs = [(tile, c, part) for tile in range(4) for c in range(4) for part in range(2)]
        attention("nat", nat_jobs, nqT, lambda c: nkT[:, c, :], lambda b, c, part: V[:, b, (2 * c + part) * HD:(2 * c + part + 1) * HD],
                  lambda tile, c, part: natb[:, tile, 2 * c + part, :], None, cut(20576, 3, 512), cut(22112, 2, 512), prep=nat_bias)

        def convolve(tag, n, src, dst, tap_col, acc):
            s_cv, s_si = sem(f"{tag}_convolved"), sem(f"{tag}_silu")
            with nc.Block() as block:
                @block.vector
                def _(dve):
                    link = linker(dve, "dve")
                    for c in range(n):
                        a = acc[:, c % 2, :].rearrange("p (s n) -> p s n", s=2)
                        if c >= 2:
                            dve.wait_ge(s_si, c - 1)
                        link(dve.tensor_scalar(a, src[:, c, :, 0:256], tap_col(0, c), None, ALU.mult))
                        for tap in range(1, TAPS):
                            ins = dve.scalar_tensor_tensor(a, src[:, c, :, tap:tap + 256], tap_col(tap, c), a, ALU.mult, ALU.add)
                            link(ins) if tap < TAPS - 1 else ins.then_inc(s_cv, 1)

                @block.scalar
                def _(act):
                    for c in range(n):
                        act.wait_ge(s_cv, c + 1)
                        act.activation(dst[:, c, :], acc[:, c % 2, :], ACT.Silu).then_inc(s_si, 1)

        FX = cut(14432, 12, NTOK)
        convolve("dn", 12, CX, FX, DNCONV, cut(20576, 2, 512))

        def gate_rows(tag, n, x, bias, alog, out_dt, out_g, sigmoid=None):
            s_1, s_2 = sem(f"{tag}_dve"), sem(f"{tag}_act")
            e, u, lnu, w, a = (hT[0:n, i, :] for i in range(5))
            a = gbias[0:n, 6:7]
            with nc.Block() as block:
                @block.vector
                def _(dve):
                    link = linker(dve, "dve")
                    link(dve.tensor_scalar(x, x, bias, None, ALU.add))
                    dve.scalar_tensor_tensor(e, x, -1.0, x, ALU.mult, ALU.min).then_inc(s_1, 1)
                    dve.wait_ge(s_2, 1)
                    dve.tensor_scalar(u, e, 1.0, None, ALU.add).then_inc(s_1, 1)
                    dve.wait_ge(s_1, 2)
                    link(dve.tensor_scalar(w, u, 1.0, None, ALU.subtract))
                    link(dve.tensor_tensor(e, e, w, ALU.subtract))
                    link(dve.reciprocal(w, u))
                    link(dve.tensor_tensor(e, e, w, ALU.mult))
                    dve.wait_ge(s_2, 2)
                    link(dve.tensor_tensor(e, e, lnu, ALU.add))
                    link(dve.scalar_tensor_tensor(out_dt, x, 0.0, e, ALU.max, ALU.add))
                    dve.wait_ge(s_2, 3)
                    link(dve.tensor_scalar(a, a, -1.0, None, ALU.mult))
                    dve.tensor_scalar(out_g, out_dt, a, None, ALU.mult)

                @block.scalar
                def _(act):
                    act.wait_ge(s_1, 1)
                    act.activation(e, e, ACT.Exp).then_inc(s_2, 1)
                    act.wait_ge(s_1, 2)
                    act.activation(lnu, u, ACT.Ln).then_inc(s_2, 1)
                    act.activation(a, alog, ACT.Exp).then_inc(s_2, 1)
                    if sigmoid is not None:
                        act.activation(sigmoid, sigmoid, ACT.Sigmoid)

        def spread(col, n, w):
            return col.rearrange("p (a b) -> p a b", b=1).to_broadcast([P, n, w])

        def heads(v, n):
            return v.rearrange("p (h e) -> p h e", h=n)

        gate_rows("dn_gates", 8, graw[0:8, 1, :], gbias[0:8, 0:1], gbias[0:8, 1:2], graw[0:8, 2, :], graw[0:8, 3, :],
                  sigmoid=graw[0:8, 0, :])

        dc = sb("delta_cols", [P, 9, 32])
        BETA, GS, GC, NGC, GL, EGC, EGL, EKD, BEG = (dc[:, i, :] for i in range(9))
        RL = small[:, 64:96]
        sq = cut(20576, 8, 512)
        s_q2, s_ssp, s_sse, s_rl, s_bc, s_nrm = (sem(f"dn_{x}") for x in
            ("squares", "norm_sums", "norm_sums_eps", "rnorm", "rnorm_spread", "normed"))
        with nc.Block() as block:
            @block.scalar
            def _(act):
                for c in range(8):
                    act.activation(sq[:, c, :], FX[:, c, :], ACT.Square).then_inc(s_q2, 1)

            @block.tensor
            def _(pe):
                for c in range(8):
                    pe.wait_ge(s_q2, c + 1)
                    for i in range(T):
                        mm = pe.matmul(bank[0][:, c * T + i:c * T + i + 1], sq[:, c, i * P:i * P + P], ones[:, 0:1], start=True, stop=True)
                mm.then_inc(s_ssp, 1)
                pe.wait_ge(s_rl, 1)
                for c in range(8):
                    if c >= 4:
                        pe.wait_ge(s_nrm, c - 3)
                    for i in range(T):
                        mm = pe.matmul(bank[1 + c % 4][:, i * P:i * P + P], RL[:, c * T + i:c * T + i + 1].to_broadcast([P, P]), ident,
                                       start=True, stop=True)
                    mm.then_inc(s_bc, 1)

            @block.gpsimd
            def _(pool):
                link = linker(pool, "pool")
                pool.wait_ge(s_sse, 1)
                link(pool.tensor_tensor(RL, RL, mhalf[:, 0:32], ALU.pow))
                link(pool.tensor_scalar(RL[:, 0:16], RL[:, 0:16], float(P) ** -0.5, None, ALU.mult))
                pool.sem_inc(s_rl, 1)

            @block.vector
            def _(dve):
                dve.wait_ge(s_ssp, 1)
                dve.tensor_scalar(RL, bank[0][:, 0:32], EPS, None, ALU.add).then_inc(s_sse, 1)
                for c in range(8):
                    dve.wait_ge(s_bc, c + 1)
                    dve.tensor_tensor(FX[:, c, :], FX[:, c, :], bank[1 + c % 4][:, :], ALU.mult).then_inc(s_nrm, 1)

        def columns_and_turns(tag, n_raw, raw, cols_out, n_g, gs, gc, ngc, gl, ekd, exps, after, turned):
            s_gt, s_gcp, s_cs, s_gl, s_ex, s_kv, s_kva, s_kvv = (sem(f"{tag}_{x}") for x in
                ("gates_turned", "gates_copied", "cumsums", "sums_copied", "exponents", "turned", "turned_copied_act", "turned_copied_dve"))
            w = T * n_raw
            nj = len(turned)
            with nc.Block() as block:
                @block.tensor
                def _(pe):
                    for g, r in enumerate(raw):
                        for i in range(T):
                            mm = pe.transpose(bank[0][:, w * g + n_raw * i:w * g + n_raw * (i + 1)], r[:, i * P:i * P + P], ident[0:n_raw, 0:n_raw])
                    mm.then_inc(s_gt, 1)

                    def turn(j):
                        if j >= 4:
                            pe.wait_ge((s_kva, s_kvv)[j % 2], (j - 4) // 2 + 1)
                        for b, src in enumerate(turned[j][0]):
                            mm = pe.transpose(bank[4 + j % 4][:, b * P:b * P + P], src, ident)
                        mm.then_inc(s_kv, 1)
                    for j in range(min(4, nj)):
                        turn(j)
                    pe.wait_ge(s_gcp, len(raw))
                    h = n_raw // 2
                    for i in range(T):
                        for d in range(2):
                            a = n_raw * i + h * d
                            pe.matmul(bank[1][:, a:a + h], cum[d], gs[:, a:a + h], start=True, stop=True)
                            mm = pe.matmul(bank[1][:, w + a:w + a + h], ones, gs[:, a:a + h], start=True, stop=True)
                    mm.then_inc(s_cs, 1)
                    for j in range(4, nj):
                        turn(j)

                def copy(eng, parity, s_done, lo, hi):
                    for j in range(lo + (parity - lo) % 2, hi, 2):
                        eng.wait_ge(s_kv, j + 1)
                        n = P * len(turned[j][0])
                        if parity == 0:
                            eng.activation(turned[j][1], bank[4 + j % 4][:, 0:n], ACT.Copy).then_inc(s_done, 1)
                        else:
                            eng.tensor_copy(turned[j][1], bank[4 + j % 4][:, 0:n]).then_inc(s_done, 1)

                @block.vector
                def _(dve):
                    link = linker(dve, "dve")
                    dve.wait_ge(s_gt, 1)
                    for g, dst in enumerate(cols_out):
                        dve.tensor_copy(dst, bank[0][:, w * g:w * g + w]).then_inc(s_gcp, 1)
                    copy(dve, 1, s_kvv, 0, min(4, nj))
                    dve.wait_ge(s_cs, 1)
                    link(dve.tensor_copy(gc, bank[1][:, 0:w]))
                    link(dve.tensor_copy(gl, bank[1][:, w:2 * w]))
                    link(dve.tensor_scalar(ngc, gc, -1.0, None, ALU.mult))
                    dve.tensor_tensor(ekd, gl, gc, ALU.subtract).then_inc(s_gl, 1)
                    copy(dve, 1, s_kvv, 4, nj)
                    dve.wait_ge(s_ex, 3)
                    after(dve)

                @block.scalar
                def _(act):
                    copy(act, 0, s_kva, 0, min(4, nj))
                    act.wait_ge(s_gl, 1)
                    for dst, src in exps:
                        act.activation(dst, src, ACT.Exp).then_inc(s_ex, 1)
                    copy(act, 0, s_kva, 4, nj)

        KT, VT = cut(0, T, 512), cut(2048, T, 512)
        columns_and_turns("dn_cols", 8, (graw[0:8, 0, :], graw[0:8, 3, :]), (BETA, GS), 8, GS, GC, NGC, GL, EKD,
                          ((EGC, GC), (EGL, GL), (EKD, EKD)),
                          lambda dve: dve.tensor_tensor(BEG, BETA, EGC, ALU.mult),
                          [([FX[:, c0 + h, i * P:i * P + P] for h in range(4)], dst[:, i, :]) for c0, dst in ((4, KT), (8, VT)) for i in range(T)])

        def col(v, i, d, h, w=4):
            a = (2 * w) * i + w * d + h
            return v[:, a:a + 1]

        KB = cut(8192, 2, 4, NTOK)
        AT, QA = cut(20576, 8, 512), cut(24672, 8, 512)
        DT = cut(12288, 2, 512)
        LMT = cut(4096, 2, LEVELS, P)
        s_bs, s_kb, s_lm, s_pd, s_pa, s_pq, s_dt, s_am, s_qm = (sem(f"dn_{x}") for x in
            ("beta_spread", "beta_keys", "level_masks", "log_decay", "kk", "kq", "decay", "a_masked", "q_masked"))
        with nc.Block() as block:
            @block.sync
            def _(sp):
                sp.dma_start(LMT, t["levels"]).then_inc(s_lm, 16)

            @block.tensor
            def _(pe):
                for d in range(2):
                    for h in range(4):
                        j = 4 * d + h
                        if j >= 2:
                            pe.wait_ge(s_kb, j - 1)
                        for i in range(T):
                            mm = pe.matmul(bank[6 + j % 2][:, i * P:i * P + P], col(BETA, i, d, h).to_broadcast([P, P]), ident, start=True, stop=True)
                        mm.then_inc(s_bs, 1)
                for g in range(8):
                    d, i = divmod(g, T)
                    tk = slice(i * P, i * P + P)
                    if g >= 2:
                        pe.wait_ge(s_dt, g - 1)
                    pe.matmul(quad(g % 2), ident, neg[d].rearrange("p (a c) -> p a c", a=1).to_broadcast([P, 4, P]), start=True, stop=False, skip_group_check=True)
                    for h in range(4):
                        mm = pe.matmul(quad(g % 2)[:, h, :], col(GS, i, d, h).to_broadcast([P, P]), cum[d], start=False, stop=(h == 3), skip_group_check=True)
                    mm.then_inc(s_pd, 1)
                    if g >= 2:
                        pe.wait_ge(s_am, g - 1)
                    pe.wait_ge(s_kb, 4 * d + 4)
                    for h in range(4):
                        mm = pe.matmul(quad(2 + g % 2)[:, h, :], FX[:, 4 + h, tk], KB[:, d, h, tk], start=True, stop=True)
                    mm.then_inc(s_pa, 1)
                    if g >= 2:
                        pe.wait_ge(s_qm, g - 1)
                    for h in range(4):
                        mm = pe.matmul(quad(4 + g % 2)[:, h, :], FX[:, 4 + h, tk], FX[:, h, tk], start=True, stop=True)
                    mm.then_inc(s_pq, 1)

            @block.scalar
            def _(act):
                for g in range(8):
                    d, i = divmod(g, T)
                    act.wait_ge(s_pd, g + 1)
                    if g >= 2:
                        act.wait_ge(s_qm, g - 1)
                    for h in range(4):
                        ins = act.activation(DT[:, g % 2, h * P:h * P + P], quad(g % 2)[:, h, :], ACT.Exp, bias=col(NGC, i, d, h))
                    ins.then_inc(s_dt, 1)

            @block.vector
            def _(dve):
                for j in range(8):
                    dve.wait_ge(s_bs, j + 1)
                    dve.tensor_tensor(KB[:, j // 4, j % 4, :], FX[:, 4 + j % 4, :], bank[6 + j % 2][:, :], ALU.mult).then_inc(s_kb, 1)
                for g in range(8):
                    dve.wait_ge(s_dt, g + 1)
                    dve.wait_ge(s_pa, g + 1)
                    dve.tensor_tensor(AT[:, g, :], bank[2 + g % 2][:, :], DT[:, g % 2, :], ALU.mult).then_inc(s_am, 1)
                    dve.wait_ge(s_pq, g + 1)
                    dve.tensor_tensor(QA[:, g, :], bank[4 + g % 2][:, :], DT[:, g % 2, :], ALU.mult).then_inc(s_qm, 1)

        XI, XT = cut(8192, 8, 512), cut(16480, 8, 512)
        T1 = hT[:, :, :]
        BT = cut(12288, 4, 512)
        s_bt, s_xt0, s_a, s_x0, s_t1, s_b, s_up = (sem(f"inv_{x}") for x in
            ("level_block", "first_xt", "first_product", "first_x", "product_copied", "second_product", "updated"))
        with nc.Block() as block:
            @block.gpsimd
            def _(pool):
                pool.wait_ge(s_lm, 16)
                for n in range(8 * LEVELS):
                    l, g = divmod(n, 8)
                    if n >= 4:
                        pool.wait_ge(s_a, n - 3)
                        pool.wait_ge(s_xt0, min(n - 3, 8))
                    m = LMT[:, g // 4, l, :].rearrange("p (a c) -> p a c", a=1).to_broadcast([P, 4, P])
                    pool.tensor_tensor(heads(BT[:, n % 4, :], 4), heads(AT[:, g, :], 4), m, ALU.mult).then_inc(s_bt, 1)
                    if l == 0:
                        pool.wait_ge(s_bt, n + 1)
                        pool.tensor_tensor(heads(XT[:, g, :], 4), ident.rearrange("p (a c) -> p a c", a=1).to_broadcast([P, 4, P]),
                                           heads(BT[:, n % 4, :], 4), ALU.subtract).then_inc(s_xt0, 1)

            @block.tensor
            def _(pe):
                for l in range(LEVELS):
                    for g in range(8):
                        n = 8 * l + g
                        pe.wait_ge(s_bt, n + 1)
                        if n >= 4:
                            pe.wait_ge(s_x0, n - 3) if n < 12 else pe.wait_ge(s_t1, n - 11)
                        if l == 1:
                            pe.wait_ge(s_x0, g + 1)
                        if l >= 2:
                            pe.wait_ge(s_up, 8 * (l - 2) + g + 1)
                        for h in range(4):
                            mm = pe.matmul(quad(n % 4)[:, h, :], BT[:, n % 4, h * P:h * P + P], ident if l == 0 else XI[:, g, h * P:h * P + P],
                                           start=True, stop=True)
                        mm.then_inc(s_a, 1)
                    if l == 0:
                        continue
                    for g in range(8):
                        m = 8 * (l - 1) + g
                        pe.wait_ge(s_t1, m + 1)
                        pe.wait_ge(s_xt0, g + 1) if l == 1 else None
                        if m >= 2:
                            pe.wait_ge(s_up, m - 1)
                        for h in range(4):
                            hs = slice(h * P, h * P + P)
                            if l < LEVELS - 1:
                                pe.matmul(quad(4 + 2 * (m % 2))[:, h, :], XT[:, g, hs], T1[:, g, hs], start=True, stop=True)
                            mm = pe.matmul(quad(5 + 2 * (m % 2))[:, h, :], T1[:, g, hs], XT[:, g, hs], start=True, stop=True)
                        mm.then_inc(s_b, 1)

            @block.scalar
            def _(act):
                for n in range(8, 8 * LEVELS):
                    act.wait_ge(s_a, n + 1)
                    act.activation(T1[:, n % 8, :], bank[n % 4][:, :], ACT.Copy).then_inc(s_t1, 1)

            @block.vector
            def _(dve):
                for g in range(8):
                    dve.wait_ge(s_a, g + 1)
                    dve.tensor_tensor(heads(XI[:, g, :], 4), ident.rearrange("p (a c) -> p a c", a=1).to_broadcast([P, 4, P]),
                                      quad(g % 4), ALU.subtract).then_inc(s_x0, 1)
                for m in range(8 * (LEVELS - 1)):
                    l, g = m // 8 + 1, m % 8
                    dve.wait_ge(s_b, m + 1)
                    if l < LEVELS - 1:
                        dve.tensor_tensor(XI[:, g, :], XI[:, g, :], bank[4 + 2 * (m % 2)][:, :], ALU.subtract)
                    dve.tensor_tensor(XT[:, g, :], XT[:, g, :], bank[5 + 2 * (m % 2)][:, :], ALU.subtract).then_inc(s_up, 1)

        U, WT, KDV = cut(8192, 8, 512), cut(20576, 8, 512), hT[:, :, :]
        BV, BW = cut(4096, 2, 512), cut(5120, 2, 512)
        s_bv, s_bw, s_pu, s_cu, s_cw = (sem(f"uw_{x}") for x in ("beta_v", "beta_k", "products", "u_copied", "w_copied"))

        def gcol(v, g, w=4):
            d, i = divmod(g, T)
            a = 2 * w * i + w * d
            return v[:, a:a + w]
        with nc.Block() as block:
            @block.vector
            def _(dve):
                for g in range(9):
                    if g < 8:
                        if g >= 2:
                            dve.wait_ge(s_pu, g - 1)
                        dve.tensor_tensor(heads(BV[:, g % 2, :], 4), heads(VT[:, g % T, :], 4), spread(gcol(BETA, g), 4, P), ALU.mult).then_inc(s_bv, 1)
                    if g >= 1:
                        dve.wait_ge(s_pu, g)
                        dve.tensor_copy(WT[:, g - 1, :], bank[2 + (g - 1) % 2][:, :]).then_inc(s_cw, 1)

            @block.gpsimd
            def _(pool):
                for g in range(8):
                    if g >= 2:
                        pool.wait_ge(s_pu, g - 1)
                    pool.tensor_tensor(heads(BW[:, g % 2, :], 4), heads(KT[:, g % T, :], 4), spread(gcol(BEG, g), 4, P), ALU.mult).then_inc(s_bw, 1)
                    pool.tensor_tensor(heads(KDV[:, g, :], 4), heads(KT[:, g % T, :], 4), spread(gcol(EKD, g), 4, P), ALU.mult)

            @block.tensor
            def _(pe):
                for g in range(8):
                    pe.wait_ge(s_bv, g + 1)
                    pe.wait_ge(s_bw, g + 1)
                    if g >= 2:
                        pe.wait_ge(s_cu, g - 1)
                        pe.wait_ge(s_cw, g - 1)
                    for h in range(4):
                        hs = slice(h * P, h * P + P)
                        pe.matmul(quad(g % 2)[:, h, :], XT[:, g, hs], BV[:, g % 2, hs], start=True, stop=True)
                        mm = pe.matmul(quad(2 + g % 2)[:, h, :], BW[:, g % 2, hs], XT[:, g, hs], start=True, stop=True)
                    mm.then_inc(s_pu, 1)

            @block.scalar
            def _(act):
                for g in range(8):
                    act.wait_ge(s_pu, g + 1)
                    act.activation(U[:, g, :], bank[g % 2][:, :], ACT.Copy).then_inc(s_cu, 1)

        S, VN = cut(12288, 2, 512), cut(13312, 2, 512)
        O = cut(16480, T, 512)
        tmp = cut(18528, 2, 512)
        s_s0, s_p1, s_vn, s_p2, s_se, s_st = (sem(f"scan_{x}") for x in
            ("state_zero", "from_state", "v_new", "products", "state_decayed", "state"))
        with nc.Block() as block:
            @block.gpsimd
            def _(pool):
                pool.memset(S, 0.0).then_inc(s_s0, 1)
                for n in range(8):
                    i, d = divmod(n, 2)
                    g = d * T + CHUNK_ORDER[d][i]
                    pool.wait_ge(s_p1, n + 1)
                    if n >= 2:
                        pool.wait_ge(s_st, n - 1)
                    else:
                        pool.wait_ge(s_s0, 1)
                    pool.tensor_tensor(heads(S[:, d, :], 4), heads(S[:, d, :], 4), spread(gcol(EGL, g), 4, P), ALU.mult).then_inc(s_se, 1)

            @block.tensor
            def _(pe):
                pe.wait_ge(s_s0, 1)
                for i in range(T):
                    for d in range(2):
                        n, tile = 2 * i + d, CHUNK_ORDER[d][i]
                        g = d * T + tile
                        if n >= 2:
                            pe.wait_ge(s_st, n - 1)
                        for h in range(4):
                            hs = slice(h * P, h * P + P)
                            pe.matmul(quad(d)[:, h, :], WT[:, g, hs], S[:, d, hs], start=True, stop=True)
                            mm = pe.matmul(quad(2 + d)[:, h, :], FX[:, h, tile * P:tile * P + P], S[:, d, hs], start=True, stop=True)
                        mm.then_inc(s_p1, 1)
                    for d in range(2):
                        n, tile = 2 * i + d, CHUNK_ORDER[d][i]
                        g = d * T + tile
                        pe.wait_ge(s_vn, n + 1)
                        for h in range(4):
                            hs = slice(h * P, h * P + P)
                            pe.matmul(quad(6 + d)[:, h, :], KDV[:, g, hs], VN[:, d, hs], start=True, stop=True)
                        for h in range(4):
                            hs = slice(h * P, h * P + P)
                            mm = pe.matmul(quad(4 + d)[:, h, :], QA[:, g, hs], VN[:, d, hs], start=True, stop=True)
                        mm.then_inc(s_p2, 1)

            @block.vector
            def _(dve):
                link = linker(dve, "dve")
                for i in range(T):
                    for d in range(2):
                        n, g = 2 * i + d, d * T + CHUNK_ORDER[d][i]
                        dve.wait_ge(s_p1, n + 1)
                        dve.tensor_tensor(VN[:, d, :], U[:, g, :], bank[d][:, :], ALU.subtract).then_inc(s_vn, 1)
                    for d in range(2):
                        n, g = 2 * i + d, d * T + CHUNK_ORDER[d][i]
                        last = dve.tensor_tensor(heads(tmp[:, d, :], 4), quad(2 + d), spread(gcol(EGC, g), 4, P), ALU.mult)
                    link(last)
                    for d in range(2):
                        n, tile = 2 * i + d, CHUNK_ORDER[d][i]
                        dve.wait_ge(s_p2, n + 1)
                        dve.wait_ge(s_se, n + 1)
                        dve.tensor_tensor(S[:, d, :], S[:, d, :], bank[6 + d][:, :], ALU.add).then_inc(s_st, 1)
                        if i in (0, 2):
                            link(dve.tensor_tensor(O[:, tile, :], tmp[:, d, :], bank[4 + d][:, :], ALU.add))
                        else:
                            link(dve.tensor_tensor(O[:, tile, :], O[:, tile, :], tmp[:, d, :], ALU.add))
                            link(dve.tensor_tensor(O[:, tile, :], O[:, tile, :], bank[4 + d][:, :], ALU.add))

        osq, zs, orr = cut(8192, 16, P), cut(0, 4, NTOK), small[:, 96:112]
        s_wo = [sem(f"l0_out_w{i}") for i in range(4)]
        wout, wouth = cut(20576, KD, D), cut(8192, KD, D)
        s_q, s_oss, s_or, s_on, s_ot, s_zs = (sem(f"gn_{x}") for x in ("squares", "sums", "rms", "normed", "turned", "silu_z"))
        with nc.Block() as block:
            @block.sync
            def _(sp):
                load_out_weights(sp, t["ev_w_out"].rearrange("(k p) n -> p k n", p=P), wout, s_wo)

            @block.scalar
            def _(act):
                act.activation(zs, zT, ACT.Silu).then_inc(s_zs, 1)

            @block.vector
            def _(dve):
                link = linker(dve, "dve")
                o3 = O.rearrange("p t (h e) -> p (t h) e", h=4)
                link(dve.tensor_tensor(osq, o3, o3, ALU.mult))
                dve.tensor_reduce(orr, osq, AX.X, ALU.add).then_inc(s_oss, 1)
                dve.wait_ge(s_or, 1)
                dve.tensor_tensor(o3, o3, spread(orr, 16, P), ALU.mult).then_inc(s_on, 1)
                dve.wait_ge(s_zs, 1)
                for h in range(4):
                    dve.wait_ge(s_ot, h + 1)
                    dve.scalar_tensor_tensor(catT[:, 4 + h, :], bank[h][:, :], DNNORM, zs[:, h, :], ALU.mult, ALU.mult)

            @block.gpsimd
            def _(pool):
                link = linker(pool, "pool")
                pool.wait_ge(s_oss, 1)
                link(pool.tensor_scalar(orr, orr, 1.0 / P, EPS, ALU.mult, ALU.add))
                pool.tensor_tensor(orr, orr, mhalf[:, 0:16], ALU.pow).then_inc(s_or, 1)

            @block.tensor
            def _(pe):
                pe.wait_ge(s_on, 1)
                for h in range(4):
                    for i in range(T):
                        mm = pe.transpose(bank[h][:, i * P:i * P + P], O[:, i, h * P:h * P + P], ident)
                    mm.then_inc(s_ot, 1)

        project_and_add("l0_out", 4, 0, 4, s_wo, wout, wouth)

        NS = 3
        W13 = [cut(4096 + i * 2048, 2, KD, P) for i in range(NS)]
        W13H = [cut(10240 + i * 2048, 2, KD, P) for i in range(NS)]
        gT, sl = cut(16384, NF, NTOK), cut(27648, 2, 512)
        W2 = [cut(i * 2048, 2, D) for i in range(NS)]
        W2H = [cut(6144 + i * 2048, 2, D) for i in range(NS)]
        s_w13 = [sem(f"ffn_w13_{i}") for i in range(NS)]
        s_w2 = [sem(f"ffn_w2_{i}") for i in range(NS)]
        s_h1, s_h3, s_sl, s_g, s_13h, s_13l = (sem(f"ffn_{x}") for x in ("h1", "h3", "silu", "gated", "w13_high", "w13_low"))
        w1v = t["ffn_w1"].rearrange("(k p) (c w) -> p k c w", p=P, w=P)
        w3v = t["ffn_w3"].rearrange("(k p) (c w) -> p k c w", p=P, w=P)
        w2v = t["ffn_w2"].rearrange("(c two p) n -> p c two n", p=P, two=2)
        NC = NF // 2

        def load_13(sp, n):
            for m, w in enumerate((w1v, w3v)):
                sp.dma_start(W13[n % NS][:, m, :, :], w[:, :, n, :]).then_inc(s_w13[n % NS], 16)

        def load_2(sp, c):
            sp.dma_start(W2[c % NS], w2v[:, c, :, :]).then_inc(s_w2[c % NS], 16)
        norm_to_hT("l0_ffn", 0, 1, range(4), cut(0, 4, D), ahead=lambda sp: [load_13(sp, n) for n in range(NS)])

        with nc.Block() as block:
            @block.sync
            def _(sp):
                for c in range(2):
                    load_2(sp, c)
                for n in range(NS, NF):
                    sp.wait_ge(s_h3, n - NS + 1)
                    load_13(sp, n)

            @block.tensor
            def _(pe):
                for n in range(NF):
                    pe.wait_ge(s_13l, n + 1)
                    for m, s_h in enumerate((s_h1, s_h3)):
                        if n >= 2:
                            pe.wait_ge((s_sl, s_g)[m], n - 1)
                        for k in range(KD):
                            w = (W13H[n % NS][:, m, k, :], W13[n % NS][:, m, k, :])
                            mm = split_matmul(pe, bank[4 * m + n % 2][:, :], w, (hT[:, k, :], catT[:, k, :]), k == 0, k == KD - 1)
                        mm.then_inc(s_h, 1)

            @block.scalar
            def _(act):
                def split(n):
                    if n < NF:
                        act.wait_ge(s_w13[n % NS], 32 * (n // NS) + 32)
                        high(act, W13H[n % NS], W13[n % NS]).then_inc(s_13h, 1)
                split(0)
                split(1)
                for n in range(NF):
                    act.wait_ge(s_h1, n + 1)
                    if n >= 2:
                        act.wait_ge(s_g, n - 1)
                    act.activation(sl[:, n % 2, :], bank[n % 2][:, :], ACT.Silu).then_inc(s_sl, 1)
                    split(n + 2)

            @block.vector
            def _(dve):
                def split(n):
                    if n < NF:
                        dve.wait_ge(s_13h, n + 1)
                        low(dve, W13[n % NS], W13H[n % NS]).then_inc(s_13l, 1)
                split(0)
                split(1)
                for n in range(NF):
                    split(n + 2)
                    dve.wait_ge(s_sl, n + 1)
                    dve.wait_ge(s_h3, n + 1)
                    dve.tensor_tensor(gT[:, n, :], sl[:, n % 2, :], bank[4 + n % 2][:, :], ALU.mult).then_inc(s_g, 1)

        s_dn, s_dy, s_dss, s_dr, s_dh, s_dl = (sem(f"ffn_{x}") for x in ("down", "down_y", "down_squares", "down_rms", "down_high", "down_low"))
        gh_rest = cut(12288, NF - 2 * KD, NTOK)

        def gh(c):
            v, at_ = (hT, 0) if c < 4 else (catT, 8) if c < 8 else (gh_rest, 16)
            return v[:, 2 * c - at_:2 * c - at_ + 2, :]
        with nc.Block() as block:
            @block.sync
            def _(sp):
                load_2(sp, 2)
                for c in range(NS, NC):
                    sp.wait_ge(s_dn, c - NS + 1)
                    load_2(sp, c)

            @block.tensor
            def _(pe):
                for c in range(NC):
                    pe.wait_ge(s_dl, c + 1)
                    for f in range(2):
                        for i in range(T):
                            x = slice(i * P, i * P + P)
                            for half in range(2):
                                o = slice(half * 512, half * 512 + 512)
                                mm = split_matmul(pe, bank[2 * i + half][:, :], (gh(c)[:, f, x], gT[:, 2 * c + f, x]), (W2H[c % NS][:, f, o], W2[c % NS][:, f, o]),
                                                  c == 0 and f == 0, c == NC - 1 and f == 1)
                    mm.then_inc(s_dn, 1)
                pe.wait_ge(s_dn, NC)
                pe.sem_inc(s_dy, 8)

            def split_high(act):
                for c in range(NC):
                    act.wait_ge(s_w2[c % NS], 16 * (c // NS) + 16)
                    high(act, gh(c), gT[:, 2 * c:2 * c + 2, :])
                    high(act, W2H[c % NS], W2[c % NS]).then_inc(s_dh, 1)

            def split_low(dve):
                for c in range(NC):
                    dve.wait_ge(s_dh, c + 1)
                    low(dve, gT[:, 2 * c:2 * c + 2, :], gh(c))
                    low(dve, W2[c % NS], W2H[c % NS]).then_inc(s_dl, 1)
            add_normed(block, 4, 1, 5, s_dy, s_dss, s_dr, small[:, 0:8], small[:, 8:16], cut(0, 8, 512), cut(4096, D), split_high, split_low)

        nc.clear_and_free_semaphores(stage_sems)
        nc.all_engine_barrier()
        stage_sems = []

        qT, kT, V1, Z1 = cut(0, 4, LAT), cut(1024, NTOK), cut(1536, T, P), cut(2048, 2, 512)
        CS = cut(3072, 8, 2, 260)
        dtr = catT[0:16, 4:8, :]
        NOD, OCH = 4, 10
        WI = [cut(12288 + i * 4096, KD, 256) for i in range(NOD)]
        WIH = [cut(14336 + i * 4096, KD, 256) for i in range(NOD)]
        s_oi = [sem(f"od_in_w{i}") for i in range(NOD)]
        s_oj, s_oa, s_ov, s_oh, s_ol = (sem(f"od_in_{x}") for x in ("product", "copied_act", "copied_dve", "high", "low"))
        WOD = t["od_w_in"].rearrange("(k p) n -> p k n", p=P)

        def od_cols(c):
            return 16 if c == OCH - 1 else 256

        def load_od(sp, c):
            sp.dma_start(WI[c % NOD][:, :, 0:od_cols(c)], WOD[:, :, c * 256:c * 256 + od_cols(c)]).then_inc(s_oi[c % NOD], 16)
        norm_to_hT("l1_mix", 1, 0, range(4), cut(0, 4, D), ahead=lambda sp: [load_od(sp, c) for c in range(NOD)])

        od_jobs = ([("q", c, c // 2, c % 2 * P) for c in range(4)] + [("k", 0, 2, 0), ("v", 0, 2, P)]
                   + [("z", i, 3 + half, half) for half in range(2) for i in range(2)]
                   + [("conv", c, 5 + c // 2, c % 2 * P) for c in range(8)] + [("dt", 0, 9, 0)])
        od_made = [sum(job[2] <= c for job in od_jobs) for c in range(OCH)]
        with nc.Block() as block:
            @block.sync
            def _(sp):
                for c in range(NOD, OCH):
                    sp.wait_ge(s_oj, od_made[c - NOD])
                    load_od(sp, c)

            @block.gpsimd
            def _(pool):
                pool.memset(CS[:, :, :, 0:2], 0.0)
                pool.memset(CS[:, :, :, 258:260], 0.0)

            @block.tensor
            def _(pe):
                for j, (kind, i, c, at_) in enumerate(od_jobs):
                    pe.wait_ge(s_ol, c + 1)
                    if j >= 8:
                        pe.wait_ge((s_oa, s_ov)[j % 2], (j - 8) // 2 + 1)
                    b, s = bank[j % 8], c % NOD
                    for tile in range(T if kind == "v" else 1):
                        for k in range(KD):
                            st, sp_ = k == 0, k == KD - 1
                            x = lambda v, a, n: (v[0][:, k, a:a + n], v[1][:, k, a:a + n])
                            h, w = (hT, catT), (WIH[s], WI[s])
                            if kind == "q":
                                mm = split_matmul(pe, b[:, 0:LAT], x(w, at_, P), x(h, 0, LAT), st, sp_)
                            elif kind == "v":
                                mm = split_matmul(pe, b[:, tile * P:tile * P + P], x(h, tile * P, P), x(w, at_, P), st, sp_)
                            elif kind == "z":
                                mm = split_matmul(pe, b[:, 0:256], x(h, i * P, P), x(w, 0, 256), st, sp_)
                            elif kind == "dt":
                                mm = split_matmul(pe, b[0:16, :], x(w, 0, 16), x(h, 0, NTOK), st, sp_)
                            else:
                                mm = split_matmul(pe, b[:, :], x(w, at_, P), x(h, 0, NTOK), st, sp_)
                    mm.then_inc(s_oj, 1)

            def od_copy(eng, parity, s_done, chunk):
                for j, (kind, i, c, at_) in enumerate(od_jobs):
                    if c != chunk or j % 2 != parity:
                        continue
                    eng.wait_ge(s_oj, j + 1)
                    b, scale = bank[j % 8][:, :], 1.0
                    if kind == "q":
                        dst, b, scale = qT[:, i, :], b[:, 0:LAT], 0.125
                    elif kind == "k":
                        dst = kT
                    elif kind == "v":
                        dst = V1.rearrange("p t n -> p (t n)")
                    elif kind == "z":
                        dst, b = Z1[:, i, at_ * 256:at_ * 256 + 256], b[:, 0:256]
                    elif kind == "conv":
                        dst, b = CS[:, i, :, 2:258], b.rearrange("p (s n) -> p s n", s=2)
                    else:
                        dst, b = dtr[:, 0, :], b[0:16, :]
                    if parity == 0:
                        eng.activation(dst, b, ACT.Copy, scale=scale).then_inc(s_done, 1)
                    else:
                        eng.tensor_scalar(dst, b, scale, None, ALU.mult).then_inc(s_done, 1)

            @block.scalar
            def _(act):
                def split(c):
                    if c < OCH:
                        act.wait_ge(s_oi[c % NOD], 16 * (c // NOD) + 16)
                        n = slice(0, od_cols(c))
                        high(act, WIH[c % NOD][:, :, n], WI[c % NOD][:, :, n]).then_inc(s_oh, 1)
                for c in range(3):
                    split(c)
                for c in range(OCH):
                    od_copy(act, 0, s_oa, c)
                    split(c + 3)

            @block.vector
            def _(dve):
                def split(c):
                    if c < OCH:
                        dve.wait_ge(s_oh, c + 1)
                        n = slice(0, od_cols(c))
                        low(dve, WI[c % NOD][:, :, n], WIH[c % NOD][:, :, n]).then_inc(s_ol, 1)
                for c in range(3):
                    split(c)
                for c in range(OCH):
                    od_copy(dve, 1, s_ov, c)
                    split(c + 3)

        rt = cut(7232, 2, 2, LAT)
        s_rp, s_rd = sem("rope_turned"), sem("rope_done")
        with nc.Block() as block:
            @block.tensor
            def _(pe):
                for c in range(5):
                    src = qT[:, c, :] if c < 4 else kT[:, 0:LAT]
                    if c >= 2:
                        pe.wait_ge(s_rd, c - 1)
                    pe.matmul(bank[c % 2][:, 0:LAT], cst("rot"), src, start=True, stop=True).then_inc(s_rp, 1)

            @block.vector
            def _(dve):
                link = linker(dve, "dve")
                for c in range(5):
                    src = qT[:, c, :] if c < 4 else kT[:, 0:LAT]
                    dve.wait_ge(s_rp, c + 1)
                    link(dve.tensor_tensor(rt[:, c % 2, 0, :], src, cst("cos"), ALU.mult))
                    link(dve.tensor_tensor(rt[:, c % 2, 1, :], bank[c % 2][:, 0:LAT], cst("sin"), ALU.mult))
                    ins = dve.tensor_tensor(src, rt[:, c % 2, 0, :], rt[:, c % 2, 1, :], ALU.add)
                    link(ins) if c >= 5 else ins.then_inc(s_rd, 1)
                    dve.wait_ge(s_rd, c + 1)

        band = cst("band").rearrange("p (t k) -> p t k", t=2)
        wa_jobs = [(tile, c, part) for tile in range(2) for c in range(4) for part in range(2)]
        attention("win", wa_jobs, qT, lambda c: kT, lambda b, c, part: V1[:, b, part * HD:part * HD + HD],
                  lambda tile, c, part: band[:, tile, :], lambda c, part: rowcol[:, c + 4 * part:c + 4 * part + 1],
                  cut(7232, 3, 512), cut(8768, 2, 512))

        FS = cut(9280, 8, NTOK)
        convolve("ssd", 8, CS, FS, SSDCONV, cut(7232, 2, 512))
        gate_rows("ssd_gates", 16, dtr[:, 0, :], gbias[:, 2:3], gbias[:, 3:4], dtr[:, 1, :], dtr[:, 2, :])
        sc = cut(13376, 9, 64)
        DTC, DA, AC, NAC, AL, EAC, EAL, EDS, DTD = (sc[:, i, :] for i in range(9))
        XT1, BT1 = cut(13952, T, 512), cut(16000, T, 2 * P)
        columns_and_turns("ssd_cols", 16, (dtr[:, 1, :], dtr[:, 2, :]), (DTC, DA), 16, DA, AC, NAC, AL, EDS,
                          ((EAC, AC), (EAL, AL), (EDS, EDS)),
                          lambda dve: dve.tensor_tensor(DTD, DTC, EDS, ALU.mult),
                          [([FS[:, c, i * P:i * P + P] for c in range(4)], XT1[:, i, :]) for i in range(T)]
                          + [([FS[:, 4 + c, i * P:i * P + P] for c in range(2)], BT1[:, i, :]) for i in range(T)])

        XS, XD = cut(17024, 2, 512), cut(18048, 2, 512)
        H, Y = cut(19072, 2, 512), cut(20096, 2, 512)
        LT, MT = cut(21120, 2, 512), cut(22144, 2, 512)
        yt = cut(23168, 512)

        def hcol(v, tile, d):
            return v[:, 16 * tile + 8 * d:16 * tile + 8 * d + 8]
        ssd_steps = [(i, d, CHUNK_ORDER[d][i]) for i in range(T) for d in range(2)]
        lat_steps = [n for n, s in enumerate(ssd_steps) if s[2] < 2]
        s_h0, s_xs, s_st, s_hd, s_h, s_ld, s_lx, s_cb, s_mt, s_mu, s_yd, s_yo, s_yv, s_xd = (sem(f"ssd_{x}") for x in
            ("state_zero", "decayed_x", "state_product", "state_decayed", "state", "log_decay", "decay", "cb", "m", "y_diag_half", "y_diag", "y_off", "y_added", "xd"))
        with nc.Block() as block:
            @block.gpsimd
            def _(pool):
                pool.memset(H, 0.0).then_inc(s_h0, 1)
                pool.wait_ge(s_h0, 1)
                for n, (i, d, tile) in enumerate(ssd_steps):
                    if n < 6:
                        if n >= 2:
                            pool.wait_ge(s_st, n - 1)
                        pool.tensor_tensor(heads(XS[:, n % 2, :], 8), heads(XT1[:, tile, :], 8), spread(hcol(DTD, tile, d), 8, HD), ALU.mult).then_inc(s_xs, 1)
                        if n >= 2:
                            pool.wait_ge(s_h, n - 1)
                        if n >= 4:
                            pool.wait_ge(s_yo, n - 3)
                        pool.tensor_tensor(heads(H[:, d, :], 8), heads(H[:, d, :], 8), spread(hcol(EAL, tile, d), 8, HD), ALU.mult).then_inc(s_hd, 1)

            @block.tensor
            def _(pe):
                for n, (i, d, tile) in enumerate(ssd_steps):
                    tk = slice(tile * P, tile * P + P)
                    if n >= 4:
                        m = n - 4
                        if m >= 1:
                            pe.wait_ge(s_mt, 2 * m)
                        for g in range(2):
                            mm = pe.matmul(quad(4)[:, g, :], FS[:, 4 + g, tk], FS[:, 6 + g, tk], start=True, stop=True)
                        mm.then_inc(s_cb, 1)
                        for g in range(2):
                            q = 2 * m + g
                            if q >= 2:
                                pe.wait_ge(s_lx, q - 1)
                            pe.matmul(quad(q % 2), ident, neg[d].rearrange("p (a c) -> p a c", a=1).to_broadcast([P, 4, P]), start=True, stop=False, skip_group_check=True)
                            for h in range(4):
                                mm = pe.matmul(quad(q % 2)[:, h, :], hcol(DA, tile, d)[:, 4 * g + h:4 * g + h + 1].to_broadcast([P, P]), cum[d], start=False, stop=(h == 3), skip_group_check=True)
                            mm.then_inc(s_ld, 1)
                        pe.wait_ge(s_h, n - 1)
                        if m >= 1:
                            pe.wait_ge(s_yv, m)
                        for g in range(2):
                            mm = pe.matmul(bank[5][:, g * 256:g * 256 + 256], FS[:, 6 + g, tk], H[:, d, g * 256:g * 256 + 256], start=True, stop=True)
                        mm.then_inc(s_yo, 1)
                        pe.wait_ge(s_xd, m + 1)
                        for g in range(2):
                            pe.wait_ge(s_mt, 2 * m + g + 1)
                            for h in range(4):
                                hh = 4 * g + h
                                mm = pe.matmul(bank[6][:, hh * HD:hh * HD + HD], MT[:, g, h * P:h * P + P], XD[:, m % 2, hh * HD:hh * HD + HD], start=True, stop=True)
                            mm.then_inc(s_yd, 1)
                    if n < 6:
                        pe.wait_ge(s_xs, n + 1)
                        if n >= 2:
                            pe.wait_ge(s_h, n - 1)
                        for g in range(2):
                            mm = pe.matmul(bank[2 + n % 2][:, g * 256:g * 256 + 256], BT1[:, tile, g * P:g * P + P], XS[:, n % 2, g * 256:g * 256 + 256], start=True, stop=True)
                        mm.then_inc(s_st, 1)

            @block.scalar
            def _(act):
                for m in range(4):
                    i, d, tile = ssd_steps[4 + m]
                    for g in range(2):
                        q = 2 * m + g
                        act.wait_ge(s_ld, q + 1)
                        if q >= 2:
                            act.wait_ge(s_mt, q - 1)
                        for h in range(4):
                            ins = act.activation(LT[:, q % 2, h * P:h * P + P], quad(q % 2)[:, h, :], ACT.Exp, bias=hcol(NAC, tile, d)[:, 4 * g + h:4 * g + h + 1])
                        ins.then_inc(s_lx, 1)

            @block.vector
            def _(dve):
                link = linker(dve, "dve")
                for i in range(2):
                    dve.tensor_tensor(heads(Y[:, i, :], 8), heads(XT1[:, i, :], 8), spread(rowcol[:, 8:16], 8, HD), ALU.mult)
                for n, (i, d, tile) in enumerate(ssd_steps):
                    m = n - 4
                    if n >= 4:
                        if m >= 2:
                            dve.wait_ge(s_yd, 2 * (m - 1))
                        dve.tensor_tensor(heads(XD[:, m % 2, :], 8), heads(XT1[:, tile, :], 8), spread(hcol(DTC, tile, d), 8, HD), ALU.mult).then_inc(s_xd, 1)
                        dve.wait_ge(s_cb, m + 1)
                        for g in range(2):
                            q = 2 * m + g
                            dve.wait_ge(s_lx, q + 1)
                            if m >= 1:
                                dve.wait_ge(s_yd, 2 * (m - 1) + g + 1)
                            dve.tensor_tensor(heads(MT[:, g, :], 4), heads(LT[:, q % 2, :], 4),
                                              quad(4)[:, g:g + 1, :].to_broadcast([P, 4, P]), ALU.mult).then_inc(s_mt, 1)
                        dve.wait_ge(s_yo, m + 1)
                        link(dve.tensor_tensor(heads(yt, 8), heads(bank[5][:, :], 8), spread(hcol(EAC, tile, d), 8, HD), ALU.mult))
                        link(dve.tensor_tensor(Y[:, tile, :], Y[:, tile, :], yt, ALU.add))
                        dve.wait_ge(s_yd, 2 * m + 2)
                        dve.tensor_tensor(Y[:, tile, :], Y[:, tile, :], bank[6][:, :], ALU.add).then_inc(s_yv, 1)
                        dve.wait_ge(s_yv, m + 1)
                    if n < 6:
                        dve.wait_ge(s_st, n + 1)
                        dve.wait_ge(s_hd, n + 1)
                        dve.tensor_tensor(H[:, d, :], H[:, d, :], bank[2 + n % 2][:, :], ALU.add).then_inc(s_h, 1)

        ysq, zs1, yr = cut(21120, 4, 256), cut(22144, 2, 512), small[:, 96:100]
        s_wo1 = [sem(f"l1_out_w{i}") for i in range(4)]
        wo1, wo1h = cut(8192, KD, D), cut(20576, KD, D)
        s_zs1, s_ys, s_yr, s_yn, s_yt1 = (sem(f"sgn_{x}") for x in ("silu_z", "sums", "rms", "normed", "turned"))
        with nc.Block() as block:
            @block.sync
            def _(sp):
                load_out_weights(sp, t["od_w_out"].rearrange("(k p) n -> p k n", p=P), wo1, s_wo1)

            @block.scalar
            def _(act):
                act.activation(zs1, Z1, ACT.Silu).then_inc(s_zs1, 1)

            @block.vector
            def _(dve):
                link = linker(dve, "dve")
                dve.wait_ge(s_zs1, 1)
                link(dve.tensor_tensor(Y, Y, zs1, ALU.mult))
                y4 = Y.rearrange("p t (g n) -> p (t g) n", g=2)
                link(dve.tensor_tensor(ysq, y4, y4, ALU.mult))
                dve.tensor_reduce(yr, ysq, AX.X, ALU.add).then_inc(s_ys, 1)
                dve.wait_ge(s_yr, 1)
                dve.tensor_tensor(y4, y4, spread(yr, 4, 256), ALU.mult).then_inc(s_yn, 1)
                for c in range(4):
                    dve.wait_ge(s_yt1, c + 1)
                    dve.tensor_scalar(catT[:, 4 + c, 0:LAT], bank[c][:, 0:LAT], SSDNORM(c), None, ALU.mult)

            @block.gpsimd
            def _(pool):
                link = linker(pool, "pool")
                pool.wait_ge(s_ys, 1)
                link(pool.tensor_scalar(yr, yr, 1.0 / 256, EPS, ALU.mult, ALU.add))
                pool.tensor_tensor(yr, yr, mhalf[:, 0:4], ALU.pow).then_inc(s_yr, 1)

            @block.tensor
            def _(pe):
                pe.wait_ge(s_yn, 1)
                for c in range(4):
                    for i in range(2):
                        mm = pe.transpose(bank[c][:, i * P:i * P + P], Y[:, i, c * P:c * P + P], ident)
                    mm.then_inc(s_yt1, 1)

        project_and_add("l1_out", 2, 2, 2, s_wo1, wo1, wo1h)

        xn1 = cut(0, 2, D)
        norm_to_hT("l1_ffn", 1, 1, range(2), xn1, split=False)
        wr = cut(2048, KD, E)
        sm = small[:, 128:640]
        lg, top, gw = sm[:, 0:16], sm[:, 16:32], sm[:, 48:64]
        sel, pos, oh = sm[:, 64:80], sm[:, 80:96], sm[:, 96:128]
        ix = sb("expert_index", [P, 16], U32)
        ixf, ee, tot = sm[:, 128:144], sm[:, 144:160], sm[:, 160:176]
        most = sb("most_tokens", [1, 1], mybir.dt.int32)
        s_wr, s_lg, s_lv, s_e1, s_cp1, s_ps = (sem(f"route_{x}") for x in ("w", "logits", "picked", "exp", "selected", "positions"))
        with nc.Block() as block:
            @block.sync
            def _(sp):
                sp.dma_start(wr, t["moe_router"].rearrange("(k p) e -> p k e", p=P)).then_inc(s_wr, 16)

            @block.tensor
            def _(pe):
                pe.wait_ge(s_wr, 16)
                for i in range(2):
                    for k in range(KD):
                        mm = pe.matmul(bank[0][:, 8 * i:8 * i + 8], hT[:, k, i * P:i * P + P], wr[:, k, :], start=(k == 0), stop=(k == KD - 1))
                mm.then_inc(s_lg, 1)
                pe.wait_ge(s_cp1, 1)
                pe.matmul(bank[1][:, 0:8], cst("before"), sel[:, 0:8], start=True, stop=True)
                pe.matmul(bank[1][:, 8:16], cst("before"), sel[:, 8:16], start=True, stop=False)
                pe.matmul(bank[1][:, 8:16], ones, sel[:, 0:8], start=False, stop=True)
                pe.matmul(bank[1][:, 16:24], ones, sel[:, 0:8], start=True, stop=False)
                pe.matmul(bank[1][:, 16:24], ones, sel[:, 8:16], start=False, stop=True).then_inc(s_ps, 1)

            @block.scalar
            def _(act):
                act.wait_ge(s_lv, 1)
                act.activation(ee[:, 0:2], ee[:, 0:2], ACT.Exp).then_inc(s_e1, 1)

            @block.vector
            def _(dve):
                link = linker(dve, "dve")
                dve.wait_ge(s_lg, 1)
                link(dve.tensor_copy(lg, bank[0][:, 0:16]))
                for i in range(2):
                    a = slice(8 * i, 8 * i + 8)
                    link(dve.max(top[:, a], lg[:, a]))
                    link(dve.max_index(ix[:, a], top[:, a], lg[:, a]))
                link(dve.tensor_copy(ixf, ix[:, :]))
                for i in range(2):
                    ins = dve.tensor_tensor(ee[:, i:i + 1], top[:, 8 * i + 1:8 * i + 2], top[:, 8 * i:8 * i + 1], ALU.subtract)
                ins.then_inc(s_lv, 1)
                dve.wait_ge(s_e1, 1)
                link(dve.tensor_scalar(ee[:, 2:4], ee[:, 0:2], 1.0, None, ALU.add))
                link(dve.reciprocal(ee[:, 4:6], ee[:, 2:4]))
                link(dve.tensor_tensor(ee[:, 6:8], ee[:, 4:6], ee[:, 0:2], ALU.mult))
                for i in range(2):
                    a = slice(8 * i, 8 * i + 8)
                    io = cst("iota")[:, 0:8]
                    link(dve.tensor_scalar(oh[:, 0:8], io, ixf[:, 8 * i:8 * i + 1], None, ALU.is_equal))
                    link(dve.tensor_scalar(oh[:, 8:16], io, ixf[:, 8 * i + 1:8 * i + 2], None, ALU.is_equal))
                    link(dve.tensor_tensor(sel[:, a], oh[:, 0:8], oh[:, 8:16], ALU.add))
                    link(dve.tensor_scalar(oh[:, 16:24], oh[:, 8:16], ee[:, 6 + i:7 + i], None, ALU.mult))
                    link(dve.scalar_tensor_tensor(gw[:, a], oh[:, 0:8], ee[:, 4 + i:5 + i], oh[:, 16:24], ALU.mult, ALU.add))
                dve.sem_inc(s_cp1, 1)
                dve.wait_ge(s_ps, 1)
                dve.tensor_copy(pos, bank[1][:, 0:16])
                link(dve.tensor_reduce(tot[:, 0:1], bank[1][:, 16:24], AX.X, ALU.max))
                dve.tensor_copy(most[:, :], tot[0:1, 0:1])

        NB = FE // 512
        RAW = [cut(4096 + s * 4096, 2048) for s in range(6)]
        HIGH = [cut(4096 + s * 4096 + 2048, 2048) for s in range(6)]

        def half_view(v, kind):
            return v.rearrange("p (k f) -> p k f", k=4) if kind < 2 else v.rearrange("p (j n) -> p j n", j=2)

        xh = [cut(2048 + q * 1024, KD, P) for q in range(2)]
        xl = [G[:, 4 + q, :].rearrange("p (k s) -> p k s", k=KD) for q in range(2)]
        disp = X[:, 2:4, :].rearrange("p a (e i s) -> p (a e) i s", i=2, s=P)
        back = catT[:, 0:4, :].rearrange("p a (e n) -> p (a e) n", n=LAT)
        backs = catT[:, 4, :].rearrange("p (q n) -> p q n", q=2)
        weighted = hT[:, 0:4, :].rearrange("p a (e i s) -> p (a e) i s", i=2, s=P)
        silu_h, prod, prodTh, prodTl = hT[:, 0:2, :], hT[:, 2:4, :], hT[:, 4:6, :], catT[:, 5:7, :]
        ysb = hT[:, 6:8, :].rearrange("p a b -> p (a b)")
        ACC = G[:, 0:2, :]
        w1e = t["moe_w1"].rearrange("e (k p) f -> p e k f", p=P)
        w3e = t["moe_w3"].rearrange("e (k p) f -> p e k f", p=P)
        w2e = t["moe_w2"].rearrange("e (j p) n -> p e j n", p=P)

        def at(e, times, add):
            return times * e + add if isinstance(e, int) else 2 * times * e[0] + (times * e[1] + add)

        def parity(e):
            return (e if isinstance(e, int) else e[1]) % 2

        def at_expert(v, e, shift=0):
            return v[:, bass.ds(at(e, 1, shift), 1)] if not isinstance(e, int) else v[:, e + shift:e + shift + 1]

        def over_experts(eng, body):
            body(0)
            with eng.Fori(0, E // 2 - 1) as p:
                body((p, 1))
                body((p, 2))
            body(E - 1)

        def misc_before(e, add=0):
            return 2 + add if e == 0 and isinstance(e, int) else at(e, 13, add - 3)

        def splits_before(e, add=0):
            return 2 + add if e == 0 and isinstance(e, int) else at(e, 9, add + 1)

        def misc_bank(e, i):
            return 4 + (i if isinstance(e, int) and e == 0 else parity(e) + 1 + i) % 2

        def pieces(c, first, last):
            return ([("scatter", c - 1)] if 1 <= c <= 4 and not first else []) + ([("gather", c - 4)] if c in (4, 5) and not last else [])

        def experts(r):
            tag = f"moe{r}"
            chain[tag] = [sem(f"{tag}_chain"), 0]
            s_dp, s_dt, s_dc = sem(f"{tag}_dispatch"), sem(f"{tag}_turned"), sem(f"{tag}_turned_copied")
            s_w = [sem(f"{tag}_w_{i}") for i in range(6)]
            s_hi = [sem(f"{tag}_high_{i}") for i in range(3)]
            s_lo = [sem(f"{tag}_low_{i}") for i in range(3)]
            s_used = [sem(f"{tag}_used_{i}") for i in range(3)]
            s_sl, s_pr, s_ms, s_mh, s_mf, s_yc, s_bk = (sem(f"{tag}_{x}") for x in
                ("silu", "gated", "misc", "misc_high", "misc_free", "y_copied", "back_copied"))
            s_vx = sem(f"{tag}_gathered_value")

            def load(sp, kind, e, c):
                src = at_expert((w1e, w3e, w2e)[kind], e).rearrange("p a k f -> p (a k) f")
                for h in range(2):
                    part = src[:, 4 * h:4 * h + 4, c * 512:c * 512 + 512] if kind < 2 else src[:, 4 * c + 2 * h:4 * c + 2 * h + 2, :]
                    s = 2 * kind + h
                    if not (isinstance(e, int) and NB * e + c == 0):
                        sp.wait_ge(s_used[kind], at(e, 2 * NB, 2 * c + h - 1))
                    sp.dma_start(half_view(RAW[s], kind), part).then_inc(s_w[s], 16)

            with nc.Block() as block:
                @block.sync
                def _(sp):
                    for kind in range(3):
                        load(sp, kind, 0, 0)

                @block.vector
                def _(dve):
                    link = linker(dve, tag)
                    if r == 0:
                        dve.memset(ACC, 0.0)
                    else:
                        link(dve.tensor_scalar(pos, pos, float(P), None, ALU.subtract))
                    for e in range(E):
                        for i in range(2):
                            a = slice(8 * i + e, 8 * i + e + 1)
                            link(dve.tensor_scalar(disp[:, e, i, :], cst("iota"), pos[:, a], sel[:, a], ALU.is_equal, ALU.mult))
                            dve.tensor_scalar(weighted[:, e, i, :], disp[:, e, i, :], gw[:, a], None, ALU.mult).then_inc(s_dp, 1)
                    for b in range(4):
                        dve.wait_ge(s_dt, b + 1)
                        dve.tensor_copy(back[:, 2 * b:2 * b + 2, :], bank[b][:, :].rearrange("p (e n) -> p e n", e=2)).then_inc(s_dc, 1)

                @block.tensor
                def _(pe):
                    for b in range(4):
                        pe.wait_ge(s_dp, 4 * b + 4)
                        for x in range(4):
                            mm = pe.transpose(quad(b)[:, x, :], weighted[:, 2 * b + x // 2, x % 2, :], ident)
                        mm.then_inc(s_dt, 1)

                @block.scalar
                def _(act):
                    pass

                @block.gpsimd
                def _(pool):
                    pass

            with nc.Block() as block:
                @block.sync
                def _(sp):
                    def body(e):
                        first = isinstance(e, int) and e == 0
                        for c in range(1 if first else 0, NB):
                            load(sp, 0, e, c)
                            load(sp, 1, e, c)
                            if c:
                                if not (first and c == 1):
                                    load(sp, 2, e, c - 1)
                            else:
                                load(sp, 2, e - 1 if isinstance(e, int) else (e[0], e[1] - 1), NB - 1)
                    over_experts(sp, body)
                    load(sp, 2, E - 1, NB - 1)

                @block.tensor
                def _(pe):
                    def up(e, c, kind, out_bank):
                        q = parity(e)
                        for h in range(2):
                            s = 2 * kind + h
                            pe.wait_ge(s_lo[kind], at(e, 2 * NB, 2 * c + h + 1))
                            wh, wl = rounded(half_view(HIGH[s], kind)), rounded(half_view(RAW[s], kind))
                            for k in range(4):
                                kk = 4 * h + k
                                hi, lo = rounded(xh[q][:, kk, :]), rounded(xl[q][:, kk, :])
                                pe.matmul(out_bank, hi, wh[:, k, :], start=(kk == 0), stop=False)
                                pe.matmul(out_bank, hi, wl[:, k, :], start=False, stop=False)
                                mm = pe.matmul(out_bank, lo, wh[:, k, :], start=False, stop=(kk == KD - 1))
                            mm.then_inc(s_used[kind], 1)

                    def misc(e, i):
                        if not (isinstance(e, int) and e == 0 and i < 0):
                            pe.wait_ge(s_mf, misc_before(e, i - 1))
                        return misc_bank(e, i)

                    def turn(e, i, n):
                        b = misc(e, i)
                        pe.wait_ge(s_pr, at(e, NB, n + 1))
                        for j in range(4):
                            mm = pe.transpose(quad(b)[:, j, :], prod[:, (parity(e) + n) % 2, j * P:j * P + P], ident)
                        mm.then_inc(s_ms, 1)

                    def down(e, i, n):
                        c = n % NB
                        if c == 0 and not (isinstance(e, int) and e == 0):
                            pe.wait_ge(s_yc, at(e, 1, 0))
                        pe.wait_ge(s_mf, misc_before(e, i + 1))
                        for h in range(2):
                            pe.wait_ge(s_lo[2], at(e, 2 * NB, 2 * n + h + 1))
                            wh, wl = rounded(half_view(HIGH[4 + h], 2)), rounded(half_view(RAW[4 + h], 2))
                            for j in range(2):
                                jj = 2 * h + j
                                x = slice(jj * P, jj * P + P)
                                hi = rounded(prodTh[:, (parity(e) + n) % 2, x])
                                lo = rounded(prodTl[:, (parity(e) + n) % 2, x])
                                st, sp_ = c == 0 and jj == 0, c == NB - 1 and jj == 3
                                for half in range(2):
                                    o = slice(half * 512, half * 512 + 512)
                                    pe.matmul(bank[6 + half][:, :], hi, wh[:, j, o], start=st, stop=False)
                                    pe.matmul(bank[6 + half][:, :], hi, wl[:, j, o], start=False, stop=False)
                                    mm = pe.matmul(bank[6 + half][:, :], lo, wh[:, j, o], start=False, stop=sp_)
                            mm.then_inc(s_used[2], 1)

                    def gather(e, i, g, shift):
                        b = misc(e, i)
                        for k in range(4):
                            for tile in range(2):
                                sl_ = at_expert(disp, e, shift)[:, :, tile, :].rearrange("p a s -> p (a s)")
                                mm = pe.matmul(quad(b)[:, k, :], xn1[:, tile, (4 * g + k) * P:(4 * g + k + 1) * P], sl_, start=(tile == 0), stop=(tile == 1))
                        mm.then_inc(s_ms, 1)

                    def scatter(e, i, x, q):
                        b = misc(e, i)
                        pe.matmul(bank[b][:, :], backs[:, q, (x // 2) * P:(x // 2) * P + P], ysb[:, (x % 2) * 512:(x % 2) * 512 + 512],
                                  start=True, stop=True).then_inc(s_ms, 1)

                    def body(e):
                        first, last = isinstance(e, int) and e == 0, isinstance(e, int) and e == E - 1
                        i = 0
                        pe.wait_ge(s_mf, 2 if first else misc_before(e, 0))
                        for c in range(NB):
                            lagged = not (first and c == 0)
                            if not (first and c < 2):
                                pe.wait_ge(s_sl, at(e, NB, c - 1))
                            up(e, c, 0, bank[(parity(e) + c) % 2][:, :])
                            if lagged:
                                turn(e, i, c - 1)
                                i += 1
                            if not (first and c < 2):
                                pe.wait_ge(s_pr, at(e, NB, c - 1))
                            up(e, c, 1, bank[2 + (parity(e) + c) % 2][:, :])
                            i_turn = i - 1
                            for kind, x in pieces(c, first, last):
                                if kind == "scatter":
                                    if x == 0:
                                        pe.wait_ge(s_yc, at(e, 1, 0))
                                        pe.wait_ge(s_bk, at(e, 1, 0))
                                    scatter(e, i, x, 1 - parity(e))
                                else:
                                    gather(e, i, x, 1)
                                i += 1
                            if lagged:
                                down(e, i_turn, c - 1)
                    for g in range(2):
                        gather(0, g - 2, g, 0)
                    over_experts(pe, body)
                    turn(E - 1, NB + 4, NB - 1)
                    down(E - 1, NB + 4, NB - 1)
                    pe.wait_ge(s_yc, E)
                    pe.wait_ge(s_bk, E)
                    for x in range(4):
                        scatter(E - 1, NB + 5 + x, x, (E - 1) % 2)

                @block.scalar
                def _(act):
                    shift, scale = modc[:, 1, 2, :, 0], modc[:, 1, 3, :, 0]

                    def high_weights(kind, e, n):
                        for h in range(2):
                            s = 2 * kind + h
                            act.wait_ge(s_w[s], at(e, 16 * NB, 16 * (n + 1)))
                            high(act, HIGH[s], RAW[s]).then_inc(s_hi[kind], 1)

                    def turned_high(e, i, n):
                        act.wait_ge(s_ms, misc_before(e, i + 1))
                        if not (isinstance(e, int) and NB * e + n < 2):
                            act.wait_ge(s_used[2], at(e, 2 * NB, 2 * n - 2))
                        act.activation(rounded(prodTh[:, (parity(e) + n) % 2, :]), bank[misc_bank(e, i)][:, :], ACT.Copy).then_inc(s_mh, 1)

                    def gathered(e, i, g, q, before):
                        act.wait_ge(s_ms, misc_before(e, i + 1))
                        for k in range(4):
                            kk = 4 * g + k
                            ins = act.activation(xl[q][:, kk, :], quad(misc_bank(e, i))[:, k, :], ACT.Identity,
                                                 bias=shift[:, kk:kk + 1], scale=scale[:, kk:kk + 1])
                        ins.then_inc(s_vx, 1)
                        act.wait_ge(s_vx, before + 1)
                        act.activation(rounded(xh[q][:, 4 * g:4 * g + 4, :]), xl[q][:, 4 * g:4 * g + 4, :], ACT.Copy).then_inc(s_mh, 1)

                    def copy_y(e):
                        act.wait_ge(s_used[2], at(e, 2 * NB, 0))
                        for half in range(2):
                            ins = act.activation(ysb[:, half * 512:half * 512 + 512], bank[6 + half][:, :], ACT.Copy)
                        ins.then_inc(s_yc, 1)

                    def body(e):
                        first, last = isinstance(e, int) and e == 0, isinstance(e, int) and e == E - 1
                        i = 0
                        for c in range(NB):
                            if not (first and c == 0):
                                turned_high(e, i, c - 1)
                                i += 1
                            act.wait_ge(s_used[0], at(e, 2 * NB, 2 * c + 2))
                            if not (first and c < 2):
                                act.wait_ge(s_pr, at(e, NB, c - 1))
                            act.activation(silu_h[:, (parity(e) + c) % 2, :], bank[(parity(e) + c) % 2][:, :], ACT.Silu).then_inc(s_sl, 1)
                            if not (last and c == NB - 1):
                                high_weights(0, e, c + 1)
                                high_weights(1, e, c + 1)
                            if c == 0 and not first:
                                copy_y(e)
                            for kind, x in pieces(c, first, last):
                                if kind == "gather":
                                    gathered(e, i, x, 1 - parity(e), at(e, 2, 2 + x))
                                i += 1
                            high_weights(2, e, c)
                    high_weights(0, 0, 0)
                    high_weights(1, 0, 0)
                    for g in range(2):
                        gathered(0, g - 2, g, 0, g)
                    over_experts(act, body)
                    turned_high(E - 1, NB + 4, NB - 1)
                    copy_y(E)

                @block.gpsimd
                def _(pool):
                    def body(e):
                        if not (isinstance(e, int) and e == 0):
                            pool.wait_ge(s_ms, at(e, 13, -7))
                        pool.tensor_copy(backs[:, parity(e), :], at_expert(back, e).rearrange("p a n -> p (a n)")).then_inc(s_bk, 1)
                    over_experts(pool, body)

                @block.vector
                def _(dve):
                    def low_weights(kind, e, n):
                        for h in range(2):
                            s = 2 * kind + h
                            dve.wait_ge(s_hi[kind], at(e, 2 * NB, 2 * n + h + 1))
                            low(dve, RAW[s], HIGH[s]).then_inc(s_lo[kind], 1)

                    def gathered(e, j, g, q):
                        dve.wait_ge(s_mh, splits_before(e, j + 1))
                        v = slice(4 * g, 4 * g + 4)
                        low(dve, xl[q][:, v, :], xh[q][:, v, :]).then_inc(s_mf, 1)

                    def turned_low(e, i, j, n):
                        dve.wait_ge(s_mh, splits_before(e, j + 1))
                        x = (parity(e) + n) % 2
                        dve.tensor_tensor(rounded(prodTl[:, x, :]), bank[misc_bank(e, i)][:, :], rounded(prodTh[:, x, :]).bitcast(F32), ALU.subtract).then_inc(s_mf, 1)

                    def add_scattered(e, i, x):
                        dve.wait_ge(s_mf, misc_before(e, i))
                        dve.wait_ge(s_ms, misc_before(e, i + 1))
                        a = ACC[:, x // 2, (x % 2) * 512:(x % 2) * 512 + 512]
                        dve.tensor_tensor(a, a, bank[misc_bank(e, i)][:, :], ALU.add).then_inc(s_mf, 1)

                    def body(e):
                        first, last = isinstance(e, int) and e == 0, isinstance(e, int) and e == E - 1
                        i = j = 0
                        for c in range(NB):
                            if not (first and c == 0):
                                turned_low(e, i, j, c - 1)
                                i, j = i + 1, j + 1
                            more = not (last and c == NB - 1)
                            if more:
                                low_weights(0, e, c + 1)
                            dve.wait_ge(s_sl, at(e, NB, c + 1))
                            dve.wait_ge(s_used[1], at(e, 2 * NB, 2 * c + 2))
                            x = (parity(e) + c) % 2
                            dve.tensor_tensor(prod[:, x, :], silu_h[:, x, :], bank[2 + x][:, :], ALU.mult).then_inc(s_pr, 1)
                            if more:
                                low_weights(1, e, c + 1)
                            for kind, x in pieces(c, first, last):
                                if kind == "scatter":
                                    add_scattered(e, i, x)
                                else:
                                    gathered(e, j, x, 1 - parity(e))
                                    j += 1
                                i += 1
                            low_weights(2, e, c)
                    low_weights(0, 0, 0)
                    low_weights(1, 0, 0)
                    for g in range(2):
                        gathered(0, g - 2, g, 0)
                    over_experts(dve, body)
                    turned_low(E - 1, NB + 4, NB, NB - 1)
                    for x in range(4):
                        add_scattered(E - 1, NB + 5 + x, x)

        experts(0)
        full = nc.values_load(most[0:1, 0:1], engines=mybir.ALL_ENGINES, min_val=0, max_val=LAT)
        with nc.If(full > P):
            experts(1)

        s_fs, s_fr, s_fx, s_out = (sem(f"end_{x}") for x in ("squares", "rms", "residual", "stored"))
        fs, tmp = small[:, 0:2], xn1
        with nc.Block() as block:
            @block.scalar
            def _(act):
                for i in range(2):
                    act.activation(cut(4096, 2, D)[:, i, :], ACC[:, i, :], ACT.Square, accum_out=fs[:, i:i + 1]).then_inc(s_fs, 1)

            @block.gpsimd
            def _(pool):
                link = linker(pool, "pool")
                pool.wait_ge(s_fs, 2)
                link(pool.tensor_scalar(fs, fs, 1.0 / D, EPS, ALU.mult, ALU.add))
                pool.tensor_tensor(fs, fs, mhalf[:, 0:2], ALU.pow).then_inc(s_fr, 1)

            @block.vector
            def _(dve):
                link = linker(dve, "dve")
                dve.wait_ge(s_fr, 1)
                for i in range(2):
                    link(dve.scalar_tensor_tensor(tmp[:, i, :], ACC[:, i, :], fs[:, i:i + 1], G[:, 3, :], ALU.mult, ALU.mult))
                    dve.tensor_tensor(X[:, i, :], X[:, i, :], tmp[:, i, :], ALU.add).then_inc(s_fx, 1)

            @block.sync
            def _(sp):
                for i in range(2):
                    sp.wait_ge(s_fx, i + 1)
                    sp.dma_start(out.rearrange("(t p) d -> p t d", p=P)[:, i, :], X[:, i, :]).then_inc(s_out, 16)
                sp.wait_ge(s_out, 32)


def shape_constants():
    import numpy as np
    c = {n: np.zeros((P, w), np.float32) for n, (_, w) in CONST.items()}
    r = np.arange(P)
    c["ident"][r, r] = 1
    c["cum0"][:] = r[:, None] <= r[None, :]
    c["cum1"][:] = r[:, None] >= r[None, :]
    c["ones"][:] = 1
    c["neg0"][:] = np.where(r[None, :] >= r[:, None], 0, -30000)
    c["neg1"][:] = np.where(r[None, :] <= r[:, None], 0, -30000)
    k = np.arange(LAT)
    for i in range(2):
        c["band"][:, i * LAT:(i + 1) * LAT] = np.where(np.abs(k[None, :] - (r[:, None] + P * i)) <= 128, 0, -1e30)
    q = r % 64
    start = np.clip(q - 8, 0, 48)[:, None]
    k = np.arange(64)[None, :]
    c["natcol"][:] = np.where((k >= start) & (k < start + 16), 0, -1e30)
    half = 16
    freqs = (10000.0 ** (-np.arange(half, dtype=np.float32) / np.float32(half))).astype(np.float32)
    pos = np.arange(LAT)
    for p in range(P):
        dd = p % 64
        at = (pos // 64 if dd < 32 else pos % 64).astype(np.float32)
        ang = (at * freqs[dd % 16]).astype(np.float32)
        c["cos"][p], c["sin"][p] = np.cos(ang), np.sin(ang)
        if dd % 32 < 16:
            c["rot"][p + 16, p] = -1
        else:
            c["rot"][p - 16, p] = 1
    c["iota"][:] = r[None, :]
    c["before"][:] = r[:, None] < r[None, :]
    c["pick"][0, 0:P] = 1
    c["pick"][1, P:2 * P] = 1
    levels = np.zeros((P, 2, LEVELS, P), np.float32)
    for l in range(LEVELS):
        b = 1 << l
        same = r[:, None] // (2 * b) == r[None, :] // (2 * b)
        levels[:, 0, l, :] = same & (r[:, None] // b < r[None, :] // b)
        levels[:, 1, l, :] = same & (r[:, None] // b > r[None, :] // b)
    return np.concatenate([c[n] for n in CONST], axis=1), levels


def nat_bias_places():
    import numpy as np
    q = np.arange(LAT)
    dr = np.arange(4)[None, :, None] - (q // 64)[:, None, None] + 7
    dc = np.clip(np.arange(64)[None, None, :] - (q % 64)[:, None, None] + 15, 0, 30)
    return (dr * 31 + dc).reshape(LAT, LAT)


def kernel(**inputs):
    import numpy as np
    import concourse.bacc as bacc
    from concourse.bass_utils import run_bass_kernel_spmd as run

    a = {k: np.ascontiguousarray(v) for k, v in inputs.items()}
    const, levels = shape_constants()
    rpb = a["na_rpb"][0].reshape(8, 15 * 31)[:, nat_bias_places()]
    arrays = {
        "x": a["x"][0], "ctx": a["ctx"][0], "c": a["c"], "c_ctx": a["c_ctx"][None, :],
        "ada_w": a["ada_w"], "ada_b": a["ada_b"], "norm_w": a["norm_w"],
        "ev_w_in": a["ev_w_in"][0], "ev_w_out": a["ev_w_out"][0],
        "nat_bias": rpb.reshape(8, 2, P, LAT).transpose(2, 1, 0, 3),
        "dn_conv": a["dn_conv"][0], "dn_a_log": a["dn_a_log"].reshape(8, 1), "dn_dt_bias": a["dn_dt_bias"].reshape(8, 1), "dn_norm": a["dn_norm"],
        "ffn_w1": a["ffn_w1"][0], "ffn_w3": a["ffn_w3"][0], "ffn_w2": a["ffn_w2"][0],
        "od_w_in": a["od_w_in"][0], "od_w_out": a["od_w_out"][0], "wa_sink": a["wa_sink"],
        "ssd_conv": a["ssd_conv"][0], "ssd_a_log": a["ssd_a_log"].reshape(16, 1), "ssd_dt_bias": a["ssd_dt_bias"].reshape(16, 1),
        "ssd_d": a["ssd_d"], "ssd_norm": a["ssd_norm"],
        "moe_router": a["moe_router"][0], "moe_w1": a["moe_w1"][0], "moe_w3": a["moe_w3"][0], "moe_w2": a["moe_w2"][0],
        "const": const, "levels": levels,
    }
    pairs = np.arange(8).reshape(2, 4).T.ravel()
    for name, axis in (("od_w_in", 1), ("od_w_out", 0)):
        w = arrays[name] if axis == 0 else arrays[name].T
        heads = w[:512].reshape(8, HD, -1)[pairs].reshape(512, -1)
        w = np.concatenate([heads, w[512:]])
        arrays[name] = w if axis == 0 else w.T
    arrays = {f"in_{k}": np.ascontiguousarray(v) for k, v in arrays.items()}
    nc = bacc.Bacc("TRN2", target_bir_lowering=False, num_devices=1)
    t = {k[3:]: nc.dram_tensor(k, v.shape, mybir.dt.from_np(v.dtype), kind="ExternalInput").ap() for k, v in arrays.items()}
    out = nc.dram_tensor("out", (LAT, D), F32, kind="ExternalOutput").ap()
    build(nc, t, out)
    got = run(nc, [arrays], core_ids=[0])
    return got.results[0]["out"].reshape(1, LAT, D)
```

```python
from contextlib import ExitStack

import concourse.bass as bass
from concourse import mybir

F32 = mybir.dt.float32
F32R = mybir.dt.float32r
U32 = mybir.dt.uint32
ALU = mybir.AluOpType
ACT = mybir.ActivationFunctionType
AX = mybir.AxisListType

P = 128
D = 1024
KD = D // P
LAT, CTX = 256, 256
T = 4
NTOK = LAT + CTX
HD = 64
FF = 2816
NF = FF // P
E, FE = 8, 3584
EPS = 1e-6
TAPS = 5
LEVELS = 7
CHUNK_ORDER = ((2, 3, 0, 1), (3, 2, 1, 0))

CONST = {}
_at = 0
for _n, _w in (("ident", P), ("cum0", P), ("cum1", P), ("ones", P), ("neg0", P), ("neg1", P), ("band", 2 * LAT),
               ("natcol", 64), ("cos", LAT), ("sin", LAT), ("rot", P), ("iota", P), ("before", P), ("eighth", 16)):
    CONST[_n] = (_at, _w)
    _at += _w
NCONST = _at


def build(nc, t, out):
    with ExitStack() as ctx:
        def sb(name, shape, dt=F32):
            return ctx.enter_context(nc.sbuf_tensor(name, shape, dt))

        twins = {}

        def sb_split(name, width, shape=None, parts=None):
            at = (nc.sbuf_base + 31) // 32 * 32
            v = sb(name, shape or [P, width])
            ends = parts or [width]
            twins[v.name] = (width, [(a, b, nc.alloc_sbuf_tensor_at(f"{name}_r{a}", [P, b - a], F32R, offset=at + 4 * a))
                                     for a, b in zip([0] + ends, ends)])
            return v

        def rounded(v):
            width, parts = twins[v.tensor.name]
            for a, b, twin in parts:
                if a <= v.offset < b:
                    return bass.AP(tensor=twin, offset=v.offset - a, ap=[[b - a, v.ap[0][1]]] + [list(x) for x in v.ap][1:])

        stage_sems = []

        def sem(name):
            s = nc.alloc_semaphore(name=name)
            stage_sems.append(s)
            return s

        bank = [ctx.enter_context(nc.psum_tensor(f"bank{i}", [P, 512], F32)) for i in range(8)]

        def quad(i):
            return bank[i][:, :].rearrange("p (a b) -> p a b", a=4)

        X = sb("residual", [P, T, D])
        C = sb("const", [P, NCONST])
        G = sb_split("gate_rows", 6 * D, [P, 6, D])
        cols = sb("channel_cols", [P, 2, P])
        modc = sb("mod_cols", [P, 2, 4, KD, 2])
        hT = sb_split("hT", KD * NTOK, [P, KD, NTOK])
        catT = sb_split("catT", KD * NTOK, [P, KD, NTOK])
        ar = sb_split("arena", 28768, parts=[8192, 16384, 28768])
        small = sb_split("small", 640)
        mhalf = sb("minus_half", [P, 64])
        gbias = sb("gate_bias", [16, 8])
        rowcol = sb("per_head_rows", [P, 16])

        def cst(name):
            a, w = CONST[name]
            return C[:, a:a + w]

        ident, ones = cst("ident"), cst("ones")
        cum, neg = (cst("cum0"), cst("cum1")), (cst("neg0"), cst("neg1"))

        def cut(at, *shape):
            n = 1
            for s in shape:
                n *= s
            v = ar[:, at:at + n]
            if len(shape) == 1:
                return v
            names = "abcd"[:len(shape)]
            return v.rearrange(f"p ({' '.join(names)}) -> p {' '.join(names)}", **dict(zip(names, shape)))

        chain = {k: [ctx.enter_context(nc.semaphore(f"{k}_chain")), 0] for k in ("act", "dve", "pool")}

        def linker(eng, key):
            def link(ins):
                chain[key][1] += 1
                ins.then_inc(chain[key][0], 1)
                eng.wait_ge(chain[key][0], chain[key][1])
            return link

        def high(act, hi, v):
            return act.activation(rounded(hi), v, ACT.Copy)

        def low(dve, v, hi):
            return dve.tensor_tensor(rounded(v), v, rounded(hi).bitcast(F32), ALU.subtract)

        def split_matmul(pe, acc, x, w, start, stop):
            xh_, xl_, wh_, wl_ = (rounded(v) for v in (*x, *w))
            pe.matmul(acc, xh_, wh_, start=start, stop=False)
            pe.matmul(acc, xh_, wl_, start=False, stop=False)
            return pe.matmul(acc, xl_, wh_, start=False, stop=stop)

        DNCONV = lambda tap, c: cols[:, 0, 64 + tap * 12 + c:65 + tap * 12 + c]
        DNNORM = cols[:, 0, 124:125]
        SSDCONV = lambda tap, c: cols[:, 1, tap * 8 + c:tap * 8 + c + 1]
        SSDNORM = lambda c: cols[:, 1, 40 + c:41 + c]

        NSLOT, NCH = 6, 24
        AW = [cut(i * 2048, 4, 512) for i in range(NSLOT)]
        AWH = ([cut((NSLOT + i) * 2048, 4, 512) for i in range(2)] + [hT[:, 2:6, :]]
               + [G[:, 2 * i:2 * i + 2, :].rearrange("p a (b n) -> p (a b) n", b=2) for i in range(3)])
        ROW = ar[0:2, 16384:16384 + 2 * 6 * D].rearrange("p (l n) -> p l n", l=2)
        flat_row = ROW.rearrange("p l (n w) -> p (l n) w", w=512)
        rows = hT[:, 0:2, 0:P]
        nwr2, nwr = (catT[0:2, a:a + 4, :].rearrange("p a b -> p (a b)") for a in (0, 4))
        scT = small[:, 0:16].rearrange("p (v k) -> p k v", v=2)
        scTh = small[:, 16:32].rearrange("p (v k) -> p k v", v=2)
        s_x, s_const, s_rows, s_nw = sem("x_in"), sem("const_in"), sem("rows_in"), sem("norm_rows_in")
        s_slot = [sem(f"ada_w{i}") for i in range(NSLOT)]
        s_tr, s_trc = sem("rows_transposed"), sem("cols_copied")
        s_sc, s_ah, s_al, s_ada, s_row, s_bias = (sem(x) for x in
            ("silu_c", "ada_high", "ada_low", "ada_used", "ada_row", "ada_bias_in"))
        s_mp, s_mh, s_g_out, s_g_in = sem("mod_transposed"), sem("minus_half_set"), sem("gate_stored"), sem("gate_spread")
        gate_dram = nc.dram_tensor("gate_rows_dram", (2, 2, 2, D), F32, kind="Internal").ap()
        s_mg = sem("gate_times_norm")

        with nc.Block() as block:
            @block.sync
            def _(sp):
                sp.dma_start(C[:, :], t["const"]).then_inc(s_const, 16)
                sp.dma_start(rows[0:64, 0, :], t["norm_w"].rearrange("l i (k p) -> (l i k) p", p=P)).then_inc(s_rows, 16)
                sp.dma_start(rows[64:124, 0, :], t["dn_conv"].rearrange("t (c p) -> (t c) p", p=P)).then_inc(s_rows, 16)
                sp.dma_start(rows[124:125, 0, :], t["dn_norm"]).then_inc(s_rows, 16)
                sp.dma_start(rows[0:40, 1, :], t["ssd_conv"].rearrange("t (c p) -> (t c) p", p=P)).then_inc(s_rows, 16)
                sp.dma_start(rows[40:44, 1, :], t["ssd_norm"].rearrange("a (c p) -> (a c) p", p=P)).then_inc(s_rows, 16)
                sp.dma_start(rows[44:52, 1, :], t["c"].rearrange("a (k p) -> (a k) p", p=P)).then_inc(s_rows, 16)
                sp.dma_start(rows[52:60, 1, :], t["c_ctx"].rearrange("a (k p) -> (a k) p", p=P)).then_inc(s_rows, 16)
                adaw = [t["ada_w"][l].rearrange("(k p) n -> p k n", p=P) for l in range(2)]
                halves = [w.rearrange("p (h k) n -> p h k n", h=2) for w in adaw]

                def load(l, n, h, s):
                    w = slice(n * 512, n * 512 + 512) if isinstance(n, int) else bass.ds(n * 512, 512)
                    sp.dma_start(AW[s], halves[l][:, h, :, w]).then_inc(s_slot[s], 16)
                for s in range(NSLOT):
                    load(0, s // 2, s % 2, s)
                for l in range(2):
                    sp.dma_start(ROW[:, l, :], t["ada_b"][l:l + 1, :].to_broadcast([2, 6 * D])).then_inc(s_bias, 16)
                sp.dma_start(X[:, 0:2, :], t["x"].rearrange("(t p) d -> p t d", p=P)).then_inc(s_x, 16)
                sp.dma_start(X[:, 2:4, :], t["ctx"].rearrange("(t p) d -> p t d", p=P)).then_inc(s_x, 16)
                for l, dst in ((0, nwr), (1, nwr2)):
                    for j, i in enumerate((1, 3)):
                        sp.dma_start(dst[:, j * D:(j + 1) * D], t["norm_w"][l, i:i + 1, :].to_broadcast([2, D])).then_inc(s_nw, 16)
                sp.dma_start(gbias[0:8, 0:1], t["dn_dt_bias"]).then_inc(s_nw, 16)
                sp.dma_start(gbias[0:8, 1:2], t["dn_a_log"]).then_inc(s_nw, 16)
                sp.dma_start(gbias[:, 2:3], t["ssd_dt_bias"]).then_inc(s_nw, 16)
                sp.dma_start(gbias[:, 3:4], t["ssd_a_log"]).then_inc(s_nw, 16)
                sp.dma_start(rowcol[:, 0:8], t["wa_sink"].to_broadcast([P, 8])).then_inc(s_nw, 16)
                sp.dma_start(rowcol[:, 8:16], t["ssd_d"].to_broadcast([P, 8])).then_inc(s_nw, 16)
                for l in range(2):
                    with sp.Fori(max(1, 4 * l), 4 * l + 4) as i:
                        for s in range(NSLOT):
                            sp.wait_ge(s_ada, NSLOT * i + (s + 1 - NSLOT))
                            load(l, 3 * i + (s // 2 - 12 * l), s % 2, s)
                sp.wait_ge(s_mg, 4)
                for l in range(2):
                    for j, part in enumerate((2, 5)):
                        sp.dma_start(gate_dram[l, j], ROW[:, l, part * D:(part + 1) * D]).then_inc(s_g_out, 16)
                sp.wait_ge(s_g_out, 64)
                sp.wait_ge(s_x, 32)

            @block.tensor
            def _(pe):
                pe.wait_ge(s_const, 16)
                pe.wait_ge(s_rows, 112)
                pe.transpose(bank[4][:, 0:125], rows[0:125, 0, :], ident[0:125, 0:125]).then_inc(s_tr, 1)
                pe.transpose(bank[5][:, 0:60], rows[0:60, 1, :], ident[0:60, 0:60]).then_inc(s_tr, 1)
                pe.wait_ge(s_sc, 3)

                def chunk(i, first):
                    for s in range(NSLOT):
                        b, h = divmod(s, 2)
                        if not first and h == 0:
                            pe.wait_ge(s_row, 3 * i + (b - 2))
                        pe.wait_ge(s_al, NSLOT * i + (s + 1))
                        for k in range(4):
                            kk = 4 * h + k
                            mm = split_matmul(pe, bank[b][0:2, :], (scTh[:, kk, :], scT[:, kk, :]), (AWH[s][:, k, :], AW[s][:, k, :]), kk == 0, kk == KD - 1)
                        mm.then_inc(s_ada, 1)
                chunk(0, True)
                with pe.Fori(1, NCH // 3) as i:
                    chunk(i, False)
                pe.wait_ge(s_row, NCH)
                n = 0
                for l in range(2):
                    for j, part in enumerate((0, 1, 3, 4)):
                        for k in range(KD):
                            n += 1
                            a = part * D + k * P
                            mm = pe.transpose(bank[4 + l][:, (j * 8 + k) * 2:(j * 8 + k) * 2 + 2], ROW[:, l, a:a + P], ident[0:2, 0:2])
                    mm.then_inc(s_mp, 1)

            @block.vector
            def _(dve):
                link = linker(dve, "dve")
                dve.memset(mhalf[:, :], -0.5).then_inc(s_mh, 1)
                dve.wait_ge(s_tr, 2)
                dve.tensor_copy(cols[:, 0, 0:125], bank[4][:, 0:125]).then_inc(s_trc, 1)
                dve.tensor_copy(cols[:, 1, 0:60], bank[5][:, 0:60]).then_inc(s_trc, 1)

                dve.wait_ge(s_sc, 2)
                low(dve, scT, scTh).then_inc(s_sc, 1)
                dve.wait_ge(s_bias, 32)

                def add_row(n, used):
                    dve.wait_ge(s_ada, used)
                    dst = flat_row[:, n, :] if isinstance(n, int) else flat_row[:, bass.ds(n, 1), :].rearrange("p a w -> p (a w)")
                    return dst

                def chunk(i, first):
                    for b in range(3):
                        for s in (2 * b, 2 * b + 1):
                            dve.wait_ge(s_ah, NSLOT * i + (s + 1))
                            low(dve, AW[s], AWH[s]).then_inc(s_al, 1)
                        if not (first and b == 0):
                            dst = add_row(3 * i + (b - 1), NSLOT * i + 2 * b)
                            dve.tensor_tensor(dst, dst, bank[(b - 1) % 3][0:2, :], ALU.add).then_inc(s_row, 1)
                chunk(0, True)
                with dve.Fori(1, NCH // 3) as i:
                    chunk(i, False)
                dst = add_row(NCH - 1, 2 * NCH)
                dve.tensor_tensor(dst, dst, bank[2][0:2, :], ALU.add).then_inc(s_row, 1)
                dve.wait_ge(s_row, NCH)
                dve.wait_ge(s_nw, 160)
                for l, w in ((0, nwr), (1, nwr2)):
                    for j, part in enumerate((2, 5)):
                        m = ROW[:, l, part * D:(part + 1) * D]
                        dve.tensor_tensor(m, m, w[:, j * D:(j + 1) * D], ALU.mult).then_inc(s_mg, 1)
                dve.wait_ge(s_mp, 2)
                dve.wait_ge(s_trc, 2)
                for l in range(2):
                    m = bank[4 + l][:, 0:64].rearrange("p (j k v) -> p j k v", j=4, k=KD)
                    for j in range(4):
                        if j % 2 == 0:
                            dve.tensor_copy(modc[:, l, j, :, :], m[:, j, :, :])
                        else:
                            link(dve.tensor_scalar(modc[:, l, j, :, :], m[:, j, :, :], 1.0, None, ALU.add))
                            w = cols[:, 0, (l * 4 + j - 1) * 8:(l * 4 + j) * 8]
                            for v in range(2):
                                dve.tensor_tensor(modc[:, l, j, :, v], modc[:, l, j, :, v], w, ALU.mult)

            @block.scalar
            def _(act):
                act.wait_ge(s_trc, 2)
                act.activation(small[:, 0:16], cols[:, 1, 44:60], ACT.Silu).then_inc(s_sc, 1)
                act.wait_ge(s_sc, 1)
                high(act, small[:, 16:32], small[:, 0:16]).then_inc(s_sc, 1)

                def chunk(i):
                    for s in range(NSLOT):
                        act.wait_ge(s_slot[s], 16 * i + 16)
                        high(act, AWH[s], AW[s]).then_inc(s_ah, 1)
                chunk(0)
                with act.Fori(1, NCH // 3) as i:
                    chunk(i)

        def norm_to_hT(tag, l, which, tiles, xn, split=True, ahead=None):
            n = len(tiles)
            s_sqa, s_sqv, s_r, s_xa, s_xv, s_tp = (sem(f"{tag}_{x}") for x in
                ("squares_act", "squares_dve", "rms", "xn_act", "xn_dve", "transposed"))
            ss, r = small[:, 0:4], small[:, 4:8]
            junk = hT[:, :, :].rearrange("p (t a) b -> p t (a b)", t=4)
            shift, scale = modc[:, l, 2 * which, :, :], modc[:, l, 2 * which + 1, :, :]
            dst = catT if split else hT
            if split:
                s_va, s_vd, s_hh = sem(f"{tag}_modulated_act"), sem(f"{tag}_modulated_dve"), sem(f"{tag}_high")
            with nc.Block() as block:
                if ahead:
                    @block.sync
                    def _(sp):
                        ahead(sp)

                @block.scalar
                def _(act):
                    link = linker(act, "act")
                    for i in range(n - 1):
                        act.activation(junk[:, i, :], X[:, i, :], ACT.Square, accum_out=ss[:, i:i + 1]).then_inc(s_sqa, 1)
                    act.wait_ge(s_r, 1)
                    for i in range(0, n, 2):
                        act.activation(xn[:, i, :], X[:, i, :], ACT.Copy, scale=r[:, i:i + 1]).then_inc(s_xa, 1)
                    for k in range(0, KD, 2):
                        for v in range(n // 2):
                            act.wait_ge(s_tp, 8 * (n - 1) + k + 1)
                            ins = act.activation(dst[:, k, 256 * v:256 * v + 256], bank[k][:, 256 * v:256 * v + 256], ACT.Identity,
                                                 bias=shift[:, k, v:v + 1], scale=scale[:, k, v:v + 1])
                        if split:
                            ins.then_inc(s_va, 1)
                    for k in range(KD if split else 0):
                        act.wait_ge((s_va, s_vd)[k % 2], k // 2 + 1)
                        high(act, hT[:, k, :], catT[:, k, :]).then_inc(s_hh, 1)

                @block.gpsimd
                def _(pool):
                    link = linker(pool, "pool")
                    pool.wait_ge(s_sqa, n - 1)
                    pool.wait_ge(s_sqv, 1)
                    link(pool.tensor_scalar(r[:, 0:n], ss[:, 0:n], 1.0 / D, EPS, ALU.mult, ALU.add))
                    pool.tensor_tensor(r[:, 0:n], r[:, 0:n], mhalf[:, 0:n], ALU.pow).then_inc(s_r, 1)

                @block.vector
                def _(dve):
                    i = n - 1
                    dve.tensor_tensor(junk[:, i, :], X[:, i, :], X[:, i, :], ALU.mult).then_inc(s_xv, 1)
                    dve.wait_ge(s_xv, 1)
                    dve.tensor_reduce(ss[:, i:i + 1], junk[:, i, :], AX.X, ALU.add).then_inc(s_sqv, 1)
                    dve.wait_ge(s_r, 1)
                    for i in range(1, n, 2):
                        dve.tensor_scalar(xn[:, i, :], X[:, i, :], r[:, i:i + 1], None, ALU.mult).then_inc(s_xv, 1)
                    for k in range(1, KD, 2):
                        for v in range(n // 2):
                            dve.wait_ge(s_tp, 8 * (n - 1) + k + 1)
                            ins = dve.tensor_scalar(dst[:, k, 256 * v:256 * v + 256], bank[k][:, 256 * v:256 * v + 256],
                                                    scale[:, k, v:v + 1], shift[:, k, v:v + 1], ALU.mult, ALU.add)
                        if split:
                            ins.then_inc(s_vd, 1)
                    for k in range(KD if split else 0):
                        dve.wait_ge(s_hh, k + 1)
                        low(dve, catT[:, k, :], hT[:, k, :])

                @block.tensor
                def _(pe):
                    for i in range(n):
                        pe.wait_ge(s_xa, i // 2 + 1) if i % 2 == 0 else pe.wait_ge(s_xv, 1 + (i + 1) // 2)
                        for k in range(KD):
                            pe.transpose(bank[k][:, i * P:(i + 1) * P], xn[:, i, k * P:(k + 1) * P], ident).then_inc(s_tp, 1)

        def load_out_weights(sp, src, raw, s_w):
            for g in range(4):
                sp.dma_start(raw[:, 2 * g:2 * g + 2, :], src[:, 2 * g:2 * g + 2, :]).then_inc(s_w[g], 16)

        def project_and_add(tag, n, gate_lat, gate_ctx, s_w, raw, hi):
            s_y, s_ss, s_r, s_h, s_l = (sem(f"{tag}_{x}") for x in ("y", "squares", "rms", "high", "low"))
            ss, r = small[:, 0:8], small[:, 8:16]
            tok = slice(0, n * P)
            with nc.Block() as block:
                @block.tensor
                def _(pe):
                    for i in range(n):
                        for half in range(2):
                            o = slice(half * 512, half * 512 + 512)
                            for k in range(KD):
                                if i == 0:
                                    pe.wait_ge(s_l, KD * half + k + 1)
                                x = slice(i * P, i * P + P)
                                mm = split_matmul(pe, bank[2 * i + half][:, :], (hT[:, k, x], catT[:, k, x]), (hi[:, k, o], raw[:, k, o]), k == 0, k == KD - 1)
                            mm.then_inc(s_y, 1)

                steps = [(half, k) for half in range(2) for k in range(KD)]

                def split_high(act):
                    for half, k in steps:
                        o = slice(half * 512, half * 512 + 512)
                        if half == 0:
                            act.wait_ge(s_w[k // 2], 16)
                            high(act, hT[:, k, tok], catT[:, k, tok])
                        high(act, hi[:, k, o], raw[:, k, o]).then_inc(s_h, 1)

                def split_low(dve):
                    for step, (half, k) in enumerate(steps):
                        o = slice(half * 512, half * 512 + 512)
                        dve.wait_ge(s_h, step + 1)
                        if half == 0:
                            low(dve, catT[:, k, tok], hT[:, k, tok])
                        low(dve, raw[:, k, o], hi[:, k, o]).then_inc(s_l, 1)
                add_normed(block, n, gate_lat, gate_ctx, s_y, s_ss, s_r, ss, r, cut(16480, 8, 512), cut(0, D), split_high, split_low)

        def add_normed(block, n, gate_lat, gate_ctx, s_y, s_ss, s_r, ss, r, junk, tmp, act_first=None, dve_first=None):

            @block.scalar
            def _(act):
                if act_first:
                    act_first(act)
                for i in range(n):
                    for half in range(2):
                        act.wait_ge(s_y, 2 * i + half + 1)
                        act.activation(junk[:, 2 * i + half, :], bank[2 * i + half][:, :], ACT.Square,
                                       accum_out=ss[:, 2 * i + half:2 * i + half + 1]).then_inc(s_ss, 1)

            @block.gpsimd
            def _(pool):
                link = linker(pool, "pool")
                for i in range(n):
                    pool.wait_ge(s_ss, 2 * i + 2)
                    link(pool.tensor_tensor(r[:, i:i + 1], ss[:, 2 * i:2 * i + 1], ss[:, 2 * i + 1:2 * i + 2], ALU.add))
                    link(pool.tensor_scalar(r[:, i:i + 1], r[:, i:i + 1], 1.0 / D, EPS, ALU.mult, ALU.add))
                    pool.tensor_tensor(r[:, i:i + 1], r[:, i:i + 1], mhalf[:, 0:1], ALU.pow).then_inc(s_r, 1)

            @block.vector
            def _(dve):
                link = linker(dve, "dve")
                if dve_first:
                    dve_first(dve)
                for i in range(n):
                    dve.wait_ge(s_r, i + 1)
                    gate = G[:, gate_lat if i < 2 else gate_ctx, :]
                    for half in range(2):
                        h = slice(half * 512, half * 512 + 512)
                        link(dve.scalar_tensor_tensor(tmp[:, h], bank[2 * i + half][:, :], r[:, i:i + 1], gate[:, h], ALU.mult, ALU.mult))
                    link(dve.tensor_tensor(X[:, i, :], X[:, i, :], tmp, ALU.add))

        def attention(tag, jobs, qT, kT_of, v_of, bias_of, sink_of, prob, probT, pool_beside, act_beside, act_after, dve_beside, bias_ready=None, dve_after=None, pe_after=None):
            s_s, s_m, s_e, s_n, s_t, s_tc, s_o, s_oc = (sem(f"{tag}_{x}") for x in
                ("scores", "max", "exp", "probs", "probs_turned", "turned_copied", "pv", "pv_copied"))
            nm, rs, ri, sk = small[:, 32:35], small[:, 35:38], small[:, 38:41], small[:, 41:44]
            n_jobs = len(jobs)
            with nc.Block() as block:
                @block.gpsimd
                def _(pool):
                    pool_beside(pool)

                @block.tensor
                def _(pe):
                    def scores(j):
                        tile, c, part = jobs[j]
                        a = 64 * part
                        if j >= 3:
                            pe.wait_ge(s_e, j - 2)
                        if tile < 2:
                            if bias_ready:
                                pe.wait_ge(*bias_ready)
                            pe.matmul(bank[j % 3][:, :], qT[a:a + 64, c, tile * P:tile * P + P], kT_of(c)[a:a + 64, :], start=True, stop=False)
                            pe.matmul(bank[j % 3][:, 0:256], ident, bias_of(tile, c, part), start=False, stop=True).then_inc(s_s, 1)
                        else:
                            pe.matmul(bank[j % 3][:, 256:512], qT[a:a + 64, c, tile * P:tile * P + P], kT_of(c)[a:a + 64, 256:512],
                                      start=True, stop=True).then_inc(s_s, 1)

                    def turn(j):
                        tile = jobs[j][0]
                        pe.wait_ge(s_n, j + 1)
                        if j >= 2:
                            pe.wait_ge(s_tc, j - 1)
                        for b in range(0 if tile < 2 else 2, 4):
                            mm = pe.transpose(bank[3 + j % 2][:, b * P:b * P + P], prob[:, j % 3, b * P:b * P + P], ident)
                        mm.then_inc(s_t, 1)

                    def pv(j):
                        tile, c, part = jobs[j]
                        pe.wait_ge(s_tc, j + 1)
                        if j >= 4:
                            pe.wait_ge(s_oc, j // 2 - 1)
                        blocks = range(0 if tile < 2 else 2, 4)
                        for b in blocks:
                            mm = pe.matmul(bank[5 + (j // 2) % 2][64 * part:64 * part + 64, 0:P], v_of(b, c, part),
                                           probT[:, j % 2, b * P:b * P + P], start=(b == blocks[0]), stop=(b == 3), skip_group_check=True)
                        mm.then_inc(s_o, 1)
                    for j in range(n_jobs + 3):
                        if j < n_jobs:
                            scores(j)
                        if 2 <= j < n_jobs + 2:
                            turn(j - 2)
                        if j >= 3:
                            pv(j - 3)
                    if pe_after:
                        pe_after(pe)

                @block.vector
                def _(dve):
                    link = linker(dve, "dve")

                    def maximum(j):
                        lo = 0 if jobs[j][0] < 2 else 256
                        dve.wait_ge(s_s, j + 1)
                        if sink_of:
                            link(dve.tensor_reduce(nm[:, j % 3:j % 3 + 1], bank[j % 3][:, lo:512], AX.X, ALU.max))
                            dve.tensor_scalar(nm[:, j % 3:j % 3 + 1], nm[:, j % 3:j % 3 + 1], sink_of(*jobs[j][1:]), -1.0,
                                              ALU.max, ALU.mult).then_inc(s_m, 1)
                        else:
                            dve.tensor_reduce(nm[:, j % 3:j % 3 + 1], bank[j % 3][:, lo:512], AX.X, ALU.max, negate=True).then_inc(s_m, 1)

                    def normalise(j):
                        lo = 0 if jobs[j][0] < 2 else 256
                        m = j % 3
                        dve.wait_ge(s_e, j + 1)
                        if sink_of:
                            link(dve.tensor_tensor(rs[:, m:m + 1], rs[:, m:m + 1], sk[:, m:m + 1], ALU.add))
                        link(dve.reciprocal(ri[:, m:m + 1], rs[:, m:m + 1]))
                        dve.tensor_scalar(prob[:, m, lo:512], prob[:, m, lo:512], ri[:, m:m + 1], None, ALU.mult).then_inc(s_n, 1)

                    def copy_o(j):
                        tile, c, _ = jobs[2 * j]
                        dve.wait_ge(s_o, 2 * j + 2)
                        dve.tensor_copy(catT[:, c, tile * P:tile * P + P], bank[5 + j % 2][:, 0:P]).then_inc(s_oc, 1)
                    for j in range(n_jobs + 5):
                        if j < n_jobs:
                            maximum(j)
                        if 1 <= j <= n_jobs:
                            normalise(j - 1)
                        if j < n_jobs:
                            dve_beside(dve, j)
                        if j >= 5 and j % 2 == 1:
                            copy_o((j - 5) // 2)
                    if dve_after:
                        dve_after(dve)

                @block.scalar
                def _(act):
                    def expo(j):
                        m = j % 3
                        lo = 0 if jobs[j][0] < 2 else 256
                        act.wait_ge(s_m, j + 1)
                        if j >= 3:
                            act.wait_ge(s_t, j - 2)
                        if sink_of:
                            act.activation(sk[:, m:m + 1], sink_of(*jobs[j][1:]), ACT.Exp, bias=nm[:, m:m + 1])
                        act.activation(prob[:, m, lo:512], bank[m][:, lo:512], ACT.Exp, bias=nm[:, m:m + 1],
                                       accum_out=rs[:, m:m + 1]).then_inc(s_e, 1)

                    def copy_t(j):
                        lo = 0 if jobs[j][0] < 2 else 256
                        act.wait_ge(s_t, j + 1)
                        if j >= 2:
                            act.wait_ge(s_o, j - 1)
                        act.activation(probT[:, j % 2, lo:512], bank[3 + j % 2][:, lo:512], ACT.Copy).then_inc(s_tc, 1)
                    for j in range(n_jobs + 2):
                        if j < n_jobs:
                            expo(j)
                            act_beside(act, j)
                        if j >= 2:
                            copy_t(j - 2)
                    act_after(act)

        nqT, nkT, V, zT = cut(0, 4, NTOK), cut(2048, 4, NTOK), cut(4096, T, 512), cut(6144, 4, NTOK)
        CX = cut(8192, 12, 2, 260)
        NWR, WCH = 3, 14
        WR = [cut(16384 + i * 4096, KD, 256) for i in range(NWR)]
        WRH = [cut(18432 + i * 4096, KD, 256) for i in range(NWR)]
        natb = cut(23136, 2, 8, 256)
        graw = catT[0:16, 4:8, :]
        wg = sb_split("gate_weights", KD * 16, [P, KD, 16])
        wgh = small[:, 256:384].rearrange("p (k n) -> p k n", k=KD)

        s_wi = [sem(f"in_w{i}") for i in range(NWR)]
        s_pj, s_pe_a, s_pe_v, s_wg, s_bias_in, s_ih, s_il = (sem(x) for x in
            ("in_product", "in_copied_act", "in_copied_dve", "gate_w", "nat_bias_in", "in_w_high", "in_w_low"))
        WIN = t["ev_w_in"].rearrange("(k p) n -> p k n", p=P)

        def load_in(sp, c):
            sp.dma_start(WR[c % NWR], WIN[:, :, c * 256:c * 256 + 256]).then_inc(s_wi[c % NWR], 16)

        def in_ahead(sp):
            load_in(sp, 0)
            for n, (l, j, v) in enumerate(((0, 0, 0), (0, 1, 0), (1, 0, 0), (1, 1, 0), (0, 0, 1), (0, 1, 1))):
                sp.dma_start(G[:, n, :], gate_dram[l, j, v:v + 1, :].to_broadcast([P, D])).then_inc(s_g_in, 16)
            for c in range(1, NWR):
                load_in(sp, c)
            sp.wait_ge(s_g_in, 96)
            sp.dma_start(wg[:, :, :], WIN[:, :, 3584:3600]).then_inc(s_wg, 16)
        norm_to_hT("l0_mix", 0, 0, range(4), cut(8192, 4, D), ahead=in_ahead)

        in_jobs = [(c, m) for c in range(WCH) for m in range(4 if c in (4, 5) else 2)]
        made = [sum(cc <= c for cc, _ in in_jobs) for c in range(WCH)]
        with nc.Block() as block:
            @block.sync
            def _(sp):
                for c in range(NWR, WCH):
                    sp.wait_ge(s_pj, made[c - NWR])
                    load_in(sp, c)

            @block.gpsimd
            def _(pool):
                pool.memset(CX[:, :, :, 0:2], 0.0)
                pool.memset(CX[:, :, :, 258:260], 0.0)

            @block.tensor
            def _(pe):
                for j, (c, m) in enumerate(in_jobs):
                    s = c % NWR
                    if m == 0:
                        pe.wait_ge(s_il, c + 1)
                    if j >= 6:
                        pe.wait_ge((s_pe_a, s_pe_v)[j % 2], (j - 6) // 2 + 1)
                    for k in range(KD):
                        st, sp_ = k == 0, k == KD - 1
                        x = slice(m * P, m * P + P)
                        if c in (4, 5):
                            mm = split_matmul(pe, bank[j % 6][:, 0:256], (hT[:, k, x], catT[:, k, x]), (WRH[s][:, k, :], WR[s][:, k, :]), st, sp_)
                        else:
                            mm = split_matmul(pe, bank[j % 6][:, :], (WRH[s][:, k, x], WR[s][:, k, x]), (hT[:, k, :], catT[:, k, :]), st, sp_)
                    mm.then_inc(s_pj, 1)
                pe.wait_ge(s_il, WCH + 1)
                for g in range(2):
                    x = slice(8 * g, 8 * g + 8)
                    for k in range(KD):
                        mm = split_matmul(pe, bank[6 + g][0:8, :], (wgh[:, k, x], wg[:, k, x]), (hT[:, k, :], catT[:, k, :]), k == 0, k == KD - 1)
                mm.then_inc(s_pj, 1)

            def evacuate(eng, parity, s_done, c):
                for j, (cc, m) in enumerate(in_jobs):
                    if cc != c or j % 2 != parity:
                        continue
                    eng.wait_ge(s_pj, j + 1)
                    b, scale = bank[j % 6][:, :], 1.0
                    f = (c % 2) * 2 + m
                    if c < 2:
                        dst, scale = nqT[:, f, :], 0.125
                    elif c < 4:
                        dst = nkT[:, f, :]
                    elif c < 6:
                        dst, b = V[:, m, (c % 2) * 256:(c % 2) * 256 + 256], b[:, 0:256]
                    elif c < 12:
                        dst, b = CX[:, 2 * (c - 6) + m, :, 2:258], b.rearrange("p (s n) -> p s n", s=2)
                    else:
                        dst = zT[:, f, :]
                    if parity == 0:
                        ins = eng.activation(dst, b, ACT.Copy, scale=scale)
                    else:
                        ins = eng.tensor_scalar(dst, b, scale, None, ALU.mult)
                    ins.then_inc(s_done, 1)

            @block.scalar
            def _(act):
                def split(c):
                    if c < WCH:
                        act.wait_ge(s_wi[c % NWR], 16 * (c // NWR) + 16)
                        high(act, WRH[c % NWR], WR[c % NWR]).then_inc(s_ih, 1)
                    elif c == WCH:
                        act.wait_ge(s_wg, 16)
                        high(act, wgh, wg[:, :, :]).then_inc(s_ih, 1)
                split(0)
                split(1)
                for c in range(WCH):
                    evacuate(act, 0, s_pe_a, c)
                    split(c + 2)
                act.wait_ge(s_pj, len(in_jobs) + 1)
                act.activation(graw[0:8, 0, :], bank[6][0:8, :], ACT.Copy)
                act.activation(graw[0:8, 1, :], bank[7][0:8, :], ACT.Copy)

            @block.vector
            def _(dve):
                def split(c):
                    if c <= WCH:
                        dve.wait_ge(s_ih, c + 1)
                        v, hi = (WR[c % NWR], WRH[c % NWR]) if c < WCH else (wg[:, :, :], wgh)
                        low(dve, v, hi).then_inc(s_il, 1)
                split(0)
                split(1)
                for c in range(WCH):
                    evacuate(dve, 1, s_pe_v, c)
                    split(c + 2)

        def convolve(tag, n, n_pool, src, dst, tap_col, tmp):
            s_cp, s_cd, s_si = sem(f"{tag}_convolved_pool"), sem(f"{tag}_convolved_dve"), sem(f"{tag}_conv_silu")

            POOL_STEPS = 2 * TAPS - 1

            def view(v):
                return v.rearrange("p (s n) -> p s n", s=2)

            def on_pool(pool):
                for c in range(n_pool):
                    a = view(dst[:, c, :])
                    pool.tensor_scalar(a, src[:, c, :, 0:256], tap_col(0, c), None, ALU.mult).then_inc(s_cp, 1)
                    for k in range(1, TAPS):
                        m = view(tmp[:, k % 2, :])
                        pool.tensor_scalar(m, src[:, c, :, k:k + 256], tap_col(k, c), None, ALU.mult).then_inc(s_cp, 1)
                        pool.wait_ge(s_cp, POOL_STEPS * c + 2 * k)
                        pool.tensor_tensor(a, a, m, ALU.add).then_inc(s_cp, 1)

            def on_dve(dve, first, last):
                for step in range(first, min(last, (n - n_pool) * TAPS)):
                    c, k = n_pool + step // TAPS, step % TAPS
                    a = view(dst[:, c, :])
                    if k == 0:
                        dve.tensor_scalar(a, src[:, c, :, 0:256], tap_col(0, c), None, ALU.mult).then_inc(s_cd, 1)
                    else:
                        dve.wait_ge(s_cd, step)
                        dve.scalar_tensor_tensor(a, src[:, c, :, k:k + 256], tap_col(k, c), a, ALU.mult, ALU.add).then_inc(s_cd, 1)

            def on_act(act):
                for c in range(n):
                    act.wait_ge(s_cp, POOL_STEPS * (c + 1)) if c < n_pool else act.wait_ge(s_cd, TAPS * (c - n_pool + 1))
                    act.activation(dst[:, c, :], dst[:, c, :], ACT.Silu).then_inc(s_si, 1)
            return on_pool, on_dve, on_act, s_si

        def gate_rows(tag, n, x, bias, alog, out_dt, out_g, sigmoid=None):
            s_1, s_2 = sem(f"{tag}_dve"), sem(f"{tag}_act")
            e, u, lnu, w = (hT[0:n, i, :] for i in range(4))
            a = gbias[0:n, 6:7]

            def on_dve(dve, step):
                if step in (2, 3):
                    return
                k = step if step < 2 else step - 2
                if k > 10:
                    return
                if k:
                    dve.wait_ge(s_1, k)
                if k == 0:
                    ins = dve.tensor_scalar(x, x, bias, None, ALU.add)
                elif k == 1:
                    ins = dve.scalar_tensor_tensor(e, x, -1.0, x, ALU.mult, ALU.min)
                elif k == 2:
                    dve.wait_ge(s_2, 1)
                    ins = dve.tensor_scalar(u, e, 1.0, None, ALU.add)
                elif k == 3:
                    ins = dve.tensor_scalar(w, u, 1.0, None, ALU.subtract)
                elif k == 4:
                    ins = dve.tensor_tensor(e, e, w, ALU.subtract)
                elif k == 5:
                    ins = dve.reciprocal(w, u)
                elif k == 6:
                    ins = dve.tensor_tensor(e, e, w, ALU.mult)
                elif k == 7:
                    dve.wait_ge(s_2, 2)
                    ins = dve.tensor_tensor(e, e, lnu, ALU.add)
                elif k == 8:
                    ins = dve.scalar_tensor_tensor(out_dt, x, 0.0, e, ALU.max, ALU.add)
                elif k == 9:
                    dve.wait_ge(s_2, 3)
                    ins = dve.tensor_scalar(a, a, -1.0, None, ALU.mult)
                else:
                    ins = dve.tensor_scalar(out_g, out_dt, a, None, ALU.mult)
                ins.then_inc(s_1, 1)

            def on_act(act, step):
                if step == 3:
                    act.wait_ge(s_1, 2)
                    act.activation(e, e, ACT.Exp).then_inc(s_2, 1)
                elif step == 6:
                    act.wait_ge(s_1, 3)
                    act.activation(lnu, u, ACT.Ln).then_inc(s_2, 1)
                    act.activation(a, alog, ACT.Exp).then_inc(s_2, 1)

            def finish(act):
                if sigmoid is not None:
                    act.activation(sigmoid, sigmoid, ACT.Sigmoid)
            return on_dve, on_act, finish

        s_ncol = sem("nat_column_mask")
        FX = cut(14432, 12, NTOK)
        conv_pool, conv_dve, conv_act, s_conv = convolve("dn", 12, 4, CX, FX, DNCONV, cut(27232, 2, 512))
        gates_dve, gates_act, gates_end = gate_rows("dn_gates", 8, graw[0:8, 1, :], gbias[0:8, 0:1], gbias[0:8, 1:2], graw[0:8, 2, :], graw[0:8, 3, :],
                                         sigmoid=graw[0:8, 0, :])

        def mask_and_convolve(pool):
            pool.dma_start(natb, t["nat_bias"]).then_inc(s_bias_in, 16)
            pool.wait_ge(s_bias_in, 16)
            for i in range(2):
                for g in range(2):
                    v = natb[:, i, 4 * g:4 * g + 4, :].rearrange("p h (r c) -> p (h r) c", c=64)
                    m = cst("natcol").rearrange("p (a c) -> p a c", a=1).to_broadcast([P, 16, 64])
                    pool.tensor_tensor(v, v, m, ALU.add).then_inc(s_ncol, 1)
            conv_pool(pool)

        sq = hT
        s_sq, s_ssp = sem("dn_squares"), sem("dn_norm_sums")

        def squares(dve):
            for c in range(8):
                dve.wait_ge(s_conv, c + 1)
                dve.tensor_tensor(sq[:, c, :], FX[:, c, :], FX[:, c, :], ALU.mult).then_inc(s_sq, 1)

        def sums(pe):
            for c in range(8):
                pe.wait_ge(s_sq, c + 1)
                mm = pe.matmul(bank[7][0:8, :], cst("eighth")[:, 7 - c:15 - c], sq[:, c, :], start=(c == 0), stop=(c == 7))
            mm.then_inc(s_ssp, 1)

        nat_jobs = [(tile, c, part) for tile in (2, 3, 0, 1) for c in range(4) for part in range(2)]
        attention("nat", nat_jobs, nqT, lambda c: nkT[:, c, :], lambda b, c, part: V[:, b, (2 * c + part) * HD:(2 * c + part + 1) * HD],
                  lambda tile, c, part: natb[:, tile, 2 * c + part, :], None, cut(20576, 3, 512), cut(22112, 2, 512),
                  mask_and_convolve, gates_act, lambda act: (gates_end(act), conv_act(act)),
                  lambda dve, j: (gates_dve(dve, j), conv_dve(dve, 40 * j // 32, 40 * (j + 1) // 32)), bias_ready=(s_ncol, 4),
                  dve_after=squares, pe_after=sums)

        def spread(col, n, w):
            return col.rearrange("p (a b) -> p a b", b=1).to_broadcast([P, n, w])

        def heads(v, n):
            return v.rearrange("p (h e) -> p h e", h=n)

        dc = sb("delta_cols", [P, 9, 32])
        BETA, GS, GC, NGC, GL, EGC, EGL, EKD, BEG = (dc[:, i, :] for i in range(9))
        RL = small[:, 64:96]
        ssum = small[0:8, 128:640]
        s_srow, s_stu, s_sse, s_rl, s_bc, s_nrm = (sem(f"dn_{x}") for x in
            ("norm_rows", "norm_rows_turned", "norm_sums_eps", "rnorm", "rnorm_spread", "normed"))
        with nc.Block() as block:
            @block.scalar
            def _(act):
                act.activation(ssum, bank[7][0:8, :], ACT.Copy).then_inc(s_srow, 1)

            @block.tensor
            def _(pe):
                pe.wait_ge(s_srow, 1)
                for i in range(T):
                    mm = pe.transpose(bank[0][:, 8 * i:8 * i + 8], ssum[:, i * P:i * P + P], ident[0:8, 0:8])
                mm.then_inc(s_stu, 1)
                pe.wait_ge(s_rl, 1)
                for c in range(8):
                    if c >= 4:
                        pe.wait_ge(s_nrm, c - 3)
                    for i in range(T):
                        mm = pe.matmul(bank[1 + c % 4][:, i * P:i * P + P], RL[:, 8 * i + c:8 * i + c + 1].to_broadcast([P, P]), ident,
                                       start=True, stop=True)
                    mm.then_inc(s_bc, 1)

            @block.gpsimd
            def _(pool):
                link = linker(pool, "pool")
                pool.wait_ge(s_sse, 1)
                link(pool.tensor_tensor(RL, RL, mhalf[:, 0:32], ALU.pow))
                queries = RL.rearrange("p (i c) -> p i c", c=8)[:, :, 0:4]
                link(pool.tensor_scalar(queries, queries, float(P) ** -0.5, None, ALU.mult))
                pool.sem_inc(s_rl, 1)

            @block.vector
            def _(dve):
                dve.wait_ge(s_stu, 1)
                dve.tensor_scalar(RL, bank[0][:, 0:32], EPS, None, ALU.add).then_inc(s_sse, 1)
                for c in range(8):
                    dve.wait_ge(s_bc, c + 1)
                    dve.tensor_tensor(FX[:, c, :], FX[:, c, :], bank[1 + c % 4][:, :], ALU.mult).then_inc(s_nrm, 1)

        def columns_and_turns(tag, n_raw, raw, cols_out, n_g, gs, gc, ngc, gl, ekd, exps, after, turned):
            s_gt, s_gcp, s_cs, s_gl, s_ex, s_kv, s_kva, s_kvv = (sem(f"{tag}_{x}") for x in
                ("gates_turned", "gates_copied", "cumsums", "sums_copied", "exponents", "turned", "turned_copied_act", "turned_copied_dve"))
            w = T * n_raw
            nj = len(turned)
            with nc.Block() as block:
                @block.tensor
                def _(pe):
                    for g, r in enumerate(raw):
                        for i in range(T):
                            mm = pe.transpose(bank[0][:, w * g + n_raw * i:w * g + n_raw * (i + 1)], r[:, i * P:i * P + P], ident[0:n_raw, 0:n_raw])
                    mm.then_inc(s_gt, 1)

                    def turn(j):
                        if j >= 4:
                            pe.wait_ge((s_kva, s_kvv)[j % 2], (j - 4) // 2 + 1)
                        for b, src in enumerate(turned[j][0]):
                            mm = pe.transpose(bank[4 + j % 4][:, b * P:b * P + P], src, ident)
                        mm.then_inc(s_kv, 1)
                    for j in range(min(4, nj)):
                        turn(j)
                    pe.wait_ge(s_gcp, len(raw))
                    h = n_raw // 2
                    for d in range(2):
                        of_dir = lambda v: v.rearrange("p (i d h) -> p i d h", i=T, d=2)[:, :, d, :]
                        pe.matmul(of_dir(bank[1][:, 0:w]), cum[d], of_dir(gs[:, 0:w]), start=True, stop=True)
                    pe.matmul(bank[1][:, w:2 * w], ones, gs[:, 0:w], start=True, stop=True).then_inc(s_cs, 1)
                    for j in range(4, nj):
                        turn(j)

                def copy(eng, parity, s_done, lo, hi):
                    for j in range(lo + (parity - lo) % 2, hi, 2):
                        eng.wait_ge(s_kv, j + 1)
                        n = P * len(turned[j][0])
                        if parity == 0:
                            eng.activation(turned[j][1], bank[4 + j % 4][:, 0:n], ACT.Copy).then_inc(s_done, 1)
                        else:
                            eng.tensor_copy(turned[j][1], bank[4 + j % 4][:, 0:n]).then_inc(s_done, 1)

                @block.vector
                def _(dve):
                    link = linker(dve, "dve")
                    dve.wait_ge(s_gt, 1)
                    for g, dst in enumerate(cols_out):
                        dve.tensor_copy(dst, bank[0][:, w * g:w * g + w]).then_inc(s_gcp, 1)
                    copy(dve, 1, s_kvv, 0, min(4, nj))
                    dve.wait_ge(s_cs, 1)
                    link(dve.tensor_copy(gc, bank[1][:, 0:w]))
                    link(dve.tensor_copy(gl, bank[1][:, w:2 * w]))
                    link(dve.tensor_scalar(ngc, gc, -1.0, None, ALU.mult))
                    dve.tensor_tensor(ekd, gl, gc, ALU.subtract).then_inc(s_gl, 1)
                    copy(dve, 1, s_kvv, 4, nj)
                    dve.wait_ge(s_ex, 3)
                    after(dve)

                @block.scalar
                def _(act):
                    copy(act, 0, s_kva, 0, min(4, nj))
                    act.wait_ge(s_gl, 1)
                    for dst, src in exps:
                        act.activation(dst, src, ACT.Exp).then_inc(s_ex, 1)
                    copy(act, 0, s_kva, 4, nj)

        KT, VT = cut(0, T, 512), cut(2048, T, 512)
        columns_and_turns("dn_cols", 8, (graw[0:8, 0, :], graw[0:8, 3, :]), (BETA, GS), 8, GS, GC, NGC, GL, EKD,
                          ((EGC, GC), (EGL, GL), (EKD, EKD)),
                          lambda dve: dve.tensor_tensor(BEG, BETA, EGC, ALU.mult),
                          [([FX[:, c0 + h, i * P:i * P + P] for h in range(4)], dst[:, i, :]) for c0, dst in ((4, KT), (8, VT)) for i in range(T)])

        def col(v, i, d, h, w=4):
            a = (2 * w) * i + w * d + h
            return v[:, a:a + 1]

        KB = cut(8192, 2, 4, NTOK)
        AT, QA = cut(20576, 8, 512), cut(24672, 8, 512)
        DT = cut(12288, 2, 512)
        LMT = cut(4096, 2, LEVELS, P)
        s_bs, s_kb, s_lm, s_pd, s_pa, s_pq, s_dt, s_am, s_qm = (sem(f"dn_{x}") for x in
            ("beta_spread", "beta_keys", "level_masks", "log_decay", "kk", "kq", "decay", "a_masked", "q_masked"))
        with nc.Block() as block:
            @block.sync
            def _(sp):
                sp.dma_start(LMT, t["levels"]).then_inc(s_lm, 16)

            @block.tensor
            def _(pe):
                for d in range(2):
                    for h in range(4):
                        j = 4 * d + h
                        if j >= 2:
                            pe.wait_ge(s_kb, j - 1)
                        for i in range(T):
                            mm = pe.matmul(bank[6 + j % 2][:, i * P:i * P + P], col(BETA, i, d, h).to_broadcast([P, P]), ident, start=True, stop=True)
                        mm.then_inc(s_bs, 1)
                for g in range(8):
                    d, i = divmod(g, T)
                    tk = slice(i * P, i * P + P)
                    if g >= 2:
                        pe.wait_ge(s_dt, g - 1)
                    pe.matmul(quad(g % 2), ident, neg[d].rearrange("p (a c) -> p a c", a=1).to_broadcast([P, 4, P]), start=True, stop=False, skip_group_check=True)
                    for h in range(4):
                        mm = pe.matmul(quad(g % 2)[:, h, :], col(GS, i, d, h).to_broadcast([P, P]), cum[d], start=False, stop=(h == 3), skip_group_check=True)
                    mm.then_inc(s_pd, 1)
                    if g >= 2:
                        pe.wait_ge(s_am, g - 1)
                    pe.wait_ge(s_kb, 4 * d + 4)
                    for h in range(4):
                        mm = pe.matmul(quad(2 + g % 2)[:, h, :], FX[:, 4 + h, tk], KB[:, d, h, tk], start=True, stop=True)
                    mm.then_inc(s_pa, 1)
                    if g >= 2:
                        pe.wait_ge(s_qm, g - 1)
                    for h in range(4):
                        mm = pe.matmul(quad(4 + g % 2)[:, h, :], FX[:, 4 + h, tk], FX[:, h, tk], start=True, stop=True)
                    mm.then_inc(s_pq, 1)

            @block.scalar
            def _(act):
                for g in range(8):
                    d, i = divmod(g, T)
                    act.wait_ge(s_pd, g + 1)
                    if g >= 2:
                        act.wait_ge(s_qm, g - 1)
                    for h in range(4):
                        ins = act.activation(DT[:, g % 2, h * P:h * P + P], quad(g % 2)[:, h, :], ACT.Exp, bias=col(NGC, i, d, h))
                    ins.then_inc(s_dt, 1)

            @block.vector
            def _(dve):
                for j in range(8):
                    dve.wait_ge(s_bs, j + 1)
                    dve.tensor_tensor(KB[:, j // 4, j % 4, :], FX[:, 4 + j % 4, :], bank[6 + j % 2][:, :], ALU.mult).then_inc(s_kb, 1)
                for g in range(8):
                    dve.wait_ge(s_dt, g + 1)
                    dve.wait_ge(s_pa, g + 1)
                    dve.tensor_tensor(AT[:, g, :], bank[2 + g % 2][:, :], DT[:, g % 2, :], ALU.mult).then_inc(s_am, 1)
                    dve.wait_ge(s_pq, g + 1)
                    dve.tensor_tensor(QA[:, g, :], bank[4 + g % 2][:, :], DT[:, g % 2, :], ALU.mult).then_inc(s_qm, 1)

        XI, XT = cut(8192, 8, 512), cut(16480, 8, 512)
        T1 = hT[:, :, :]
        BT = cut(12288, 4, 512)

        def of_pair(v, l, side):
            return v.rearrange("p (q two b) -> p q two b", two=2, b=1 << l)[:, :, side, :]
        s_bt, s_btd, s_xt0, s_a, s_x0, s_t1, s_b, s_up = (sem(f"inv_{x}") for x in
            ("level_block", "level_block_dve", "first_xt", "first_product", "first_x", "product_copied", "second_product", "updated"))
        def level_block(eng, n):
            l, g = divmod(n, 8)
            if n >= 4:
                eng.wait_ge(s_a, n - 3)
                eng.wait_ge(s_xt0, min(n - 3, 8))
            m = LMT[:, g // 4, l, :].rearrange("p (a c) -> p a c", a=1).to_broadcast([P, 4, P])
            return eng.tensor_tensor(heads(BT[:, n % 4, :], 4), heads(AT[:, g, :], 4), m, ALU.mult)

        with nc.Block() as block:
            @block.gpsimd
            def _(pool):
                pool.wait_ge(s_lm, 16)
                for n in range(8 * LEVELS):
                    if n < 8 or n % 2 == 0:
                        level_block(pool, n).then_inc(s_bt, 1)

            @block.tensor
            def _(pe):
                def first(l, g):
                    n = 8 * l + g
                    if l == 0:
                        pe.wait_ge(s_bt, n + 1)
                    elif g % 2 == 0:
                        pe.wait_ge(s_bt, 8 + 4 * (l - 1) + g // 2 + 1)
                    else:
                        pe.wait_ge(s_btd, 4 * (l - 1) + g // 2 + 1)
                    if n >= 4:
                        pe.wait_ge(s_x0, n - 3) if n < 12 else pe.wait_ge(s_t1, n - 11)
                    if l == 1:
                        pe.wait_ge(s_x0, g + 1)
                    if l >= 2:
                        pe.wait_ge(s_up, 8 * (l - 2) + g + 1)
                    for h in range(4):
                        mm = pe.matmul(quad(n % 4)[:, h, :], BT[:, n % 4, h * P:h * P + P], ident if l == 0 else XI[:, g, h * P:h * P + P],
                                       start=True, stop=True)
                    mm.then_inc(s_a, 1)

                def second(l, g):
                    m = 8 * (l - 1) + g
                    pe.wait_ge(s_t1, m + 1)
                    pe.wait_ge(s_xt0, g + 1) if l == 1 else None
                    if m >= 2:
                        pe.wait_ge(s_up, m - 1)
                    for h in range(4):
                        hs, d = slice(h * P, h * P + P), g // 4
                        if l < LEVELS - 1:
                            pe.matmul(of_pair(quad(4 + 2 * (m % 2))[:, h, :], l, d), XT[:, g, hs], of_pair(T1[:, g, hs], l, d), start=True, stop=True)
                        mm = pe.matmul(of_pair(quad(5 + 2 * (m % 2))[:, h, :], l, 1 - d), T1[:, g, hs], of_pair(XT[:, g, hs], l, 1 - d), start=True, stop=True)
                    mm.then_inc(s_b, 1)
                for l in range(2):
                    for g in range(8):
                        first(l, g)
                for l in range(1, LEVELS):
                    for g in range(8 + 3):
                        if g < 8:
                            second(l, g)
                        if g >= 3 and l + 1 < LEVELS:
                            first(l + 1, g - 3)

            @block.scalar
            def _(act):
                for n in range(8, 8 * LEVELS):
                    act.wait_ge(s_a, n + 1)
                    act.activation(T1[:, n % 8, :], bank[n % 4][:, :], ACT.Copy).then_inc(s_t1, 1)

            @block.vector
            def _(dve):
                def odd_blocks(l, groups):
                    for g in groups if l < LEVELS else ():
                        level_block(dve, 8 * l + g).then_inc(s_btd, 1)
                for g in range(8):
                    dve.wait_ge(s_bt, g + 1)
                    dve.tensor_tensor(heads(XT[:, g, :], 4), ident.rearrange("p (a c) -> p a c", a=1).to_broadcast([P, 4, P]),
                                      heads(BT[:, g % 4, :], 4), ALU.subtract).then_inc(s_xt0, 1)
                    dve.wait_ge(s_a, g + 1)
                    dve.tensor_tensor(heads(XI[:, g, :], 4), ident.rearrange("p (a c) -> p a c", a=1).to_broadcast([P, 4, P]),
                                      quad(g % 4), ALU.subtract).then_inc(s_x0, 1)
                odd_blocks(1, (1, 3, 5, 7))
                for m in range(8 * (LEVELS - 1)):
                    l, g = m // 8 + 1, m % 8
                    dve.wait_ge(s_b, m + 1)
                    if l < LEVELS - 1:
                        x = of_pair(XI[:, g, :], l, g // 4)
                        dve.tensor_tensor(x, x, of_pair(bank[4 + 2 * (m % 2)][:, :], l, g // 4), ALU.subtract)
                    x = of_pair(XT[:, g, :], l, 1 - g // 4)
                    dve.tensor_tensor(x, x, of_pair(bank[5 + 2 * (m % 2)][:, :], l, 1 - g // 4), ALU.subtract).then_inc(s_up, 1)
                    odd_blocks(l + 1, {1: (1,), 2: (3,), 5: (5,), 7: (7,)}.get(g, ()))

        U, WT, KDV = cut(8192, 8, 512), cut(20576, 8, 512), hT[:, :, :]
        BV, BW = cut(4096, 2, 512), cut(5120, 2, 512)
        s_bv, s_bw, s_pu, s_cu, s_cw = (sem(f"uw_{x}") for x in ("beta_v", "beta_k", "products", "u_copied", "w_copied"))

        def gcol(v, g, w=4):
            d, i = divmod(g, T)
            a = 2 * w * i + w * d
            return v[:, a:a + w]
        with nc.Block() as block:
            @block.vector
            def _(dve):
                for g in range(9):
                    if g < 8:
                        if g >= 2:
                            dve.wait_ge(s_pu, g - 1)
                        dve.tensor_tensor(heads(BV[:, g % 2, :], 4), heads(VT[:, g % T, :], 4), spread(gcol(BETA, g), 4, P), ALU.mult).then_inc(s_bv, 1)
                    if g >= 1:
                        dve.wait_ge(s_pu, g)
                        dve.tensor_copy(WT[:, g - 1, :], bank[2 + (g - 1) % 2][:, :]).then_inc(s_cw, 1)

            @block.gpsimd
            def _(pool):
                for g in range(8):
                    if g >= 2:
                        pool.wait_ge(s_pu, g - 1)
                    pool.tensor_tensor(heads(BW[:, g % 2, :], 4), heads(KT[:, g % T, :], 4), spread(gcol(BEG, g), 4, P), ALU.mult).then_inc(s_bw, 1)
                    pool.tensor_tensor(heads(KDV[:, g, :], 4), heads(KT[:, g % T, :], 4), spread(gcol(EKD, g), 4, P), ALU.mult)

            @block.tensor
            def _(pe):
                for g in range(8):
                    pe.wait_ge(s_bv, g + 1)
                    pe.wait_ge(s_bw, g + 1)
                    if g >= 2:
                        pe.wait_ge(s_cu, g - 1)
                        pe.wait_ge(s_cw, g - 1)
                    for h in range(4):
                        hs = slice(h * P, h * P + P)
                        pe.matmul(quad(g % 2)[:, h, :], XT[:, g, hs], BV[:, g % 2, hs], start=True, stop=True)
                        mm = pe.matmul(quad(2 + g % 2)[:, h, :], BW[:, g % 2, hs], XT[:, g, hs], start=True, stop=True)
                    mm.then_inc(s_pu, 1)

            @block.scalar
            def _(act):
                for g in range(8):
                    act.wait_ge(s_pu, g + 1)
                    act.activation(U[:, g, :], bank[g % 2][:, :], ACT.Copy).then_inc(s_cu, 1)

        S, VN = cut(12288, 2, 512), cut(13312, 2, 512)
        O = cut(16480, T, 512)
        tmp = cut(18528, 2, 512)
        s_s0, s_p1, s_vn, s_p2, s_se, s_st = (sem(f"scan_{x}") for x in
            ("state_zero", "from_state", "v_new", "products", "state_decayed", "state"))
        with nc.Block() as block:
            @block.gpsimd
            def _(pool):
                pool.memset(S, 0.0).then_inc(s_s0, 1)
                for n in range(8):
                    i, d = divmod(n, 2)
                    g = d * T + CHUNK_ORDER[d][i]
                    pool.wait_ge(s_p1, n + 1)
                    if n >= 2:
                        pool.wait_ge(s_st, n - 1)
                    else:
                        pool.wait_ge(s_s0, 1)
                    pool.tensor_tensor(heads(S[:, d, :], 4), heads(S[:, d, :], 4), spread(gcol(EGL, g), 4, P), ALU.mult).then_inc(s_se, 1)

            @block.tensor
            def _(pe):
                pe.wait_ge(s_s0, 1)
                for i in range(T):
                    for d in range(2):
                        n, tile = 2 * i + d, CHUNK_ORDER[d][i]
                        g = d * T + tile
                        if n >= 2:
                            pe.wait_ge(s_st, n - 1)
                        for h in range(4):
                            hs = slice(h * P, h * P + P)
                            pe.matmul(quad(d)[:, h, :], WT[:, g, hs], S[:, d, hs], start=True, stop=True)
                            mm = pe.matmul(quad(2 + d)[:, h, :], FX[:, h, tile * P:tile * P + P], S[:, d, hs], start=True, stop=True)
                        mm.then_inc(s_p1, 1)
                    for d in range(2):
                        n, tile = 2 * i + d, CHUNK_ORDER[d][i]
                        g = d * T + tile
                        pe.wait_ge(s_vn, n + 1)
                        for h in range(4):
                            hs = slice(h * P, h * P + P)
                            pe.matmul(quad(6 + d)[:, h, :], KDV[:, g, hs], VN[:, d, hs], start=True, stop=True)
                        for h in range(4):
                            hs = slice(h * P, h * P + P)
                            mm = pe.matmul(quad(4 + d)[:, h, :], QA[:, g, hs], VN[:, d, hs], start=True, stop=True)
                        mm.then_inc(s_p2, 1)

            @block.vector
            def _(dve):
                link = linker(dve, "dve")
                for i in range(T):
                    for d in range(2):
                        n, g = 2 * i + d, d * T + CHUNK_ORDER[d][i]
                        dve.wait_ge(s_p1, n + 1)
                        dve.tensor_tensor(VN[:, d, :], U[:, g, :], bank[d][:, :], ALU.subtract).then_inc(s_vn, 1)
                    for d in range(2):
                        n, g = 2 * i + d, d * T + CHUNK_ORDER[d][i]
                        last = dve.tensor_tensor(heads(tmp[:, d, :], 4), quad(2 + d), spread(gcol(EGC, g), 4, P), ALU.mult)
                    link(last)
                    for d in range(2):
                        n, tile = 2 * i + d, CHUNK_ORDER[d][i]
                        dve.wait_ge(s_p2, n + 1)
                        dve.wait_ge(s_se, n + 1)
                        dve.tensor_tensor(S[:, d, :], S[:, d, :], bank[6 + d][:, :], ALU.add).then_inc(s_st, 1)
                        if i in (0, 2):
                            link(dve.tensor_tensor(O[:, tile, :], tmp[:, d, :], bank[4 + d][:, :], ALU.add))
                        else:
                            link(dve.tensor_tensor(O[:, tile, :], O[:, tile, :], tmp[:, d, :], ALU.add))
                            link(dve.tensor_tensor(O[:, tile, :], O[:, tile, :], bank[4 + d][:, :], ALU.add))

        osq, zs, orr = cut(8192, 16, P), cut(0, 4, NTOK), small[:, 96:112]
        s_wo = [sem(f"l0_out_w{i}") for i in range(4)]
        wout, wouth = cut(20576, KD, D), cut(8192, KD, D)
        s_q, s_oss, s_or, s_on, s_ot, s_zs = (sem(f"gn_{x}") for x in ("squares", "sums", "rms", "normed", "turned", "silu_z"))
        with nc.Block() as block:
            @block.sync
            def _(sp):
                load_out_weights(sp, t["ev_w_out"].rearrange("(k p) n -> p k n", p=P), wout, s_wo)

            @block.scalar
            def _(act):
                act.activation(zs, zT, ACT.Silu).then_inc(s_zs, 1)

            @block.vector
            def _(dve):
                link = linker(dve, "dve")
                o3 = O.rearrange("p t (h e) -> p (t h) e", h=4)
                link(dve.tensor_tensor(osq, o3, o3, ALU.mult))
                dve.tensor_reduce(orr, osq, AX.X, ALU.add).then_inc(s_oss, 1)
                dve.wait_ge(s_or, 1)
                dve.tensor_tensor(o3, o3, spread(orr, 16, P), ALU.mult).then_inc(s_on, 1)
                dve.wait_ge(s_zs, 1)
                for h in range(4):
                    dve.wait_ge(s_ot, h + 1)
                    dve.scalar_tensor_tensor(catT[:, 4 + h, :], bank[h][:, :], DNNORM, zs[:, h, :], ALU.mult, ALU.mult)

            @block.gpsimd
            def _(pool):
                link = linker(pool, "pool")
                pool.wait_ge(s_oss, 1)
                link(pool.tensor_scalar(orr, orr, 1.0 / P, EPS, ALU.mult, ALU.add))
                pool.tensor_tensor(orr, orr, mhalf[:, 0:16], ALU.pow).then_inc(s_or, 1)

            @block.tensor
            def _(pe):
                pe.wait_ge(s_on, 1)
                for h in range(4):
                    for i in range(T):
                        mm = pe.transpose(bank[h][:, i * P:i * P + P], O[:, i, h * P:h * P + P], ident)
                    mm.then_inc(s_ot, 1)

        project_and_add("l0_out", 4, 0, 4, s_wo, wout, wouth)

        NS = 3
        W13 = [cut(4096 + i * 2048, 2, KD, P) for i in range(NS)]
        W13H = [cut(10240 + i * 2048, 2, KD, P) for i in range(NS)]
        gT, sl = cut(16384, NF, NTOK), cut(27648, 2, 512)
        W2 = [cut(i * 2048, 2, D) for i in range(NS)]
        W2H = [cut(6144 + i * 2048, 2, D) for i in range(NS)]
        s_w13 = [sem(f"ffn_w13_{i}") for i in range(NS)]
        s_w2 = [sem(f"ffn_w2_{i}") for i in range(NS)]
        s_h1, s_h3, s_sl, s_g, s_13h, s_13l = (sem(f"ffn_{x}") for x in ("h1", "h3", "silu", "gated", "w13_high", "w13_low"))
        w1v = t["ffn_w1"].rearrange("(k p) (c w) -> p k c w", p=P, w=P)
        w3v = t["ffn_w3"].rearrange("(k p) (c w) -> p k c w", p=P, w=P)
        w2v = t["ffn_w2"].rearrange("(c two p) n -> p c two n", p=P, two=2)
        NC = NF // 2

        def load_13(sp, n):
            for m, w in enumerate((w1v, w3v)):
                sp.dma_start(W13[n % NS][:, m, :, :], w[:, :, n, :]).then_inc(s_w13[n % NS], 16)

        def load_2(sp, c):
            sp.dma_start(W2[c % NS], w2v[:, c, :, :]).then_inc(s_w2[c % NS], 16)
        norm_to_hT("l0_ffn", 0, 1, range(4), cut(0, 4, D), ahead=lambda sp: [load_13(sp, n) for n in range(NS)])

        with nc.Block() as block:
            @block.sync
            def _(sp):
                for c in range(2):
                    load_2(sp, c)
                for n in range(NS, NF):
                    sp.wait_ge(s_h3, n - NS + 1)
                    load_13(sp, n)

            @block.tensor
            def _(pe):
                for n in range(NF):
                    for m, s_h in enumerate((s_h1, s_h3)):
                        pe.wait_ge(s_13l, 2 * n + m + 1)
                        if n >= 2:
                            pe.wait_ge((s_sl, s_g)[m], n - 1)
                        for k in range(KD):
                            w = (W13H[n % NS][:, m, k, :], W13[n % NS][:, m, k, :])
                            mm = split_matmul(pe, bank[4 * m + n % 2][:, :], w, (hT[:, k, :], catT[:, k, :]), k == 0, k == KD - 1)
                        mm.then_inc(s_h, 1)

            @block.scalar
            def _(act):
                def split(n):
                    if n < NF:
                        act.wait_ge(s_w13[n % NS], 32 * (n // NS) + 32)
                        for m in range(2):
                            high(act, W13H[n % NS][:, m], W13[n % NS][:, m]).then_inc(s_13h, 1)
                split(0)
                split(1)
                for n in range(NF):
                    act.wait_ge(s_h1, n + 1)
                    if n >= 2:
                        act.wait_ge(s_g, n - 1)
                    act.activation(sl[:, n % 2, :], bank[n % 2][:, :], ACT.Silu).then_inc(s_sl, 1)
                    split(n + 2)

            @block.vector
            def _(dve):
                def split(n):
                    if n < NF:
                        for m in range(2):
                            dve.wait_ge(s_13h, 2 * n + m + 1)
                            low(dve, W13[n % NS][:, m], W13H[n % NS][:, m]).then_inc(s_13l, 1)
                split(0)
                split(1)
                for n in range(NF):
                    split(n + 2)
                    dve.wait_ge(s_sl, n + 1)
                    dve.wait_ge(s_h3, n + 1)
                    dve.tensor_tensor(gT[:, n, :], sl[:, n % 2, :], bank[4 + n % 2][:, :], ALU.mult).then_inc(s_g, 1)

        s_dn, s_dy, s_dss, s_dr, s_dh, s_dl = (sem(f"ffn_{x}") for x in ("down", "down_y", "down_squares", "down_rms", "down_high", "down_low"))
        gh_rest = cut(12288, NF - 2 * KD, NTOK)

        def gh(c):
            v, at_ = (hT, 0) if c < 4 else (catT, 8) if c < 8 else (gh_rest, 16)
            return v[:, 2 * c - at_:2 * c - at_ + 2, :]
        with nc.Block() as block:
            @block.sync
            def _(sp):
                load_2(sp, 2)
                for c in range(NS, NC):
                    sp.wait_ge(s_dn, c - NS + 1)
                    load_2(sp, c)

            @block.tensor
            def _(pe):
                def product(c, f, i, half):
                    x, o = slice(i * P, i * P + P), slice(half * 512, half * 512 + 512)
                    return split_matmul(pe, bank[2 * i + half][:, :], (gh(c)[:, f, x], gT[:, 2 * c + f, x]), (W2H[c % NS][:, f, o], W2[c % NS][:, f, o]),
                                        c == 0 and f == 0, c == NC - 1 and f == 1)
                for c in range(NC):
                    pe.wait_ge(s_dl, c + 1)
                    if c < NC - 1:
                        for f in range(2):
                            for i in range(T):
                                for half in range(2):
                                    mm = product(c, f, i, half)
                        mm.then_inc(s_dn, 1)
                    else:
                        for i in range(T):
                            for half in range(2):
                                product(c, 0, i, half)
                                product(c, 1, i, half).then_inc(s_dy, 1)

            def split_high(act):
                for c in range(NC):
                    act.wait_ge(s_w2[c % NS], 16 * (c // NS) + 16)
                    high(act, gh(c), gT[:, 2 * c:2 * c + 2, :])
                    high(act, W2H[c % NS], W2[c % NS]).then_inc(s_dh, 1)

            def split_low(dve):
                for c in range(NC):
                    dve.wait_ge(s_dh, c + 1)
                    low(dve, gT[:, 2 * c:2 * c + 2, :], gh(c))
                    low(dve, W2[c % NS], W2H[c % NS]).then_inc(s_dl, 1)
            add_normed(block, 4, 1, 5, s_dy, s_dss, s_dr, small[:, 0:8], small[:, 8:16], cut(16384, 8, 512), cut(20480, D), split_high, split_low)

        nc.clear_and_free_semaphores(stage_sems)
        nc.all_engine_barrier()
        stage_sems = []

        qT, kT, V1, Z1 = cut(0, 4, LAT), cut(1024, NTOK), cut(1536, T, P), cut(2048, 2, 512)
        CS = cut(3072, 8, 2, 260)
        dtr = catT[0:16, 4:8, :]
        NOD, OCH = 4, 10
        WI = [cut(12288 + i * 4096, KD, 256) for i in range(NOD)]
        WIH = [cut(14336 + i * 4096, KD, 256) for i in range(NOD)]
        s_oi = [sem(f"od_in_w{i}") for i in range(NOD)]
        s_oj, s_oa, s_ov, s_oh, s_ol = (sem(f"od_in_{x}") for x in ("product", "copied_act", "copied_dve", "high", "low"))
        WOD = t["od_w_in"].rearrange("(k p) n -> p k n", p=P)

        def od_cols(c):
            return 16 if c == OCH - 1 else 256

        def load_od(sp, c):
            sp.dma_start(WI[c % NOD][:, :, 0:od_cols(c)], WOD[:, :, c * 256:c * 256 + od_cols(c)]).then_inc(s_oi[c % NOD], 16)
        norm_to_hT("l1_mix", 1, 0, range(4), cut(0, 4, D), ahead=lambda sp: [load_od(sp, c) for c in range(NOD)])

        od_jobs = ([("q", c, c // 2, c % 2 * P) for c in range(4)] + [("k", 0, 2, 0), ("v", 0, 2, P)]
                   + [("z", i, 3 + half, half) for half in range(2) for i in range(2)]
                   + [("conv", c, 5 + c // 2, c % 2 * P) for c in range(8)] + [("dt", 0, 9, 0)])
        od_made = [sum(job[2] <= c for job in od_jobs) for c in range(OCH)]
        with nc.Block() as block:
            @block.sync
            def _(sp):
                for c in range(NOD, OCH):
                    sp.wait_ge(s_oj, od_made[c - NOD])
                    load_od(sp, c)

            @block.gpsimd
            def _(pool):
                pool.memset(CS[:, :, :, 0:2], 0.0)
                pool.memset(CS[:, :, :, 258:260], 0.0)

            @block.tensor
            def _(pe):
                for j, (kind, i, c, at_) in enumerate(od_jobs):
                    pe.wait_ge(s_ol, c + 1)
                    if j >= 8:
                        pe.wait_ge((s_oa, s_ov)[j % 2], (j - 8) // 2 + 1)
                    b, s = bank[j % 8], c % NOD
                    for tile in range(T if kind == "v" else 1):
                        for k in range(KD):
                            st, sp_ = k == 0, k == KD - 1
                            x = lambda v, a, n: (v[0][:, k, a:a + n], v[1][:, k, a:a + n])
                            h, w = (hT, catT), (WIH[s], WI[s])
                            if kind == "q":
                                mm = split_matmul(pe, b[:, 0:LAT], x(w, at_, P), x(h, 0, LAT), st, sp_)
                            elif kind == "v":
                                mm = split_matmul(pe, b[:, tile * P:tile * P + P], x(h, tile * P, P), x(w, at_, P), st, sp_)
                            elif kind == "z":
                                mm = split_matmul(pe, b[:, 0:256], x(h, i * P, P), x(w, 0, 256), st, sp_)
                            elif kind == "dt":
                                mm = split_matmul(pe, b[0:16, :], x(w, 0, 16), x(h, 0, NTOK), st, sp_)
                            else:
                                mm = split_matmul(pe, b[:, :], x(w, at_, P), x(h, 0, NTOK), st, sp_)
                    mm.then_inc(s_oj, 1)

            def od_copy(eng, parity, s_done, chunk):
                for j, (kind, i, c, at_) in enumerate(od_jobs):
                    if c != chunk or j % 2 != parity:
                        continue
                    eng.wait_ge(s_oj, j + 1)
                    b, scale = bank[j % 8][:, :], 1.0
                    if kind == "q":
                        dst, b, scale = qT[:, i, :], b[:, 0:LAT], 0.125
                    elif kind == "k":
                        dst = kT
                    elif kind == "v":
                        dst = V1.rearrange("p t n -> p (t n)")
                    elif kind == "z":
                        dst, b = Z1[:, i, at_ * 256:at_ * 256 + 256], b[:, 0:256]
                    elif kind == "conv":
                        dst, b = CS[:, i, :, 2:258], b.rearrange("p (s n) -> p s n", s=2)
                    else:
                        dst, b = dtr[:, 0, :], b[0:16, :]
                    if parity == 0:
                        eng.activation(dst, b, ACT.Copy, scale=scale).then_inc(s_done, 1)
                    else:
                        eng.tensor_scalar(dst, b, scale, None, ALU.mult).then_inc(s_done, 1)

            @block.scalar
            def _(act):
                def split(c):
                    if c < OCH:
                        act.wait_ge(s_oi[c % NOD], 16 * (c // NOD) + 16)
                        n = slice(0, od_cols(c))
                        high(act, WIH[c % NOD][:, :, n], WI[c % NOD][:, :, n]).then_inc(s_oh, 1)
                for c in range(3):
                    split(c)
                for c in range(OCH):
                    od_copy(act, 0, s_oa, c)
                    split(c + 3)

            @block.vector
            def _(dve):
                def split(c):
                    if c < OCH:
                        dve.wait_ge(s_oh, c + 1)
                        n = slice(0, od_cols(c))
                        low(dve, WI[c % NOD][:, :, n], WIH[c % NOD][:, :, n]).then_inc(s_ol, 1)
                for c in range(3):
                    split(c)
                for c in range(OCH):
                    od_copy(dve, 1, s_ov, c)
                    split(c + 3)

        rt = cut(7232, 2, 2, LAT)
        s_rp, s_rd = sem("rope_turned"), sem("rope_done")
        with nc.Block() as block:
            @block.tensor
            def _(pe):
                for c in range(5):
                    src = qT[:, c, :] if c < 4 else kT[:, 0:LAT]
                    if c >= 2:
                        pe.wait_ge(s_rd, c - 1)
                    pe.matmul(bank[c % 2][:, 0:LAT], cst("rot"), src, start=True, stop=True).then_inc(s_rp, 1)

            @block.vector
            def _(dve):
                link = linker(dve, "dve")
                for c in range(5):
                    src = qT[:, c, :] if c < 4 else kT[:, 0:LAT]
                    dve.wait_ge(s_rp, c + 1)
                    link(dve.tensor_tensor(rt[:, c % 2, 0, :], src, cst("cos"), ALU.mult))
                    link(dve.tensor_tensor(rt[:, c % 2, 1, :], bank[c % 2][:, 0:LAT], cst("sin"), ALU.mult))
                    ins = dve.tensor_tensor(src, rt[:, c % 2, 0, :], rt[:, c % 2, 1, :], ALU.add)
                    link(ins) if c >= 5 else ins.then_inc(s_rd, 1)
                    dve.wait_ge(s_rd, c + 1)

        FS = cut(9280, 8, NTOK)
        conv_pool1, conv_dve1, conv_act1, _ = convolve("ssd", 8, 3, CS, FS, SSDCONV, cut(15936, 2, 512))
        gates_dve1, gates_act1, gates_end1 = gate_rows("ssd_gates", 16, dtr[:, 0, :], gbias[:, 2:3], gbias[:, 3:4], dtr[:, 1, :], dtr[:, 2, :])
        band = cst("band").rearrange("p (t k) -> p t k", t=2)
        wa_jobs = [(tile, c, part) for tile in range(2) for c in range(4) for part in range(2)]
        attention("win", wa_jobs, qT, lambda c: kT, lambda b, c, part: V1[:, b, part * HD:part * HD + HD],
                  lambda tile, c, part: band[:, tile, :], lambda c, part: rowcol[:, c + 4 * part:c + 4 * part + 1],
                  cut(13376, 3, 512), cut(14912, 2, 512), conv_pool1, gates_act1, lambda act: (gates_end1(act), conv_act1(act)),
                  lambda dve, j: (gates_dve1(dve, j), conv_dve1(dve, 25 * j // 16, 25 * (j + 1) // 16)))

        sc = cut(13376, 9, 64)
        DTC, DA, AC, NAC, AL, EAC, EAL, EDS, DTD = (sc[:, i, :] for i in range(9))
        XT1, BT1 = cut(13952, T, 512), cut(16000, T, 2 * P)
        columns_and_turns("ssd_cols", 16, (dtr[:, 1, :], dtr[:, 2, :]), (DTC, DA), 16, DA, AC, NAC, AL, EDS,
                          ((EAC, AC), (EAL, AL), (EDS, EDS)),
                          lambda dve: dve.tensor_tensor(DTD, DTC, EDS, ALU.mult),
                          [([FS[:, c, i * P:i * P + P] for c in range(4)], XT1[:, i, :]) for i in range(T)]
                          + [([FS[:, 4 + c, i * P:i * P + P] for c in range(2)], BT1[:, i, :]) for i in range(T)])

        XS, XD = cut(17024, 2, 512), cut(18048, 2, 512)
        H, Y = cut(19072, 2, 512), cut(20096, 2, 512)
        LT, MT = cut(21120, 2, 512), cut(22144, 2, 512)
        yt = cut(23168, 512)

        def hcol(v, tile, d):
            return v[:, 16 * tile + 8 * d:16 * tile + 8 * d + 8]
        ssd_steps = [(i, d, CHUNK_ORDER[d][i]) for i in range(T) for d in range(2)]
        s_h0, s_xs, s_st, s_hd, s_h, s_ld, s_lx, s_cb, s_mt, s_mu, s_yd, s_yo, s_yv, s_xd = (sem(f"ssd_{x}") for x in
            ("state_zero", "decayed_x", "state_product", "state_decayed", "state", "log_decay", "decay", "cb", "m", "y_diag_half", "y_diag", "y_off", "y_added", "xd"))
        with nc.Block() as block:
            @block.gpsimd
            def _(pool):
                pool.memset(H, 0.0).then_inc(s_h0, 1)
                pool.wait_ge(s_h0, 1)
                for n, (i, d, tile) in enumerate(ssd_steps):
                    if n < 6:
                        if n >= 2:
                            pool.wait_ge(s_st, n - 1)
                        pool.tensor_tensor(heads(XS[:, n % 2, :], 8), heads(XT1[:, tile, :], 8), spread(hcol(DTD, tile, d), 8, HD), ALU.mult).then_inc(s_xs, 1)
                        if n >= 2:
                            pool.wait_ge(s_h, n - 1)
                        if n >= 4:
                            pool.wait_ge(s_yo, n - 3)
                        pool.tensor_tensor(heads(H[:, d, :], 8), heads(H[:, d, :], 8), spread(hcol(EAL, tile, d), 8, HD), ALU.mult).then_inc(s_hd, 1)

            @block.tensor
            def _(pe):
                for n, (i, d, tile) in enumerate(ssd_steps):
                    tk = slice(tile * P, tile * P + P)
                    if n >= 4:
                        m = n - 4
                        if m >= 1:
                            pe.wait_ge(s_mt, 2 * m)
                        for g in range(2):
                            mm = pe.matmul(quad(4)[:, g, :], FS[:, 4 + g, tk], FS[:, 6 + g, tk], start=True, stop=True)
                        mm.then_inc(s_cb, 1)
                        for g in range(2):
                            q = 2 * m + g
                            if q >= 2:
                                pe.wait_ge(s_lx, q - 1)
                            pe.matmul(quad(q % 2), ident, neg[d].rearrange("p (a c) -> p a c", a=1).to_broadcast([P, 4, P]), start=True, stop=False, skip_group_check=True)
                            for h in range(4):
                                mm = pe.matmul(quad(q % 2)[:, h, :], hcol(DA, tile, d)[:, 4 * g + h:4 * g + h + 1].to_broadcast([P, P]), cum[d], start=False, stop=(h == 3), skip_group_check=True)
                            mm.then_inc(s_ld, 1)
                        pe.wait_ge(s_h, n - 1)
                        if m >= 1:
                            pe.wait_ge(s_yv, m)
                        for g in range(2):
                            mm = pe.matmul(bank[5][:, g * 256:g * 256 + 256], FS[:, 6 + g, tk], H[:, d, g * 256:g * 256 + 256], start=True, stop=True)
                        mm.then_inc(s_yo, 1)
                        pe.wait_ge(s_xd, m + 1)
                        for g in range(2):
                            pe.wait_ge(s_mt, 2 * m + g + 1)
                            for h in range(4):
                                hh = 4 * g + h
                                mm = pe.matmul(bank[6][:, hh * HD:hh * HD + HD], MT[:, g, h * P:h * P + P], XD[:, m % 2, hh * HD:hh * HD + HD], start=True, stop=True)
                            mm.then_inc(s_yd, 1)
                    if n < 6:
                        pe.wait_ge(s_xs, n + 1)
                        if n >= 2:
                            pe.wait_ge(s_h, n - 1)
                        for g in range(2):
                            mm = pe.matmul(bank[2 + n % 2][:, g * 256:g * 256 + 256], BT1[:, tile, g * P:g * P + P], XS[:, n % 2, g * 256:g * 256 + 256], start=True, stop=True)
                        mm.then_inc(s_st, 1)

            @block.scalar
            def _(act):
                for m in range(4):
                    i, d, tile = ssd_steps[4 + m]
                    for g in range(2):
                        q = 2 * m + g
                        act.wait_ge(s_ld, q + 1)
                        if q >= 2:
                            act.wait_ge(s_mt, q - 1)
                        for h in range(4):
                            ins = act.activation(LT[:, q % 2, h * P:h * P + P], quad(q % 2)[:, h, :], ACT.Exp, bias=hcol(NAC, tile, d)[:, 4 * g + h:4 * g + h + 1])
                        ins.then_inc(s_lx, 1)

            @block.vector
            def _(dve):
                link = linker(dve, "dve")
                for i in range(2):
                    dve.tensor_tensor(heads(Y[:, i, :], 8), heads(XT1[:, i, :], 8), spread(rowcol[:, 8:16], 8, HD), ALU.mult)
                for n, (i, d, tile) in enumerate(ssd_steps):
                    m = n - 4
                    if n >= 4:
                        if m >= 2:
                            dve.wait_ge(s_yd, 2 * (m - 1))
                        dve.tensor_tensor(heads(XD[:, m % 2, :], 8), heads(XT1[:, tile, :], 8), spread(hcol(DTC, tile, d), 8, HD), ALU.mult).then_inc(s_xd, 1)
                        dve.wait_ge(s_cb, m + 1)
                        for g in range(2):
                            q = 2 * m + g
                            dve.wait_ge(s_lx, q + 1)
                            if m >= 1:
                                dve.wait_ge(s_yd, 2 * (m - 1) + g + 1)
                            dve.tensor_tensor(heads(MT[:, g, :], 4), heads(LT[:, q % 2, :], 4),
                                              quad(4)[:, g:g + 1, :].to_broadcast([P, 4, P]), ALU.mult).then_inc(s_mt, 1)
                        dve.wait_ge(s_yo, m + 1)
                        link(dve.tensor_tensor(heads(yt, 8), heads(bank[5][:, :], 8), spread(hcol(EAC, tile, d), 8, HD), ALU.mult))
                        link(dve.tensor_tensor(Y[:, tile, :], Y[:, tile, :], yt, ALU.add))
                        dve.wait_ge(s_yd, 2 * m + 2)
                        dve.tensor_tensor(Y[:, tile, :], Y[:, tile, :], bank[6][:, :], ALU.add).then_inc(s_yv, 1)
                        dve.wait_ge(s_yv, m + 1)
                    if n < 6:
                        dve.wait_ge(s_st, n + 1)
                        dve.wait_ge(s_hd, n + 1)
                        dve.tensor_tensor(H[:, d, :], H[:, d, :], bank[2 + n % 2][:, :], ALU.add).then_inc(s_h, 1)

        ysq, zs1, yr = cut(21120, 4, 256), cut(22144, 2, 512), small[:, 96:100]
        s_wo1 = [sem(f"l1_out_w{i}") for i in range(4)]
        wo1, wo1h = cut(8192, KD, D), cut(20576, KD, D)
        s_zs1, s_ys, s_yr, s_yn, s_yt1 = (sem(f"sgn_{x}") for x in ("silu_z", "sums", "rms", "normed", "turned"))
        with nc.Block() as block:
            @block.sync
            def _(sp):
                load_out_weights(sp, t["od_w_out"].rearrange("(k p) n -> p k n", p=P), wo1, s_wo1)

            @block.scalar
            def _(act):
                act.activation(zs1, Z1, ACT.Silu).then_inc(s_zs1, 1)

            @block.vector
            def _(dve):
                link = linker(dve, "dve")
                dve.wait_ge(s_zs1, 1)
                link(dve.tensor_tensor(Y, Y, zs1, ALU.mult))
                y4 = Y.rearrange("p t (g n) -> p (t g) n", g=2)
                link(dve.tensor_tensor(ysq, y4, y4, ALU.mult))
                dve.tensor_reduce(yr, ysq, AX.X, ALU.add).then_inc(s_ys, 1)
                dve.wait_ge(s_yr, 1)
                dve.tensor_tensor(y4, y4, spread(yr, 4, 256), ALU.mult).then_inc(s_yn, 1)
                for c in range(4):
                    dve.wait_ge(s_yt1, c + 1)
                    dve.tensor_scalar(catT[:, 4 + c, 0:LAT], bank[c][:, 0:LAT], SSDNORM(c), None, ALU.mult)

            @block.gpsimd
            def _(pool):
                link = linker(pool, "pool")
                pool.wait_ge(s_ys, 1)
                link(pool.tensor_scalar(yr, yr, 1.0 / 256, EPS, ALU.mult, ALU.add))
                pool.tensor_tensor(yr, yr, mhalf[:, 0:4], ALU.pow).then_inc(s_yr, 1)

            @block.tensor
            def _(pe):
                pe.wait_ge(s_yn, 1)
                for c in range(4):
                    for i in range(2):
                        mm = pe.transpose(bank[c][:, i * P:i * P + P], Y[:, i, c * P:c * P + P], ident)
                    mm.then_inc(s_yt1, 1)

        project_and_add("l1_out", 2, 2, 2, s_wo1, wo1, wo1h)

        xn1 = cut(0, 2, D)
        norm_to_hT("l1_ffn", 1, 1, range(2), xn1, split=False)
        wr = cut(2048, KD, E)
        sm = small[:, 128:640]
        lg, top, gw = sm[:, 0:16], sm[:, 16:32], sm[:, 48:64]
        sel, pos, oh = sm[:, 64:80], sm[:, 80:96], sm[:, 96:128]
        ix = sb("expert_index", [P, 16], U32)
        ixf, ee, tot = sm[:, 128:144], sm[:, 144:160], sm[:, 160:176]
        most = sb("most_tokens", [1, 1], mybir.dt.int32)
        s_wr, s_lg, s_lv, s_e1, s_cp1, s_ps = (sem(f"route_{x}") for x in ("w", "logits", "picked", "exp", "selected", "positions"))
        with nc.Block() as block:
            @block.sync
            def _(sp):
                sp.dma_start(wr, t["moe_router"].rearrange("(k p) e -> p k e", p=P)).then_inc(s_wr, 16)

            @block.tensor
            def _(pe):
                pe.wait_ge(s_wr, 16)
                for i in range(2):
                    for k in range(KD):
                        mm = pe.matmul(bank[0][:, 8 * i:8 * i + 8], hT[:, k, i * P:i * P + P], wr[:, k, :], start=(k == 0), stop=(k == KD - 1))
                mm.then_inc(s_lg, 1)
                pe.wait_ge(s_cp1, 1)
                pe.matmul(bank[1][:, 0:8], cst("before"), sel[:, 0:8], start=True, stop=True)
                pe.matmul(bank[1][:, 8:16], cst("before"), sel[:, 8:16], start=True, stop=False)
                pe.matmul(bank[1][:, 8:16], ones, sel[:, 0:8], start=False, stop=True)
                pe.matmul(bank[1][:, 16:24], ones, sel[:, 0:8], start=True, stop=False)
                pe.matmul(bank[1][:, 16:24], ones, sel[:, 8:16], start=False, stop=True).then_inc(s_ps, 1)

            @block.scalar
            def _(act):
                act.wait_ge(s_lv, 1)
                act.activation(ee[:, 0:2], ee[:, 0:2], ACT.Exp).then_inc(s_e1, 1)

            @block.vector
            def _(dve):
                link = linker(dve, "dve")
                dve.wait_ge(s_lg, 1)
                link(dve.tensor_copy(lg, bank[0][:, 0:16]))
                for i in range(2):
                    a = slice(8 * i, 8 * i + 8)
                    link(dve.max(top[:, a], lg[:, a]))
                    link(dve.max_index(ix[:, a], top[:, a], lg[:, a]))
                link(dve.tensor_copy(ixf, ix[:, :]))
                for i in range(2):
                    ins = dve.tensor_tensor(ee[:, i:i + 1], top[:, 8 * i + 1:8 * i + 2], top[:, 8 * i:8 * i + 1], ALU.subtract)
                ins.then_inc(s_lv, 1)
                dve.wait_ge(s_e1, 1)
                link(dve.tensor_scalar(ee[:, 2:4], ee[:, 0:2], 1.0, None, ALU.add))
                link(dve.reciprocal(ee[:, 4:6], ee[:, 2:4]))
                link(dve.tensor_tensor(ee[:, 6:8], ee[:, 4:6], ee[:, 0:2], ALU.mult))
                for i in range(2):
                    a = slice(8 * i, 8 * i + 8)
                    io = cst("iota")[:, 0:8]
                    link(dve.tensor_scalar(oh[:, 0:8], io, ixf[:, 8 * i:8 * i + 1], None, ALU.is_equal))
                    link(dve.tensor_scalar(oh[:, 8:16], io, ixf[:, 8 * i + 1:8 * i + 2], None, ALU.is_equal))
                    link(dve.tensor_tensor(sel[:, a], oh[:, 0:8], oh[:, 8:16], ALU.add))
                    link(dve.tensor_scalar(oh[:, 16:24], oh[:, 8:16], ee[:, 6 + i:7 + i], None, ALU.mult))
                    link(dve.scalar_tensor_tensor(gw[:, a], oh[:, 0:8], ee[:, 4 + i:5 + i], oh[:, 16:24], ALU.mult, ALU.add))
                dve.sem_inc(s_cp1, 1)
                dve.wait_ge(s_ps, 1)
                dve.tensor_copy(pos, bank[1][:, 0:16])
                link(dve.tensor_reduce(tot[:, 0:1], bank[1][:, 16:24], AX.X, ALU.max))
                dve.tensor_copy(most[:, :], tot[0:1, 0:1])

        NB = FE // 512
        RAW = [cut(4096 + s * 4096, 2048) for s in range(6)]
        HIGH = [cut(4096 + s * 4096 + 2048, 2048) for s in range(6)]

        def half_view(v, kind):
            return v.rearrange("p (k f) -> p k f", k=4) if kind < 2 else v.rearrange("p (j n) -> p j n", j=2)

        xh = [cut(2048 + q * 1024, KD, P) for q in range(2)]
        xl = [G[:, 4 + q, :].rearrange("p (k s) -> p k s", k=KD) for q in range(2)]
        disp = X[:, 2:4, :].rearrange("p a (e i s) -> p (a e) i s", i=2, s=P)
        back = catT[:, 0:4, :].rearrange("p a (e n) -> p (a e) n", n=LAT)
        backs = catT[:, 4, :].rearrange("p (q n) -> p q n", q=2)
        weighted = hT[:, 0:4, :].rearrange("p a (e i s) -> p (a e) i s", i=2, s=P)
        silu_h, prod, prodTh, prodTl = hT[:, 0:2, :], hT[:, 2:4, :], hT[:, 4:6, :], catT[:, 5:7, :]
        ysb = hT[:, 6:8, :].rearrange("p a b -> p (a b)")
        ACC = G[:, 0:2, :]
        w1e = t["moe_w1"].rearrange("e (k p) f -> p e k f", p=P)
        w3e = t["moe_w3"].rearrange("e (k p) f -> p e k f", p=P)
        w2e = t["moe_w2"].rearrange("e (j p) n -> p e j n", p=P)

        def at(e, times, add):
            return times * e + add if isinstance(e, int) else 2 * times * e[0] + (times * e[1] + add)

        def parity(e):
            return (e if isinstance(e, int) else e[1]) % 2

        def at_expert(v, e, shift=0):
            return v[:, bass.ds(at(e, 1, shift), 1)] if not isinstance(e, int) else v[:, e + shift:e + shift + 1]

        def over_experts(eng, body):
            body(0)
            with eng.Fori(0, E // 2 - 1) as p:
                body((p, 1))
                body((p, 2))
            body(E - 1)

        def misc_before(e, add=0):
            return 2 + add if e == 0 and isinstance(e, int) else at(e, 13, add - 3)

        def splits_before(e, add=0):
            return 2 + add if e == 0 and isinstance(e, int) else at(e, 9, add + 1)

        def misc_bank(e, i):
            return 4 + (i if isinstance(e, int) and e == 0 else parity(e) + 1 + i) % 2

        def pieces(c, first, last):
            return ([("scatter", c - 1)] if 1 <= c <= 4 and not first else []) + ([("gather", c - 4)] if c in (4, 5) and not last else [])

        def experts(r):
            tag = f"moe{r}"
            chain[tag] = [sem(f"{tag}_chain"), 0]
            s_dp, s_dt, s_dc = sem(f"{tag}_dispatch"), sem(f"{tag}_turned"), sem(f"{tag}_turned_copied")
            s_w = [sem(f"{tag}_w_{i}") for i in range(6)]
            s_hi = [sem(f"{tag}_high_{i}") for i in range(3)]
            s_lo = [sem(f"{tag}_low_{i}") for i in range(3)]
            s_used = [sem(f"{tag}_used_{i}") for i in range(3)]
            s_sl, s_pr, s_ms, s_mh, s_mf, s_yc, s_bk = (sem(f"{tag}_{x}") for x in
                ("silu", "gated", "misc", "misc_high", "misc_free", "y_copied", "back_copied"))
            s_vx = sem(f"{tag}_gathered_value")

            def load(sp, kind, e, c):
                src = at_expert((w1e, w3e, w2e)[kind], e).rearrange("p a k f -> p (a k) f")
                for h in range(2):
                    part = src[:, 4 * h:4 * h + 4, c * 512:c * 512 + 512] if kind < 2 else src[:, 4 * c + 2 * h:4 * c + 2 * h + 2, :]
                    s = 2 * kind + h
                    if not (isinstance(e, int) and NB * e + c == 0):
                        sp.wait_ge(s_used[kind], at(e, 2 * NB, 2 * c + h - 1))
                    sp.dma_start(half_view(RAW[s], kind), part).then_inc(s_w[s], 16)

            with nc.Block() as block:
                @block.sync
                def _(sp):
                    for kind in range(3):
                        load(sp, kind, 0, 0)

                @block.vector
                def _(dve):
                    link = linker(dve, tag)
                    if r == 0:
                        dve.memset(ACC, 0.0)
                    else:
                        link(dve.tensor_scalar(pos, pos, float(P), None, ALU.subtract))
                    for e in range(E):
                        for i in range(2):
                            a = slice(8 * i + e, 8 * i + e + 1)
                            link(dve.tensor_scalar(disp[:, e, i, :], cst("iota"), pos[:, a], sel[:, a], ALU.is_equal, ALU.mult))
                            dve.tensor_scalar(weighted[:, e, i, :], disp[:, e, i, :], gw[:, a], None, ALU.mult).then_inc(s_dp, 1)
                    for b in range(4):
                        dve.wait_ge(s_dt, b + 1)
                        dve.tensor_copy(back[:, 2 * b:2 * b + 2, :], bank[b][:, :].rearrange("p (e n) -> p e n", e=2)).then_inc(s_dc, 1)

                @block.tensor
                def _(pe):
                    for b in range(4):
                        pe.wait_ge(s_dp, 4 * b + 4)
                        for x in range(4):
                            mm = pe.transpose(quad(b)[:, x, :], weighted[:, 2 * b + x // 2, x % 2, :], ident)
                        mm.then_inc(s_dt, 1)

                @block.scalar
                def _(act):
                    pass

                @block.gpsimd
                def _(pool):
                    pass

            with nc.Block() as block:
                @block.sync
                def _(sp):
                    def body(e):
                        first = isinstance(e, int) and e == 0
                        for c in range(1 if first else 0, NB):
                            load(sp, 0, e, c)
                            load(sp, 1, e, c)
                            if c:
                                if not (first and c == 1):
                                    load(sp, 2, e, c - 1)
                            else:
                                load(sp, 2, e - 1 if isinstance(e, int) else (e[0], e[1] - 1), NB - 1)
                    over_experts(sp, body)
                    load(sp, 2, E - 1, NB - 1)

                @block.tensor
                def _(pe):
                    def up(e, c, kind, out_bank):
                        q = parity(e)
                        for h in range(2):
                            s = 2 * kind + h
                            pe.wait_ge(s_lo[kind], at(e, 2 * NB, 2 * c + h + 1))
                            wh, wl = rounded(half_view(HIGH[s], kind)), rounded(half_view(RAW[s], kind))
                            for k in range(4):
                                kk = 4 * h + k
                                hi, lo = rounded(xh[q][:, kk, :]), rounded(xl[q][:, kk, :])
                                pe.matmul(out_bank, hi, wh[:, k, :], start=(kk == 0), stop=False)
                                pe.matmul(out_bank, hi, wl[:, k, :], start=False, stop=False)
                                mm = pe.matmul(out_bank, lo, wh[:, k, :], start=False, stop=(kk == KD - 1))
                            mm.then_inc(s_used[kind], 1)

                    def misc(e, i):
                        if not (isinstance(e, int) and e == 0 and i < 0):
                            pe.wait_ge(s_mf, misc_before(e, i - 1))
                        return misc_bank(e, i)

                    def turn(e, i, n):
                        b = misc(e, i)
                        pe.wait_ge(s_pr, at(e, NB, n + 1))
                        for j in range(4):
                            mm = pe.transpose(quad(b)[:, j, :], prod[:, (parity(e) + n) % 2, j * P:j * P + P], ident)
                        mm.then_inc(s_ms, 1)

                    def down(e, i, n):
                        c = n % NB
                        if c == 0 and not (isinstance(e, int) and e == 0):
                            pe.wait_ge(s_yc, at(e, 1, 0))
                        pe.wait_ge(s_mf, misc_before(e, i + 1))
                        for h in range(2):
                            pe.wait_ge(s_lo[2], at(e, 2 * NB, 2 * n + h + 1))
                            wh, wl = rounded(half_view(HIGH[4 + h], 2)), rounded(half_view(RAW[4 + h], 2))
                            for j in range(2):
                                jj = 2 * h + j
                                x = slice(jj * P, jj * P + P)
                                hi = rounded(prodTh[:, (parity(e) + n) % 2, x])
                                lo = rounded(prodTl[:, (parity(e) + n) % 2, x])
                                st, sp_ = c == 0 and jj == 0, c == NB - 1 and jj == 3
                                for half in range(2):
                                    o = slice(half * 512, half * 512 + 512)
                                    pe.matmul(bank[6 + half][:, :], hi, wh[:, j, o], start=st, stop=False)
                                    pe.matmul(bank[6 + half][:, :], hi, wl[:, j, o], start=False, stop=False)
                                    mm = pe.matmul(bank[6 + half][:, :], lo, wh[:, j, o], start=False, stop=sp_)
                            mm.then_inc(s_used[2], 1)

                    def gather(e, i, g, shift):
                        b = misc(e, i)
                        for k in range(4):
                            for tile in range(2):
                                sl_ = at_expert(disp, e, shift)[:, :, tile, :].rearrange("p a s -> p (a s)")
                                mm = pe.matmul(quad(b)[:, k, :], xn1[:, tile, (4 * g + k) * P:(4 * g + k + 1) * P], sl_, start=(tile == 0), stop=(tile == 1))
                        mm.then_inc(s_ms, 1)

                    def scatter(e, i, x, q):
                        b = misc(e, i)
                        pe.matmul(bank[b][:, :], backs[:, q, (x // 2) * P:(x // 2) * P + P], ysb[:, (x % 2) * 512:(x % 2) * 512 + 512],
                                  start=True, stop=True).then_inc(s_ms, 1)

                    def body(e):
                        first, last = isinstance(e, int) and e == 0, isinstance(e, int) and e == E - 1
                        i = 0
                        pe.wait_ge(s_mf, 2 if first else misc_before(e, 0))
                        for c in range(NB):
                            lagged = not (first and c == 0)
                            if not (first and c < 2):
                                pe.wait_ge(s_sl, at(e, NB, c - 1))
                            up(e, c, 0, bank[(parity(e) + c) % 2][:, :])
                            if lagged:
                                turn(e, i, c - 1)
                                i += 1
                            if not (first and c < 2):
                                pe.wait_ge(s_pr, at(e, NB, c - 1))
                            up(e, c, 1, bank[2 + (parity(e) + c) % 2][:, :])
                            i_turn = i - 1
                            for kind, x in pieces(c, first, last):
                                if kind == "scatter":
                                    if x == 0:
                                        pe.wait_ge(s_yc, at(e, 1, 0))
                                        pe.wait_ge(s_bk, at(e, 1, 0))
                                    scatter(e, i, x, 1 - parity(e))
                                else:
                                    gather(e, i, x, 1)
                                i += 1
                            if lagged:
                                down(e, i_turn, c - 1)
                    for g in range(2):
                        gather(0, g - 2, g, 0)
                    over_experts(pe, body)
                    turn(E - 1, NB + 4, NB - 1)
                    down(E - 1, NB + 4, NB - 1)
                    pe.wait_ge(s_yc, E)
                    pe.wait_ge(s_bk, E)
                    for x in range(4):
                        scatter(E - 1, NB + 5 + x, x, (E - 1) % 2)

                @block.scalar
                def _(act):
                    shift, scale = modc[:, 1, 2, :, 0], modc[:, 1, 3, :, 0]

                    def high_weights(kind, e, n):
                        for h in range(2):
                            s = 2 * kind + h
                            act.wait_ge(s_w[s], at(e, 16 * NB, 16 * (n + 1)))
                            high(act, HIGH[s], RAW[s]).then_inc(s_hi[kind], 1)

                    def turned_high(e, i, n):
                        act.wait_ge(s_ms, misc_before(e, i + 1))
                        if not (isinstance(e, int) and NB * e + n < 2):
                            act.wait_ge(s_used[2], at(e, 2 * NB, 2 * n - 2))
                        act.activation(rounded(prodTh[:, (parity(e) + n) % 2, :]), bank[misc_bank(e, i)][:, :], ACT.Copy).then_inc(s_mh, 1)

                    def gathered(e, i, g, q, before):
                        act.wait_ge(s_ms, misc_before(e, i + 1))
                        for k in range(4):
                            kk = 4 * g + k
                            ins = act.activation(xl[q][:, kk, :], quad(misc_bank(e, i))[:, k, :], ACT.Identity,
                                                 bias=shift[:, kk:kk + 1], scale=scale[:, kk:kk + 1])
                        ins.then_inc(s_vx, 1)
                        act.wait_ge(s_vx, before + 1)
                        act.activation(rounded(xh[q][:, 4 * g:4 * g + 4, :]), xl[q][:, 4 * g:4 * g + 4, :], ACT.Copy).then_inc(s_mh, 1)

                    def copy_y(e):
                        act.wait_ge(s_used[2], at(e, 2 * NB, 0))
                        for half in range(2):
                            ins = act.activation(ysb[:, half * 512:half * 512 + 512], bank[6 + half][:, :], ACT.Copy)
                        ins.then_inc(s_yc, 1)

                    def body(e):
                        first, last = isinstance(e, int) and e == 0, isinstance(e, int) and e == E - 1
                        i = 0
                        for c in range(NB):
                            if not (first and c == 0):
                                turned_high(e, i, c - 1)
                                i += 1
                            act.wait_ge(s_used[0], at(e, 2 * NB, 2 * c + 2))
                            if not (first and c < 2):
                                act.wait_ge(s_pr, at(e, NB, c - 1))
                            act.activation(silu_h[:, (parity(e) + c) % 2, :], bank[(parity(e) + c) % 2][:, :], ACT.Silu).then_inc(s_sl, 1)
                            if not (last and c == NB - 1):
                                high_weights(0, e, c + 1)
                                high_weights(1, e, c + 1)
                            if c == 0 and not first:
                                copy_y(e)
                            for kind, x in pieces(c, first, last):
                                if kind == "gather":
                                    gathered(e, i, x, 1 - parity(e), at(e, 2, 2 + x))
                                i += 1
                            high_weights(2, e, c)
                    high_weights(0, 0, 0)
                    high_weights(1, 0, 0)
                    for g in range(2):
                        gathered(0, g - 2, g, 0, g)
                    over_experts(act, body)
                    turned_high(E - 1, NB + 4, NB - 1)
                    copy_y(E)

                @block.gpsimd
                def _(pool):
                    def body(e):
                        if not (isinstance(e, int) and e == 0):
                            pool.wait_ge(s_ms, at(e, 13, -7))
                        pool.tensor_copy(backs[:, parity(e), :], at_expert(back, e).rearrange("p a n -> p (a n)")).then_inc(s_bk, 1)
                    over_experts(pool, body)

                @block.vector
                def _(dve):
                    def low_weights(kind, e, n):
                        for h in range(2):
                            s = 2 * kind + h
                            dve.wait_ge(s_hi[kind], at(e, 2 * NB, 2 * n + h + 1))
                            low(dve, RAW[s], HIGH[s]).then_inc(s_lo[kind], 1)

                    def gathered(e, j, g, q):
                        dve.wait_ge(s_mh, splits_before(e, j + 1))
                        v = slice(4 * g, 4 * g + 4)
                        low(dve, xl[q][:, v, :], xh[q][:, v, :]).then_inc(s_mf, 1)

                    def turned_low(e, i, j, n):
                        dve.wait_ge(s_mh, splits_before(e, j + 1))
                        x = (parity(e) + n) % 2
                        dve.tensor_tensor(rounded(prodTl[:, x, :]), bank[misc_bank(e, i)][:, :], rounded(prodTh[:, x, :]).bitcast(F32), ALU.subtract).then_inc(s_mf, 1)

                    def add_scattered(e, i, x):
                        dve.wait_ge(s_mf, misc_before(e, i))
                        dve.wait_ge(s_ms, misc_before(e, i + 1))
                        a = ACC[:, x // 2, (x % 2) * 512:(x % 2) * 512 + 512]
                        dve.tensor_tensor(a, a, bank[misc_bank(e, i)][:, :], ALU.add).then_inc(s_mf, 1)

                    def body(e):
                        first, last = isinstance(e, int) and e == 0, isinstance(e, int) and e == E - 1
                        i = j = 0
                        for c in range(NB):
                            if not (first and c == 0):
                                turned_low(e, i, j, c - 1)
                                i, j = i + 1, j + 1
                            more = not (last and c == NB - 1)
                            if more:
                                low_weights(0, e, c + 1)
                            dve.wait_ge(s_sl, at(e, NB, c + 1))
                            dve.wait_ge(s_used[1], at(e, 2 * NB, 2 * c + 2))
                            x = (parity(e) + c) % 2
                            dve.tensor_tensor(prod[:, x, :], silu_h[:, x, :], bank[2 + x][:, :], ALU.mult).then_inc(s_pr, 1)
                            if more:
                                low_weights(1, e, c + 1)
                            for kind, x in pieces(c, first, last):
                                if kind == "scatter":
                                    add_scattered(e, i, x)
                                else:
                                    gathered(e, j, x, 1 - parity(e))
                                    j += 1
                                i += 1
                            low_weights(2, e, c)
                    low_weights(0, 0, 0)
                    low_weights(1, 0, 0)
                    for g in range(2):
                        gathered(0, g - 2, g, 0)
                    over_experts(dve, body)
                    turned_low(E - 1, NB + 4, NB, NB - 1)
                    for x in range(4):
                        add_scattered(E - 1, NB + 5 + x, x)

        experts(0)
        full = nc.values_load(most[0:1, 0:1], engines=mybir.ALL_ENGINES, min_val=0, max_val=LAT)
        with nc.If(full > P):
            experts(1)

        s_fs, s_fr, s_fx, s_out = (sem(f"end_{x}") for x in ("squares", "rms", "residual", "stored"))
        fs, tmp = small[:, 0:2], xn1
        with nc.Block() as block:
            @block.scalar
            def _(act):
                for i in range(2):
                    act.activation(cut(4096, 2, D)[:, i, :], ACC[:, i, :], ACT.Square, accum_out=fs[:, i:i + 1]).then_inc(s_fs, 1)

            @block.gpsimd
            def _(pool):
                link = linker(pool, "pool")
                pool.wait_ge(s_fs, 2)
                link(pool.tensor_scalar(fs, fs, 1.0 / D, EPS, ALU.mult, ALU.add))
                pool.tensor_tensor(fs, fs, mhalf[:, 0:2], ALU.pow).then_inc(s_fr, 1)

            @block.vector
            def _(dve):
                link = linker(dve, "dve")
                dve.wait_ge(s_fr, 1)
                for i in range(2):
                    link(dve.scalar_tensor_tensor(tmp[:, i, :], ACC[:, i, :], fs[:, i:i + 1], G[:, 3, :], ALU.mult, ALU.mult))
                    dve.tensor_tensor(X[:, i, :], X[:, i, :], tmp[:, i, :], ALU.add).then_inc(s_fx, 1)

            @block.sync
            def _(sp):
                for i in range(2):
                    sp.wait_ge(s_fx, i + 1)
                    sp.dma_start(out.rearrange("(t p) d -> p t d", p=P)[:, i, :], X[:, i, :]).then_inc(s_out, 16)
                sp.wait_ge(s_out, 32)


def shape_constants():
    import numpy as np
    c = {n: np.zeros((P, w), np.float32) for n, (_, w) in CONST.items()}
    r = np.arange(P)
    c["ident"][r, r] = 1
    c["cum0"][:] = r[:, None] <= r[None, :]
    c["cum1"][:] = r[:, None] >= r[None, :]
    c["ones"][:] = 1
    c["neg0"][:] = np.where(r[None, :] >= r[:, None], 0, -30000)
    c["neg1"][:] = np.where(r[None, :] <= r[:, None], 0, -30000)
    k = np.arange(LAT)
    for i in range(2):
        c["band"][:, i * LAT:(i + 1) * LAT] = np.where(np.abs(k[None, :] - (r[:, None] + P * i)) <= 128, 0, -1e30)
    q = r % 64
    start = np.clip(q - 8, 0, 48)[:, None]
    k = np.arange(64)[None, :]
    c["natcol"][:] = np.where((k >= start) & (k < start + 16), 0, -1e30)
    half = 16
    freqs = (10000.0 ** (-np.arange(half, dtype=np.float32) / np.float32(half))).astype(np.float32)
    pos = np.arange(LAT)
    for p in range(P):
        dd = p % 64
        at = (pos // 64 if dd < 32 else pos % 64).astype(np.float32)
        ang = (at * freqs[dd % 16]).astype(np.float32)
        c["cos"][p], c["sin"][p] = np.cos(ang), np.sin(ang)
        if dd % 32 < 16:
            c["rot"][p + 16, p] = -1
        else:
            c["rot"][p - 16, p] = 1
    c["iota"][:] = r[None, :]
    c["before"][:] = r[:, None] < r[None, :]
    c["eighth"][:, 7] = 1
    levels = np.zeros((P, 2, LEVELS, P), np.float32)
    for l in range(LEVELS):
        b = 1 << l
        same = r[:, None] // (2 * b) == r[None, :] // (2 * b)
        levels[:, 0, l, :] = same & (r[:, None] // b < r[None, :] // b)
        levels[:, 1, l, :] = same & (r[:, None] // b > r[None, :] // b)
    return np.concatenate([c[n] for n in CONST], axis=1), levels


def nat_bias_places():
    import numpy as np
    q = np.arange(LAT)
    dr = np.arange(4)[None, :, None] - (q // 64)[:, None, None] + 7
    dc = np.clip(np.arange(64)[None, None, :] - (q % 64)[:, None, None] + 15, 0, 30)
    return (dr * 31 + dc).reshape(LAT, LAT)


def kernel(**inputs):
    import numpy as np
    import concourse.bacc as bacc
    from concourse.bass_utils import run_bass_kernel_spmd as run

    a = {k: np.ascontiguousarray(v) for k, v in inputs.items()}
    const, levels = shape_constants()
    rpb = a["na_rpb"][0].reshape(8, 15 * 31)[:, nat_bias_places()]
    arrays = {
        "x": a["x"][0], "ctx": a["ctx"][0], "c": a["c"], "c_ctx": a["c_ctx"][None, :],
        "ada_w": a["ada_w"], "ada_b": a["ada_b"], "norm_w": a["norm_w"],
        "ev_w_in": a["ev_w_in"][0], "ev_w_out": a["ev_w_out"][0],
        "nat_bias": rpb.reshape(8, 2, P, LAT).transpose(2, 1, 0, 3),
        "dn_conv": a["dn_conv"][0], "dn_a_log": a["dn_a_log"].reshape(8, 1), "dn_dt_bias": a["dn_dt_bias"].reshape(8, 1), "dn_norm": a["dn_norm"],
        "ffn_w1": a["ffn_w1"][0], "ffn_w3": a["ffn_w3"][0], "ffn_w2": a["ffn_w2"][0],
        "od_w_in": a["od_w_in"][0], "od_w_out": a["od_w_out"][0], "wa_sink": a["wa_sink"],
        "ssd_conv": a["ssd_conv"][0], "ssd_a_log": a["ssd_a_log"].reshape(16, 1), "ssd_dt_bias": a["ssd_dt_bias"].reshape(16, 1),
        "ssd_d": a["ssd_d"], "ssd_norm": a["ssd_norm"],
        "moe_router": a["moe_router"][0], "moe_w1": a["moe_w1"][0], "moe_w3": a["moe_w3"][0], "moe_w2": a["moe_w2"][0],
        "const": const, "levels": levels,
    }
    pairs = np.arange(8).reshape(2, 4).T.ravel()
    for name, axis in (("od_w_in", 1), ("od_w_out", 0)):
        w = arrays[name] if axis == 0 else arrays[name].T
        heads = w[:512].reshape(8, HD, -1)[pairs].reshape(512, -1)
        w = np.concatenate([heads, w[512:]])
        arrays[name] = w if axis == 0 else w.T
    arrays = {f"in_{k}": np.ascontiguousarray(v) for k, v in arrays.items()}
    nc = bacc.Bacc("TRN2", target_bir_lowering=False, num_devices=1)
    t = {k[3:]: nc.dram_tensor(k, v.shape, mybir.dt.from_np(v.dtype), kind="ExternalInput").ap() for k, v in arrays.items()}
    out = nc.dram_tensor("out", (LAT, D), F32, kind="ExternalOutput").ap()
    build(nc, t, out)
    got = run(nc, [arrays], core_ids=[0])
    return got.results[0]["out"].reshape(1, LAT, D)
```
